# Optimizing a Trainium2 kernel written in Bass

```python
import math
import jax
import jax.numpy as jnp
from jax import lax
import numpy as np

D_MODEL = 1024
BATCH = 1
SEQ = 256
DEPTH = 2

CHUNK = 64
Q_BLOCK = 128
RMS_EPS = 1e-6

LRU_WIDTH = D_MODEL // 2
LRU_BLOCKS = 8
LRU_BLOCK_DIM = LRU_WIDTH // LRU_BLOCKS
CONV_WIDTH = 4
LRU_C = 8.0
MLSTM_WIDTH = D_MODEL // 2
MLSTM_HEADS = 4
MLSTM_HEAD_DIM = MLSTM_WIDTH // MLSTM_HEADS
AB_IN_COLS = 2 * LRU_WIDTH + 4 * MLSTM_WIDTH + 2 * MLSTM_HEADS
AB_OUT_WIDTH = LRU_WIDTH + MLSTM_WIDTH

DIFF_HEADS = 8
DIFF_V_DIM = D_MODEL // DIFF_HEADS
DIFF_QK_DIM = DIFF_V_DIM // 2
DIFF_WIDTH = DIFF_HEADS * DIFF_V_DIM

N_GROUPS = 4
EXPERTS_PER_GROUP = 8
N_EXPERTS = N_GROUPS * EXPERTS_PER_GROUP
TOP_K = 2
EXPERT_FF = D_MODEL // 2

N_AB_LAYERS = (DEPTH + 1) // 2
N_DIFF_LAYERS = DEPTH // 2

kernel_name = 'chunk_causal_hybrid_rglru_mlstm_diffattn_hmoe'

def rms_norm(x, g):
    xf = x.astype(jnp.float32)
    y = xf * lax.rsqrt(jnp.mean(xf * xf, axis=-1, keepdims=True) + RMS_EPS)
    return (y * g.astype(jnp.float32)).astype(x.dtype)

def causal_depthwise_conv(x, w, b):
    out = lax.conv_general_dilated(
        x, w[:, None, :].astype(x.dtype), window_strides=(1,),
        padding=[(CONV_WIDTH - 1, 0)], dimension_numbers=('NWC', 'WIO', 'NWC'),
        feature_group_count=x.shape[-1])
    return out + b.astype(x.dtype)

def block_diag_linear(x, w, b):
    xb = x.reshape(x.shape[:-1] + (LRU_BLOCKS, LRU_BLOCK_DIM))
    y = jnp.einsum('bsnd,nde->bsne', xb, w.astype(jnp.float32))
    return y.reshape(x.shape) + b.astype(jnp.float32)

def rg_lru(x, w_r, b_r, w_i, b_i, lam):
    xf = x.astype(jnp.float32)
    r = jax.nn.sigmoid(block_diag_linear(xf, w_r, b_r))
    i = jax.nn.sigmoid(block_diag_linear(xf, w_i, b_i))
    log_a = LRU_C * r * jax.nn.log_sigmoid(lam.astype(jnp.float32))
    a = jnp.exp(log_a)
    u = jnp.sqrt(-jnp.expm1(2.0 * log_a)) * (i * xf)

    def combine(left, right):
        a1, b1 = left
        a2, b2 = right
        return a1 * a2, a2 * b1 + b2

    _, h = lax.associative_scan(combine, (a, u), axis=1)
    return h.astype(x.dtype)

def mlstm_chunkwise(q, k, v, i_pre, f_pre):
    B, S, H, dh = q.shape
    nc = S // CHUNK

    def to_chunks(t):
        t = t.astype(jnp.float32).reshape((B, nc, CHUNK, H) + t.shape[3:])
        return jnp.moveaxis(jnp.moveaxis(t, 1, 0), 3, 2)

    qc = to_chunks(q)
    kc = to_chunks(k) * (dh ** -0.5)
    vc = to_chunks(v)
    ic = to_chunks(i_pre)
    bc = jnp.cumsum(jax.nn.log_sigmoid(to_chunks(f_pre)), axis=-1)
    causal = jnp.tril(jnp.ones((CHUNK, CHUNK), dtype=bool))

    def step(carry, inp):
        C, n, m = carry
        q_, k_, v_, b_, i_ = inp
        g_ = b_[..., -1]
        log_d = jnp.where(causal, b_[..., :, None] - b_[..., None, :] + i_[..., None, :], -jnp.inf)
        log_inter = b_ + m[..., None]
        m_t = jnp.maximum(log_inter, jnp.max(log_d, axis=-1))
        w_intra = jnp.exp(log_d - m_t[..., None])
        w_inter = jnp.exp(log_inter - m_t)
        s = jnp.einsum('bhld,bhsd->bhls', q_, k_) * w_intra
        num = (w_inter[..., None] * jnp.einsum('bhld,bhde->bhle', q_, C)
               + jnp.einsum('bhls,bhse->bhle', s, v_))
        den = w_inter * jnp.einsum('bhld,bhd->bhl', q_, n) + jnp.sum(s, axis=-1)
        h = num / jnp.maximum(jnp.abs(den), jnp.exp(-m_t))[..., None]
        log_w = g_[..., None] - b_ + i_
        m_new = jnp.maximum(g_ + m, jnp.max(log_w, axis=-1))
        w_state = jnp.exp(log_w - m_new[..., None])
        decay = jnp.exp(g_ + m - m_new)
        C = decay[..., None, None] * C + jnp.einsum('bhs,bhsd,bhse->bhde', w_state, k_, v_)
        n = decay[..., None] * n + jnp.einsum('bhs,bhsd->bhd', w_state, k_)
        return (C, n, m_new), h

    init = (jnp.zeros((B, H, dh, dh), jnp.float32),
            jnp.zeros((B, H, dh), jnp.float32),
            jnp.zeros((B, H), jnp.float32))
    _, h = lax.scan(step, init, (qc, kc, vc, bc, ic))
    return jnp.moveaxis(h, 0, 1).transpose(0, 1, 3, 2, 4).reshape(B, S, H, dh)

def hybrid_lru_mlstm_mixer(xn, w_in, w_out, conv_w, conv_b, w_r, b_r, w_i, b_i, lam,
                           mb_i, mb_f, mnorm_g):
    B, S, _ = xn.shape
    proj = xn @ w_in
    idx = np.cumsum([LRU_WIDTH, LRU_WIDTH, MLSTM_WIDTH, MLSTM_WIDTH, MLSTM_WIDTH,
                     MLSTM_WIDTH, MLSTM_HEADS]).tolist()
    xa, ga, q, k, v, o, ip, fp = jnp.split(proj, idx, axis=-1)
    xa = causal_depthwise_conv(xa, conv_w, conv_b)
    ya = rg_lru(xa, w_r, b_r, w_i, b_i, lam) * jax.nn.gelu(ga)
    hs = (B, S, MLSTM_HEADS, MLSTM_HEAD_DIM)
    hb = mlstm_chunkwise(q.reshape(hs), k.reshape(hs), v.reshape(hs),
                         ip + mb_i.astype(ip.dtype), fp + mb_f.astype(fp.dtype))
    hb = rms_norm(hb, mnorm_g) * jax.nn.sigmoid(o.astype(jnp.float32)).reshape(hs)
    yb = hb.reshape(B, S, MLSTM_WIDTH).astype(xn.dtype)
    return jnp.concatenate([ya, yb], axis=-1) @ w_out

def diff_attention(xn, w_qkv, w_o, lq1, lk1, lq2, lk2, norm_g, lambda_init):
    B, S, _ = xn.shape
    H = DIFF_HEADS
    q, k, v = jnp.split(xn @ w_qkv, [DIFF_WIDTH, 2 * DIFF_WIDTH], axis=-1)
    q = q.reshape(B, S, H, 2, DIFF_QK_DIM)
    k = k.reshape(B, S, H, 2, DIFF_QK_DIM)
    v = v.reshape(B, S, H, DIFF_V_DIM)
    f32 = jnp.float32
    lam = (jnp.exp(jnp.sum(lq1.astype(f32) * lk1.astype(f32)))
           - jnp.exp(jnp.sum(lq2.astype(f32) * lk2.astype(f32))) + lambda_init)
    slopes = jnp.exp2(-8.0 * jnp.arange(1, H + 1, dtype=f32) / H)
    scale = DIFF_QK_DIM ** -0.5
    n_blocks = S // Q_BLOCK
    q_blocks = jnp.moveaxis(q.reshape(B, n_blocks, Q_BLOCK, H, 2, DIFF_QK_DIM), 1, 0)
    k_pos = jnp.arange(S)

    def attend_block(args):
        q_blk, blk = args
        q_pos = blk * Q_BLOCK + jnp.arange(Q_BLOCK)
        scores = jnp.einsum('bqhcd,bkhcd->bhcqk', q_blk, k).astype(f32) * scale
        dist = jnp.abs(q_pos[:, None] - k_pos[None, :]).astype(f32)
        scores = scores - (slopes[:, None, None] * dist)[None, :, None]
        allowed = (k_pos[None, :] // CHUNK) <= (q_pos[:, None] // CHUNK)
        probs = jax.nn.softmax(jnp.where(allowed, scores, -jnp.inf), axis=-1)
        diff = probs[:, :, 0] - lam * probs[:, :, 1]
        return jnp.einsum('bhqk,bkhe->bqhe', diff.astype(v.dtype), v)

    out = lax.map(attend_block, (q_blocks, jnp.arange(n_blocks)))
    out = jnp.moveaxis(out, 0, 1).reshape(B, S, H, DIFF_V_DIM)
    out = rms_norm(out, norm_g) * (1.0 - lambda_init)
    return out.reshape(B, S, DIFF_WIDTH) @ w_o

def hierarchical_moe(xn, w_group, b_group, w_expert, b_expert, w_up, w_down):
    B, S, D = xn.shape
    t = xn.reshape(B * S, D)
    f32 = jnp.float32
    group_logits = (t @ w_group).astype(f32) + b_group.astype(f32)
    group_prob = jax.nn.softmax(group_logits, axis=-1)
    g_idx = jnp.argmax(group_logits, axis=-1)
    g_weight = jnp.take_along_axis(group_prob, g_idx[:, None], axis=-1)
    e_logits = ((t @ w_expert).astype(f32) + b_expert.astype(f32)).reshape(-1, N_GROUPS, EXPERTS_PER_GROUP)
    in_group = jnp.take_along_axis(e_logits, g_idx[:, None, None], axis=1)[:, 0]
    top_logits, top_idx = lax.top_k(in_group, TOP_K)
    top_w = jax.nn.softmax(top_logits, axis=-1) * g_weight
    expert_id = g_idx[:, None] * EXPERTS_PER_GROUP + top_idx
    gates = jnp.sum(jax.nn.one_hot(expert_id, N_EXPERTS, dtype=f32) * top_w[..., None], axis=1)
    y = jnp.zeros((B * S, D), f32)
    for e in range(N_EXPERTS):
        h = t @ w_up[e]
        h = jax.nn.silu(h[:, :EXPERT_FF]) * h[:, EXPERT_FF:]
        y = y + gates[:, e:e + 1] * (h @ w_down[e]).astype(f32)
    return y.astype(xn.dtype).reshape(B, S, D)

def setup_inputs(seed: int = 0) -> dict:
    key = jax.random.key(seed)
    ks = jax.random.split(key, 32)
    f32 = jnp.float32

    def nrm(k, shape, scale):
        return jax.random.normal(k, shape, f32) * scale

    u = jax.random.uniform(ks[10], (N_AB_LAYERS, LRU_WIDTH), f32, minval=0.9, maxval=0.999)
    a0 = u ** (1.0 / LRU_C)
    lru_lambda = jnp.log(a0) - jnp.log1p(-a0)
    return {
        'x': nrm(ks[0], (BATCH, SEQ, D_MODEL), 1.0),
        'norm_mix_g': 1.0 + nrm(ks[1], (DEPTH, D_MODEL), 0.05),
        'norm_ffn_g': 1.0 + nrm(ks[2], (DEPTH, D_MODEL), 0.05),
        'ab_w_in': nrm(ks[3], (N_AB_LAYERS, D_MODEL, AB_IN_COLS), D_MODEL ** -0.5),
        'ab_w_out': nrm(ks[4], (N_AB_LAYERS, AB_OUT_WIDTH, D_MODEL), AB_OUT_WIDTH ** -0.5),
        'lru_conv_w': nrm(ks[5], (N_AB_LAYERS, CONV_WIDTH, LRU_WIDTH), CONV_WIDTH ** -0.5),
        'lru_conv_b': nrm(ks[6], (N_AB_LAYERS, LRU_WIDTH), 0.02),
        'lru_w_r': nrm(ks[7], (N_AB_LAYERS, LRU_BLOCKS, LRU_BLOCK_DIM, LRU_BLOCK_DIM), LRU_BLOCK_DIM ** -0.5),
        'lru_b_r': nrm(ks[8], (N_AB_LAYERS, LRU_WIDTH), 0.02),
        'lru_w_i': nrm(ks[9], (N_AB_LAYERS, LRU_BLOCKS, LRU_BLOCK_DIM, LRU_BLOCK_DIM), LRU_BLOCK_DIM ** -0.5),
        'lru_b_i': nrm(ks[11], (N_AB_LAYERS, LRU_WIDTH), 0.02),
        'lru_lambda': lru_lambda,
        'mlstm_b_i': nrm(ks[12], (N_AB_LAYERS, MLSTM_HEADS), 0.1),
        'mlstm_b_f': jnp.linspace(3.0, 6.0, MLSTM_HEADS, dtype=f32)[None, :] + nrm(ks[13], (N_AB_LAYERS, MLSTM_HEADS), 0.1),
        'mlstm_norm_g': 1.0 + nrm(ks[14], (N_AB_LAYERS, MLSTM_HEADS, MLSTM_HEAD_DIM), 0.05),
        'diff_w_qkv': nrm(ks[15], (N_DIFF_LAYERS, D_MODEL, 3 * DIFF_WIDTH), D_MODEL ** -0.5),
        'diff_w_o': nrm(ks[16], (N_DIFF_LAYERS, DIFF_WIDTH, D_MODEL), DIFF_WIDTH ** -0.5),
        'diff_lambda_q1': nrm(ks[17], (N_DIFF_LAYERS, DIFF_QK_DIM), 0.1),
        'diff_lambda_k1': nrm(ks[18], (N_DIFF_LAYERS, DIFF_QK_DIM), 0.1),
        'diff_lambda_q2': nrm(ks[19], (N_DIFF_LAYERS, DIFF_QK_DIM), 0.1),
        'diff_lambda_k2': nrm(ks[20], (N_DIFF_LAYERS, DIFF_QK_DIM), 0.1),
        'diff_norm_g': 1.0 + nrm(ks[21], (N_DIFF_LAYERS, DIFF_HEADS, DIFF_V_DIM), 0.05),
        'moe_w_group': nrm(ks[22], (DEPTH, D_MODEL, N_GROUPS), D_MODEL ** -0.5),
        'moe_b_group': nrm(ks[23], (DEPTH, N_GROUPS), 0.01),
        'moe_w_expert': nrm(ks[24], (DEPTH, D_MODEL, N_EXPERTS), D_MODEL ** -0.5),
        'moe_b_expert': nrm(ks[25], (DEPTH, N_EXPERTS), 0.01),
        'moe_w_up': nrm(ks[26], (DEPTH, N_EXPERTS, D_MODEL, 2 * EXPERT_FF), D_MODEL ** -0.5),
        'moe_w_down': nrm(ks[27], (DEPTH, N_EXPERTS, EXPERT_FF, D_MODEL), EXPERT_FF ** -0.5),
        'final_norm_g': 1.0 + nrm(ks[28], (D_MODEL,), 0.05),
    }

def reference(x, norm_mix_g, norm_ffn_g, ab_w_in, ab_w_out, lru_conv_w, lru_conv_b, lru_w_r,
              lru_b_r, lru_w_i, lru_b_i, lru_lambda, mlstm_b_i, mlstm_b_f, mlstm_norm_g,
              diff_w_qkv, diff_w_o, diff_lambda_q1, diff_lambda_k1, diff_lambda_q2,
              diff_lambda_k2, diff_norm_g, moe_w_group, moe_b_group, moe_w_expert,
              moe_b_expert, moe_w_up, moe_w_down, final_norm_g):
    h = x
    for layer in range(DEPTH):
        hn = rms_norm(h, norm_mix_g[layer])
        j = layer // 2
        if layer % 2 == 0:
            h = h + hybrid_lru_mlstm_mixer(
                hn, ab_w_in[j], ab_w_out[j], lru_conv_w[j], lru_conv_b[j], lru_w_r[j],
                lru_b_r[j], lru_w_i[j], lru_b_i[j], lru_lambda[j], mlstm_b_i[j],
                mlstm_b_f[j], mlstm_norm_g[j])
        else:
            lambda_init = 0.8 - 0.6 * math.exp(-0.3 * layer)
            h = h + diff_attention(
                hn, diff_w_qkv[j], diff_w_o[j], diff_lambda_q1[j], diff_lambda_k1[j],
                diff_lambda_q2[j], diff_lambda_k2[j], diff_norm_g[j], lambda_init)
        h = h + hierarchical_moe(rms_norm(h, norm_ffn_g[layer]), moe_w_group[layer],
                                 moe_b_group[layer], moe_w_expert[layer], moe_b_expert[layer],
                                 moe_w_up[layer], moe_w_down[layer])
    return rms_norm(h, final_norm_g)


_drawn_inputs = setup_inputs


def setup_inputs(seed=0):
    import zlib

    import numpy as np

    out = dict(_drawn_inputs(seed))
    spreads = {}
    factors = {'lru_b_r': 10.18, 'lru_b_i': 3.915, 'mlstm_b_i': 200.0, 'diff_lambda_k2': 3.827}
    for name, (base, spread) in spreads.items():
        noise = np.random.default_rng([zlib.crc32(name.encode()), seed]).standard_normal(out[name].shape)
        drawn = base * np.exp(spread * noise) if base else spread * noise
        out[name] = jnp.asarray(drawn.astype(out[name].dtype))
    for name, factor in factors.items():
        out[name] = (out[name] * factor).astype(out[name].dtype)
    return out
```

```python
import math
from contextlib import ExitStack

import concourse.bass as bass
from concourse import mybir

F32 = mybir.dt.float32
I32 = mybir.dt.int32
ALU = mybir.AluOpType
ACT = mybir.ActivationFunctionType
AX = mybir.AxisListType

P = 128
D = 1024
KT = D // P
S = 256
TT = S // P
EPS = 1e-6
HALF = 512
NH = D // HALF

W = 512
WT = W // P
TAPS = 4
LRU_C = 8.0
MH = 4
K_SCALE = float(P) ** -0.5
CHUNK = 64

DH = 8
DQK = 64
Q_SCALE = float(DQK) ** -0.5
LAMBDA_INIT = 0.8 - 0.6 * math.exp(-0.3 * 1)

LAYERS = 2
NG = 4
EPG = 8
NE = NG * EPG
FF = 512
FT = FF // P
CAP = 32
EB = P // CAP
NB = NE // EB
GH = KT // 2

SLOTS = 8
SLOT = 4096
MIX_STEPS = 8
MOE_STEPS = KT + FT
LAYER_STEPS = MIX_STEPS + NB * MOE_STEPS
FILL_BANKS = 4

R_MIX, R_FFN, R_CW, R_CB, R_BR, R_BI, R_LAM, R_MNG, R_DNG = 0, 16, 32, 48, 52, 56, 60, 64, 68
NR = 76

FILLS = (
    ["columns"] + [f"norm0.{i}" for i in range(4)] + ["gates", "xa0", "xa1", "ga0", "ga1", "q0", "q1"]
    + [f"lru{j}" for j in range(WT)] + ["k0", "k1", "v0", "v1", "cols_am", "o0", "o1"]
    + [f"{x}{h}" for h in range(MH) for x in ("mmax", "sc")] + ["yb0", "yb1"]
    + [f"mix0.{i}" for i in range(4)] + [f"norm1.{i}" for i in range(4)] + ["router0", "rank0"]
    + [f"norm2.{i}" for i in range(4)] + [f"dq{i}" for i in range(4)] + [f"dk{i}" for i in range(4)]
    + [f"dv{i}" for i in range(4)] + ["ds0.0", "ds0.1"]
    + [x for u in range(2 * DH) for x in ([f"ds{u + 1}.0", f"ds{u + 1}.1"] if u + 1 < 2 * DH else []) + [f"dt{u}"]]
    + [f"dy{i}" for i in range(4)] + [f"mix1.{i}" for i in range(4)]
    + [f"norm3.{i}" for i in range(4)] + ["router1", "rank1"]
)
TURN = {name: n for n, name in enumerate(FILLS)}


def build(nc, x, norm_mix_g, norm_ffn_g, ab_w_in, ab_w_out, lru_conv_w, lru_conv_b, lru_w_r, lru_b_r, lru_w_i,
          lru_b_i, lru_lambda, mlstm_b_i, mlstm_b_f, mlstm_norm_g, diff_w_qkv, diff_w_o, diff_lambda_q1,
          diff_lambda_k1, diff_lambda_q2, diff_lambda_k2, diff_norm_g, moe_w_group, moe_b_group, moe_w_expert,
          moe_b_expert, moe_w_up, moe_w_down, final_norm_g, out):
    with ExitStack() as ctx:
        def sb(name, shape, dt=F32):
            return ctx.enter_context(nc.sbuf_tensor(name, shape, dt))

        def sem(name):
            return ctx.enter_context(nc.semaphore(name))

        ring = sb("ring", [P, SLOTS, SLOT])
        h = sb("h", [P, TT, D])
        xs = sb("xs", [P, TT, D])
        xT = sb("xT", [P, KT, S])
        rows = sb("rows", [NR, P])
        cols = sb("cols", [P, NR])
        ident = sb("ident", [P, P])
        before = sb("before", [P, P])
        upto = sb("upto", [P, P])
        ones = sb("ones", [P, P])
        slot_no = sb("slot_no", [P, CAP])
        prio = sb("prio", [P, NE])
        zrow = sb("zrow", [1, P])
        w_gate = sb("w_gate", [P, KT, 2 * MH])
        w_route = sb("w_route", [P, LAYERS, KT, NG + NE])
        b_route = sb("b_route", [P, LAYERS, NG + NE])
        w_block = sb("w_block", [P, 2, WT, P])
        b_if = sb("b_if", [MH, 2])
        lam_rows = sb("lam_rows", [P, 4, DQK])
        small = sb("small", [P, 136])
        flag = sb("flag", [1, LAYERS], I32)
        arena = sb("arena", [P, 10560])

        def view(at, *dims):
            n = 1
            for d in dims:
                n *= d
            v = arena[:, at:at + n]
            if len(dims) == 1:
                return v
            names = "abcd"[:len(dims)]
            return v.rearrange(f"p ({' '.join(names)}) -> p {' '.join(names)}",
                               **{c: d for c, d in zip(names, dims)})

        xpad = view(0, WT, S + TAPS - 1)
        root = view(0, WT * S)
        xc, r_g, i_g, t1, ga = (view(1040 + 1024 * n, WT, S) for n in range(5))
        flat = [view(1040 + 1024 * n, WT * S) for n in range(5)]
        xc_f, r_f, i_f, t1_f, ga_f = flat
        qT, kT, v_t, so = (view(6160 + 1024 * n, WT, S) for n in range(4))
        v_n = view(6160 + 2048, TT, W)
        yb = view(6160, TT, MH, P)
        sq = view(7184, TT, MH, P)
        lrow = view(10256, 256)
        yT = xs[:, :, :].rearrange("p a (b s) -> p (a b) s", s=S)
        gr = [sb(f"gr{n}", [MH, S]) for n in range(2)] + [yT[0:MH, WT + n, :] for n in range(4)]
        wbuf = xT[:, 0:3, :].rearrange("p a s -> p (a s)").rearrange("p (b w) -> p b w", b=2)
        pbuf = xT[:, 3:6, :].rearrange("p a s -> p (a s)").rearrange("p (b w) -> p b w", b=2)
        dq = view(0, DH, S)
        dk = view(2048, DH, S)
        dv = view(4096, TT, D)
        sp_ = view(6144, 2, 2, S)
        dif = view(7168, 2, S)
        dT = view(7680, 2, S)
        dist = view(8192, TT, S)
        on = xT[:, :, :].rearrange("p a s -> p (a s)").rearrange("p (t d) -> p t d", t=TT)
        xg = view(0, 2, KT, P)
        sel = view(2048, TT, EB, CAP)
        selg = view(2304, TT, EB, CAP)
        sgt = view(2560, 2, TT, P)
        sig = view(3072, FF)
        hid = view(3584, FF)
        hT = view(4096, FT, P)
        y_s = view(4608, D)
        lg = view(5632, TT, NG + NE)
        mg = view(5704, TT, NG)
        el = view(5712, TT, NE)
        m1 = view(5776, TT, NE)
        m2 = view(5840, TT, NE)
        tmp = view(5904, TT, NE)
        both = view(5968, TT, NE)
        rankm = view(6032, TT, NE + EB)
        gates = view(6104, TT, NE + EB)
        extra = view(6176, TT, NE)
        rs = view(6240, 64)
        rs2 = view(6304, TT, NG)
        ovh = view(6400, FT, S)
        ovs = view(7424, S)
        fg = view(8192, D)

        ss, rstd = small[:, 0:2], small[:, 2:4]
        c4 = small[:, 4:8]
        l1a, l1b, l1c = small[:, 8:12], small[:, 12:16], small[:, 16:20]
        am = small[:, 20:36]
        enm = small[:, 36:44]
        den = small[:, 44:52]
        den2 = small[:, 52:60]
        hss = small[:, 60:68]
        lsum = small[:, 68:70]
        nlam = small[:, 70:71]
        mx = small[:, 72:76]
        sums = small[:, 76:80]
        rsum = small[:, 80:84]
        oss = small[:, 84:100]
        dng2 = small[:, 100:108]
        minus_half = small[:, 108:124]

        psum = [ctx.enter_context(nc.psum_tensor(f"bank{n}", [P, HALF], F32)) for n in range(8)]
        den_ps = psum[5]
        num_ps = psum[6:8]
        o_ps = psum[4:8]
        hy = psum[0:2]
        gather_ps, turn_ps = psum[2], psum[3]
        acc = psum[4:8]

        x_loaded = sem("x_loaded")
        rows_loaded = sem("rows_loaded")
        blocks_zeroed = sem("blocks_zeroed")
        params_loaded = sem("params_loaded")
        fgain_loaded = sem("fgain_loaded")
        slot_loaded = [sem(f"slot_loaded{n}") for n in range(SLOTS)]
        steps_done = sem("steps_done")
        ident_ready = sem("ident_ready")
        consts_ready = sem("consts_ready")
        pool_step = sem("pool_step")
        dist_ready = sem("dist_ready")
        qk_free = sem("qk_free")
        fill_full = [sem(f"fill_full{n}") for n in range(FILL_BANKS)]
        fill_free = [sem(f"fill_free{n}") for n in range(FILL_BANKS)]
        dve_step = sem("dve_step")
        act_step = sem("act_step")
        cols_ready = sem("cols_ready")
        squares = sem("squares")
        mean_ready = sem("mean_ready")
        root_ready = sem("root_ready")
        xs_ready = sem("xs_ready")
        h_ready = sem("h_ready")
        lam_abs = sem("lam_abs")
        lam_exp = sem("lam_exp")
        lsum_ready = sem("lsum_ready")
        lsum_exp = sem("lsum_exp")
        f_abs = sem("f_abs")
        f_exp = sem("f_exp")
        am_rows = sem("am_rows")
        am_cols = sem("am_cols")
        enm_ready = sem("enm_ready")
        conv_done = sem("conv_done")
        lru_sig = sem("lru_sig")
        lru_tanh = sem("lru_tanh")
        lru_floor = sem("lru_floor")
        lru_root = sem("lru_root")
        gelu_in = sem("gelu_in")
        gelu_tanh = sem("gelu_tanh")
        ya_ready = sem("ya_ready")
        w_arg = sem("w_arg")
        w_exp = sem("w_exp")
        p_ready = sem("p_ready")
        num_done = sem("num_done")
        yb_ready = sem("yb_ready")
        yT_ready = sem("yT_ready")
        soft_max = sem("soft_max")
        soft_exp = sem("soft_exp")
        diff_ready = sem("diff_ready")
        pv_done = sem("pv_done")
        o_copied = sem("o_copied")
        on_ready = sem("on_ready")
        dyT_ready = sem("dyT_ready")
        route_arg = sem("route_arg")
        route_exp = sem("route_exp")
        picked = sem("picked")
        flag_ready = sem("flag_ready")
        sel_step = sem("sel_step")
        sel_ready = sem("sel_ready")
        gather_full = sem("gather_full")
        gather_free = sem("gather_free")
        sig_done = sem("sig_done")
        hid_step = sem("hid_step")
        hid_done = sem("hid_done")
        hT_full = sem("hT_full")
        hT_ready = sem("hT_ready")
        y_act = sem("y_act")
        y_dve = sem("y_dve")
        scattered = sem("scattered")
        dense_load = [sem(f"dense_load{l}") for l in range(LAYERS)]
        dense_gu = [sem(f"dense_gu{l}") for l in range(LAYERS)]
        dense_sig = [sem(f"dense_sig{l}") for l in range(LAYERS)]
        dense_mul = [sem(f"dense_mul{l}") for l in range(LAYERS)]
        dense_h = [sem(f"dense_h{l}") for l in range(LAYERS)]
        dense_y = [sem(f"dense_y{l}") for l in range(LAYERS)]
        dense_add = [sem(f"dense_add{l}") for l in range(LAYERS)]
        fin_ready = sem("fin_ready")
        out_stored = sem("out_stored")

        N_ROWS, N_PARAMS = 9, 19

        def bank_of(name):
            return psum[TURN[name] % FILL_BANKS]

        def wait_full(eng, name):
            eng.wait_ge(fill_full[TURN[name] % FILL_BANKS], TURN[name] // FILL_BANKS + 1)

        def wait_free(eng, name):
            if TURN[name] >= FILL_BANKS:
                eng.wait_ge(fill_free[TURN[name] % FILL_BANKS], TURN[name] // FILL_BANKS)

        def full(ins, name):
            ins.then_inc(fill_full[TURN[name] % FILL_BANKS], 1)

        def free(ins, name):
            ins.then_inc(fill_free[TURN[name] % FILL_BANKS], 1)

        def slot(step):
            return ring[:, step % SLOTS, :]

        def slot_k(step):
            return slot(step).rearrange("p (k n) -> p k n", k=KT)

        def slot_e(step):
            return slot(step).rearrange("p (e n) -> p e n", e=EB)

        def wait_slot(eng, step):
            eng.wait_ge(slot_loaded[step % SLOTS], 16 * (step // SLOTS + 1))

        block = ctx.enter_context(nc.Block())

        @block.sync
        def _(sp):
            sp.dma_start(h[:, :, :], x[0].rearrange("(t p) d -> p t d", p=P)).then_inc(x_loaded, 16)

            def mixer(layer, w_in, w_out):
                base = layer * LAYER_STEPS
                chunks = [w_in[:, HALF * n:HALF * (n + 1)] for n in range(6)]
                chunks += [w_out[:, HALF * n:HALF * (n + 1)] for n in range(NH)]
                for n, src in enumerate(chunks):
                    step = base + n
                    if step >= SLOTS:
                        sp.wait_ge(steps_done, step - SLOTS + 1)
                    sp.dma_start(slot_k(step), src.rearrange("(k p) n -> p k n", p=P))\
                        .then_inc(slot_loaded[step % SLOTS], 16)

            def experts(layer):
                base = layer * LAYER_STEPS + MIX_STEPS
                with sp.Fori(0, NB // 2) as i:
                    for par in range(2):
                        e0 = i * (2 * EB) + par * EB
                        for n in range(MOE_STEPS):
                            j = par * MOE_STEPS + n
                            w = moe_w_up if n < KT else moe_w_down
                            k = n if n < KT else n - KT
                            sp.wait_ge(steps_done, i * (2 * MOE_STEPS) + (base + j - SLOTS + 1))
                            sp.dma_start(slot_e(j), w[layer, bass.ds(e0, EB), k * P:(k + 1) * P, :]
                                         .rearrange("e p n -> p e n")).then_inc(slot_loaded[j % SLOTS], 16)

            def dense_expert(layer, e):
                sp.dma_start(ring[:, 0:2, :].rearrange("p a (k n) -> p (a k) n", k=KT // 2),
                             moe_w_up[layer, e].rearrange("(k p) n -> p k n", p=P)).then_inc(dense_load[layer], 16)
                sp.dma_start(ring[:, 2, :].rearrange("p (k n) -> p k n", k=FT),
                             moe_w_down[layer, e].rearrange("(k p) n -> p k n", p=P)).then_inc(dense_load[layer], 16)

            def dense(layer):
                sp.wait_ge(flag_ready, layer + 1)
                over = sp.value_load(flag[0:1, layer:layer + 1], min_val=0, max_val=1)
                with sp.If(over != 0):
                    sp.wait_ge(steps_done, (layer + 1) * LAYER_STEPS)
                    dense_expert(layer, 0)
                    with sp.Fori(0, NE - 1) as e:
                        sp.wait_ge(dense_y[layer], e * 4 + 4)
                        dense_expert(layer, e + 1)
                    sp.wait_ge(dense_y[layer], 4 * NE)

            mixer(0, ab_w_in[0], ab_w_out[0])
            experts(0)
            dense(0)
            mixer(1, diff_w_qkv[0], diff_w_o[0])
            experts(1)
            dense(1)
            sp.wait_ge(fin_ready, TT)
            sp.dma_start(out[0].rearrange("(t p) d -> p t d", p=P), xs[:, :, :]).then_inc(out_stored, 16)
            sp.wait_ge(out_stored, 16)

        @block.gpsimd
        def _(pool):
            steps = [0]

            def link(ins):
                steps[0] += 1
                ins.then_inc(pool_step, 1)
                pool.wait_ge(pool_step, steps[0])

            link(pool.memset(minus_half, -0.5))
            pool.memset(w_block[:, :, :, :], 0.0).then_inc(blocks_zeroed, 1)
            link(pool.memset(ident[:, :], 0.0))
            pool.affine_select(out=ident[:, :], in_=ident[:, :], compare_op=ALU.not_equal, fill=1.0, base=0,
                               pattern=[[-1, P]], channel_multiplier=1).then_inc(ident_ready, 1)
            link(pool.memset(ones[:, :], 1.0))
            pool.affine_select(out=before[:, :], in_=ones[:, :], compare_op=ALU.is_gt, fill=0.0, base=0,
                               pattern=[[1, P]], channel_multiplier=-1)
            pool.affine_select(out=upto[:, :], in_=ones[:, :], compare_op=ALU.is_ge, fill=0.0, base=0,
                               pattern=[[1, P]], channel_multiplier=-1)
            pool.iota(slot_no[:, :], pattern=[[1, CAP]], base=0, channel_multiplier=0,
                      allow_small_or_imprecise_dtypes=True)
            pool.iota(prio[:, :], pattern=[[-1, NE]], base=NE, channel_multiplier=0,
                      allow_small_or_imprecise_dtypes=True)
            pool.memset(zrow[:, :], 0.0).then_inc(consts_ready, 1)
            n_roots = [0]

            def inverse_root(v):
                n_roots[0] += 1
                pool.wait_ge(mean_ready, n_roots[0])
                pool.tensor_tensor(v, v, minus_half[:, 0:v.shape[1]], ALU.pow).then_inc(root_ready, 1)

            inverse_root(rstd)
            inverse_root(hss)
            inverse_root(rstd)
            inverse_root(rstd)
            pool.wait_ge(h_ready, 2)
            for t in range(TT):
                for n, sign in enumerate((1, -1)):
                    part = sp_[:, n, t, :]
                    link(pool.iota(part, pattern=[[sign, S]], base=-sign * t * P, channel_multiplier=-sign,
                                   allow_small_or_imprecise_dtypes=True))
                    link(pool.affine_select(out=part, in_=part, compare_op=ALU.is_gt, fill=0.0, base=sign * t * P,
                                            pattern=[[-sign, S]], channel_multiplier=sign))
                link(pool.tensor_tensor(dist[:, t, :], sp_[:, 0, t, :], sp_[:, 1, t, :], ALU.add))
            for t in range(TT):
                for c in range(P // CHUNK):
                    seen = t * P + (c + 1) * CHUNK
                    if seen < S:
                        ins = pool.memset(dist[c * CHUNK:(c + 1) * CHUNK, t, seen:S], -1e30)
            ins.then_inc(dist_ready, 1)
            inverse_root(oss)
            inverse_root(rstd)
            inverse_root(rstd)

        @block.tensor
        def _(pe):
            def feature_major(n):
                pe.wait_ge(xs_ready, n + 1)
                for i in range(4):
                    name = f"norm{n}.{i}"
                    wait_free(pe, name)
                    for c in range(2):
                        for t in range(TT):
                            k = 2 * i + c
                            ins = pe.transpose(bank_of(name)[:, c * S + t * P:c * S + (t + 1) * P],
                                               xs[:, t, k * P:(k + 1) * P], ident[:, :])
                    full(ins, name)

            def xT_complete(n):
                for i in range(4):
                    pe.wait_ge(fill_free[TURN[f"norm{n}.{i}"] % FILL_BANKS], TURN[f"norm{n}.{i}"] // FILL_BANKS + 1)

            def project_T(step, names):
                wait_slot(pe, step)
                w = slot_k(step)
                for i, name in enumerate(names):
                    wait_free(pe, name)
                    for c in range(2):
                        for k in range(KT):
                            n = (2 * i + c) * P
                            ins = pe.matmul(bank_of(name)[:, c * S:(c + 1) * S], w[:, k, n:n + P], xT[:, k, :],
                                            start=(k == 0), stop=(k == KT - 1))
                    full(ins, name)

            def project_N(step, names, lhs=xT, adds=None):
                wait_slot(pe, step)
                w = slot_k(step)
                for t, name in enumerate(names):
                    wait_free(pe, name)
                    for k in range(KT):
                        ins = pe.matmul(bank_of(name)[:, :], lhs[:, k, t * P:(t + 1) * P], w[:, k, :],
                                        start=(k == 0), stop=(k == KT - 1))
                    full(ins, name)

            def step_done(name):
                pe.wait_ge(fill_full[TURN[name] % FILL_BANKS], TURN[name] // FILL_BANKS + 1)
                pe.sem_inc(steps_done, 1)

            pe.wait_ge(ident_ready, 1)
            pe.wait_ge(rows_loaded, 16 * N_ROWS)
            full(pe.transpose(bank_of("columns")[:, 0:NR], rows[:, :], ident[0:NR, 0:NR]), "columns")
            feature_major(0)
            xT_complete(0)
            pe.wait_ge(params_loaded, 16 * N_PARAMS)
            wait_free(pe, "gates")
            for g in range(2):
                for k in range(KT):
                    ins = pe.matmul(bank_of("gates")[0:MH, g * S:(g + 1) * S], w_gate[:, k, g * MH:(g + 1) * MH],
                                    xT[:, k, :], start=(k == 0), stop=(k == KT - 1))
            full(ins, "gates")
            project_T(0, ["xa0", "xa1"])
            step_done("xa1")
            project_T(1, ["ga0", "ga1"])
            step_done("ga1")
            project_T(2, ["q0", "q1"])
            step_done("q1")
            pe.wait_ge(conv_done, 1)
            for j in range(WT):
                name = f"lru{j}"
                wait_free(pe, name)
                for g in range(2):
                    ins = pe.matmul(bank_of(name)[:, g * S:(g + 1) * S], w_block[:, g, j, :], xc[:, j, :],
                                    start=True, stop=True)
                full(ins, name)
            project_T(3, ["k0", "k1"])
            step_done("k1")
            project_N(4, ["v0", "v1"])
            step_done("v1")
            pe.wait_ge(am_rows, 1)
            wait_free(pe, "cols_am")
            for g, src in enumerate((gr[4], gr[5])):
                for t in range(TT):
                    at = (g * TT + t) * MH
                    ins = pe.transpose(bank_of("cols_am")[:, at:at + MH], src[:, t * P:(t + 1) * P],
                                       ident[0:MH, 0:MH])
            full(ins, "cols_am")
            project_T(5, ["o0", "o1"])
            step_done("o1")

            def head_scores(hd):
                name = f"mmax{hd}"
                wait_free(pe, name)
                full(pe.matmul(bank_of(name)[:, 0:S], ident[0:MH, hd:hd + 1].broadcast_to([MH, P]), gr[3],
                               start=True, stop=True), name)
                name = f"sc{hd}"
                wait_free(pe, name)
                pe.matmul(bank_of(name)[:, 0:S], kT[:, hd, 0:P], qT[:, hd, :], start=True, stop=True)
                full(pe.matmul(bank_of(name)[:, S:S + P], kT[:, hd, P:S], qT[:, hd, P:S], start=True, stop=True),
                     name)

            def head_values(hd):
                pe.wait_ge(p_ready, hd + 1)
                pb = pbuf[:, hd % 2, :]
                vh = slice(hd * P, (hd + 1) * P)
                pe.matmul(num_ps[0][:, vh], pb[:, 0:P], v_n[:, 0, vh], start=True, stop=True)
                pe.matmul(num_ps[1][:, vh], pb[:, P:2 * P], v_n[:, 0, vh], start=True, stop=False)
                pe.matmul(num_ps[1][:, vh], pb[:, 2 * P:3 * P], v_n[:, 1, vh], start=False, stop=True)
                pe.matmul(den_ps[:, hd:hd + 1], pb[:, 0:P], ones[:, 0:1], start=True, stop=True)
                pe.matmul(den_ps[:, MH + hd:MH + hd + 1], pb[:, P:2 * P], ones[:, 0:1], start=True, stop=False)
                pe.matmul(den_ps[:, MH + hd:MH + hd + 1], pb[:, 2 * P:3 * P], ones[:, 0:1], start=False,
                          stop=True).then_inc(num_done, 1)

            for name in ("q0", "q1", "k0", "k1", "v0", "v1"):
                pe.wait_ge(fill_free[TURN[name] % FILL_BANKS], TURN[name] // FILL_BANKS + 1)
            pe.wait_ge(consts_ready, 1)
            head_scores(0)
            for hd in range(MH):
                if hd + 1 < MH:
                    head_scores(hd + 1)
                head_values(hd)
            pe.wait_ge(yb_ready, 1)
            for i in range(2):
                name = f"yb{i}"
                wait_free(pe, name)
                for c in range(2):
                    for t in range(TT):
                        ins = pe.transpose(bank_of(name)[:, c * S + t * P:c * S + (t + 1) * P],
                                           yb[:, t, 2 * i + c, :], ident[:, :])
                full(ins, name)
            pe.wait_ge(ya_ready, 1)
            pe.wait_ge(yT_ready, 1)
            for n in range(NH):
                names = [f"mix0.{2 * n}", f"mix0.{2 * n + 1}"]
                project_N(6 + n, names, lhs=yT)
                step_done(names[-1])

            def gather(g):
                pe.wait_ge(sel_ready, g + 1)
                for part in range(2):
                    pe.wait_ge(gather_free, g * 3 + (part + 1))
                    for k in range(GH):
                        kt = part * GH + k
                        for t in range(TT):
                            ins = pe.matmul(gather_ps[:, k * P:(k + 1) * P], xs[:, t, kt * P:(kt + 1) * P],
                                            sel[:, t, :, :].rearrange("p e c -> p (e c)"), start=(t == 0),
                                            stop=(t == TT - 1))
                    ins.then_inc(gather_full, 1)
                    if part == 0:
                        yield
                pe.wait_ge(gather_free, g * 3 + 3)
                for t in range(TT):
                    ins = pe.transpose(gather_ps[:, t * P:(t + 1) * P],
                                       selg[:, t, :, :].rearrange("p e c -> p (e c)"), ident[:, :])
                ins.then_inc(gather_full, 1)

            def packed(layer, i, par):
                base = layer * LAYER_STEPS + MIX_STEPS
                b = i * 2 + (layer * NB + par)
                g = i * 2 + (layer * (NB + 1) + par + 1)
                buf = par
                nxt = gather(g)
                for n in range(KT):
                    j = par * MOE_STEPS + n
                    if n == 0:
                        pe.wait_ge(gather_free, g * 3 + 1)
                    pe.wait_ge(slot_loaded[j % SLOTS], i * (16 * 3) + 16 * ((base + j) // SLOTS + 1))
                    for half in range(NH):
                        for e in range(EB):
                            ins = pe.matmul(hy[half][e * CAP:(e + 1) * CAP, :], xg[:, buf, n, e * CAP:(e + 1) * CAP],
                                            slot_e(j)[:, e, half * HALF:(half + 1) * HALF],
                                            start=(n == 0), stop=(n == KT - 1), skip_group_check=True)
                    ins.then_inc(steps_done, 1)
                    if n == KT // 2 - 1:
                        next(nxt)
                for _ in nxt:
                    pass
                pe.wait_ge(hid_done, b + 1)
                for f in range(FT):
                    ins = pe.transpose(turn_ps[:, f * P:(f + 1) * P], hid[:, f * P:(f + 1) * P], ident[:, :])
                ins.then_inc(hT_full, 1)
                pe.wait_ge(hT_ready, b + 1)
                for n in range(FT):
                    j = par * MOE_STEPS + KT + n
                    pe.wait_ge(slot_loaded[j % SLOTS], i * (16 * 3) + 16 * ((base + j) // SLOTS + 1))
                    for half in range(NH):
                        for e in range(EB):
                            ins = pe.matmul(hy[half][e * CAP:(e + 1) * CAP, :], hT[:, n, e * CAP:(e + 1) * CAP],
                                            slot_e(j)[:, e, half * HALF:(half + 1) * HALF],
                                            start=(n == 0), stop=(n == FT - 1), skip_group_check=True)
                    ins.then_inc(steps_done, 1)
                pe.wait_ge(y_act, b + 1)
                pe.wait_ge(y_dve, b + 1)
                for t in range(TT):
                    for half in range(NH):
                        ins = pe.matmul(acc[t * NH + half][:, :], sgt[:, buf, t, :], y_s[:, half * HALF:(half + 1) * HALF],
                                        start=False, stop=False, skip_group_check=True)
                ins.then_inc(scattered, 1)

            def experts(layer):
                n = 1 + 2 * layer
                feature_major(n)
                xT_complete(n)
                name = f"router{layer}"
                wait_free(pe, name)
                for t in range(TT):
                    for k in range(KT):
                        at = t * (NG + NE)
                        ins = pe.matmul(bank_of(name)[:, at:at + NG + NE], xT[:, k, t * P:(t + 1) * P],
                                        w_route[:, layer, k, :], start=(k == 0), stop=(k == KT - 1))
                full(ins, name)
                name = f"rank{layer}"
                wait_free(pe, name)
                pe.wait_ge(picked, layer + 1)
                bank = bank_of(name)
                pe.matmul(bank[:, 0:NE], before[:, :], both[:, 0, :], start=True, stop=True)
                pe.matmul(bank[:, NE:2 * NE], ones[:, :], both[:, 0, :], start=True, stop=False)
                pe.matmul(bank[:, NE:2 * NE], before[:, :], both[:, 1, :], start=False, stop=True)
                pe.matmul(bank[:, 2 * NE:3 * NE], ones[:, :], both[:, 0, :], start=True, stop=False)
                full(pe.matmul(bank[:, 2 * NE:3 * NE], ones[:, :], both[:, 1, :], start=False, stop=True), name)
                for a in acc:
                    pe.matmul(a[:, :], zrow[:, :], h[0:1, 0, 0:HALF], start=True, stop=False, skip_group_check=True)
                for b in range(FILL_BANKS):
                    last = max(t for t in range(TURN[name] + 1) if t % FILL_BANKS == b)
                    pe.wait_ge(fill_free[b], last // FILL_BANKS + 1)
                for _ in gather(layer * (NB + 1)):
                    pass
                with pe.Fori(0, NB // 2) as i:
                    for par in range(2):
                        packed(layer, i, par)

            def dense(layer):
                pe.wait_ge(flag_ready, layer + 1)
                over = pe.value_load(flag[0:1, layer:layer + 1], min_val=0, max_val=1)
                with pe.If(over != 0):
                    up = ring[:, 0:2, :].rearrange("p a (k n) -> p (a k) n", k=KT // 2)
                    down = ring[:, 2, :].rearrange("p (k n) -> p k n", k=FT)
                    with pe.Fori(0, NE) as e:
                        pe.wait_ge(dense_load[layer], e * 32 + 32)
                        for f in range(FT):
                            pe.wait_ge(dense_h[layer], e * FT + (f + 1))
                            for g in range(2):
                                for k in range(KT):
                                    ins = pe.matmul(psum[f % 2][:, g * S:(g + 1) * S],
                                                    up[:, k, g * FF + f * P:g * FF + (f + 1) * P], xT[:, k, :],
                                                    start=(k == 0), stop=(k == KT - 1))
                            ins.then_inc(dense_gu[layer], 1)
                        pe.wait_ge(dense_h[layer], e * FT + (FT + 2))
                        for n in range(TT * NH):
                            pe.wait_ge(dense_add[layer], e * 4 + (n + 1))
                            for f in range(FT):
                                ins = pe.matmul(psum[2 + n % 2][:, :], ovh[:, f, (n // NH) * P:(n // NH + 1) * P],
                                                down[:, f, (n % NH) * HALF:(n % NH + 1) * HALF],
                                                start=(f == 0), stop=(f == FT - 1))
                            ins.then_inc(dense_y[layer], 1)

            experts(0)
            dense(0)

            feature_major(2)
            xT_complete(2)
            s1 = LAYER_STEPS
            for n in range(2):
                project_T(s1 + n, [f"dq{2 * n}", f"dq{2 * n + 1}"])
                step_done(f"dq{2 * n + 1}")
            for n in range(2):
                project_T(s1 + 2 + n, [f"dk{2 * n}", f"dk{2 * n + 1}"])
                step_done(f"dk{2 * n + 1}")
            for n in range(2):
                project_N(s1 + 4 + n, [f"dv{2 * n}", f"dv{2 * n + 1}"])
                step_done(f"dv{2 * n + 1}")

            def unit_scores(u):
                hd, t = u // TT, u % TT
                nk = (t + 1) * P
                for c in range(2):
                    name = f"ds{u}.{c}"
                    wait_free(pe, name)
                    full(pe.matmul(bank_of(name)[:, 0:nk], dq[c * DQK:(c + 1) * DQK, hd, t * P:(t + 1) * P],
                                   dk[c * DQK:(c + 1) * DQK, hd, 0:nk], start=True, stop=True), name)

            def unit_values(u):
                hd, t = u // TT, u % TT
                name = f"dt{u}"
                wait_free(pe, name)
                pe.wait_ge(diff_ready, u + 1)
                for kt in range(t + 1):
                    ins = pe.transpose(bank_of(name)[:, kt * P:(kt + 1) * P], dif[:, u % 2, kt * P:(kt + 1) * P],
                                       ident[:, :])
                full(ins, name)
                pe.wait_ge(fill_free[TURN[name] % FILL_BANKS], TURN[name] // FILL_BANKS + 1)
                at = (hd % 4) * P
                for kt in range(t + 1):
                    ins = pe.matmul(o_ps[t * NH + hd // 4][:, at:at + P], dT[:, u % 2, kt * P:(kt + 1) * P],
                                    dv[:, kt, hd * P:(hd + 1) * P], start=(kt == 0), stop=(kt == t))
                ins.then_inc(pv_done, 1)

            for name in [f"{x}{i}" for x in ("dq", "dk", "dv") for i in range(4)]:
                pe.wait_ge(fill_free[TURN[name] % FILL_BANKS], TURN[name] // FILL_BANKS + 1)
            unit_scores(0)
            for u in range(TT * DH):
                if u + 1 < TT * DH:
                    unit_scores(u + 1)
                unit_values(u)
            pe.wait_ge(on_ready, 1)
            for i in range(4):
                name = f"dy{i}"
                wait_free(pe, name)
                for c in range(2):
                    for t in range(TT):
                        k = 2 * i + c
                        ins = pe.transpose(bank_of(name)[:, c * S + t * P:c * S + (t + 1) * P],
                                           on[:, t, k * P:(k + 1) * P], ident[:, :])
                full(ins, name)
            for i in range(4):
                pe.wait_ge(fill_free[TURN[f"dy{i}"] % FILL_BANKS], TURN[f"dy{i}"] // FILL_BANKS + 1)
            for n in range(NH):
                names = [f"mix1.{2 * n}", f"mix1.{2 * n + 1}"]
                project_N(s1 + 6 + n, names, lhs=yT)
                step_done(names[-1])
            experts(1)
            dense(1)

        @block.scalar
        def _(act):
            n_rows = [0]

            def load_rows(at, src):
                n = src.shape[0]
                act.dma_start(rows[at:at + n, :], src).then_inc(rows_loaded, 16)
                n_rows[0] += 1

            load_rows(R_MIX, norm_mix_g.rearrange("l (k p) -> (l k) p", p=P))
            load_rows(R_FFN, norm_ffn_g.rearrange("l (k p) -> (l k) p", p=P))
            load_rows(R_CW, lru_conv_w[0].rearrange("w (k p) -> (w k) p", p=P))
            load_rows(R_CB, lru_conv_b[0].rearrange("(k p) -> k p", p=P))
            load_rows(R_BR, lru_b_r[0].rearrange("(k p) -> k p", p=P))
            load_rows(R_BI, lru_b_i[0].rearrange("(k p) -> k p", p=P))
            load_rows(R_LAM, lru_lambda[0].rearrange("(k p) -> k p", p=P))
            load_rows(R_MNG, mlstm_norm_g[0])
            load_rows(R_DNG, diff_norm_g[0])
            assert n_rows[0] == N_ROWS

            n_params = [0]

            def load(dst, src):
                act.dma_start(dst, src).then_inc(params_loaded, 16)
                n_params[0] += 1

            load(w_gate[:, :, :], ab_w_in[0][:, 6 * HALF:6 * HALF + 2 * MH].rearrange("(k p) n -> p k n", p=P))
            load(b_if[:, 0:1], mlstm_b_i.rearrange("a h -> h a"))
            load(b_if[:, 1:2], mlstm_b_f.rearrange("a h -> h a"))
            act.wait_ge(blocks_zeroed, 1)
            for g, w in enumerate((lru_w_r, lru_w_i)):
                for half in range(2):
                    lo = half * 64
                    load(w_block[lo:lo + 64, g, :, lo:lo + 64],
                         w[0].rearrange("(j b) d e -> b d j e", b=2)[half])
            for layer in range(LAYERS):
                load(w_route[:, layer, :, 0:NG], moe_w_group[layer].rearrange("(k p) n -> p k n", p=P))
                load(w_route[:, layer, :, NG:], moe_w_expert[layer].rearrange("(k p) n -> p k n", p=P))
                load(b_route[:, layer, 0:NG], moe_b_group[layer].partition_broadcast(P))
                load(b_route[:, layer, NG:], moe_b_expert[layer].partition_broadcast(P))
            for n, v in enumerate((diff_lambda_q1, diff_lambda_k1, diff_lambda_q2, diff_lambda_k2)):
                load(lam_rows[:, n, :], v[0].partition_broadcast(P))
            assert n_params[0] == N_PARAMS

            def norm_squares(n):
                if n == 0:
                    act.wait_ge(x_loaded, 16)
                else:
                    act.wait_ge(h_ready, n)
                for t in range(TT):
                    act.activation(xs[:, t, :], h[:, t, :], ACT.Square, accum_out=ss[:, t:t + 1])\
                        .then_inc(squares, 1)

            def copy_fill(dst, name):
                wait_full(act, name)
                free(act.activation(dst, bank_of(name)[:, :], ACT.Copy), name)

            def pair(t, i):
                return t[:, 2 * i:2 * i + 2, :].rearrange("p a s -> p (a s)")

            norm_squares(0)
            act.wait_ge(lam_abs, 1)
            act.activation(l1b, l1a, ACT.Exp, scale=-1.0).then_inc(lam_exp, 1)
            act.wait_ge(f_abs, 1)
            act.activation(gr[2], gr[2], ACT.Exp, scale=-1.0).then_inc(f_exp, 1)
            for i in range(2):
                name = f"xa{i}"
                wait_full(act, name)
                free(act.activation(xpad[:, 2 * i:2 * i + 2, TAPS - 1:],
                                    bank_of(name)[:, :].rearrange("p (a s) -> p a s", a=2), ACT.Copy), name)
            for i in range(2):
                copy_fill(pair(ga, i), f"ga{i}")
            for i in range(2):
                copy_fill(pair(qT, i), f"q{i}")
            for j in range(WT):
                name = f"lru{j}"
                wait_full(act, name)
                act.activation(r_g[:, j, :], bank_of(name)[:, 0:S], ACT.Sigmoid, bias=cols[:, R_BR + j:R_BR + j + 1])
                free(act.activation(i_g[:, j, :], bank_of(name)[:, S:2 * S], ACT.Sigmoid,
                                    bias=cols[:, R_BI + j:R_BI + j + 1]), name)
            for j in range(WT):
                name = f"lru{j}"
                act.wait_ge(fill_free[TURN[name] % FILL_BANKS], TURN[name] // FILL_BANKS + 1)
            for j in range(WT):
                ins = act.activation(r_g[:, j, :], r_g[:, j, :], ACT.Tanh, scale=c4[:, j:j + 1])
            ins.then_inc(lru_tanh, 1)
            act.wait_ge(gelu_in, 1)
            act.activation(yT[:, 0:WT, :].rearrange("p a s -> p (a s)"),
                           yT[:, 0:WT, :].rearrange("p a s -> p (a s)"), ACT.Tanh,
                           scale=math.sqrt(2.0 / math.pi)).then_inc(gelu_tanh, 1)
            act.wait_ge(lru_floor, 1)
            act.activation(root, root, ACT.Sqrt).then_inc(lru_root, 1)
            for i in range(2):
                copy_fill(pair(kT, i), f"k{i}")
            for t in range(TT):
                copy_fill(v_n[:, t, :], f"v{t}")
            for i in range(2):
                name = f"o{i}"
                wait_full(act, name)
                free(act.activation(pair(so, i), bank_of(name)[:, :], ACT.Sigmoid), name)
            act.wait_ge(am_cols, 1)
            act.activation(enm, am[:, 8:16], ACT.Exp).then_inc(enm_ready, 1)
            for hd in range(MH):
                act.wait_ge(w_arg, hd + 1)
                act.activation(wbuf[:, hd % 2, :], wbuf[:, hd % 2, :], ACT.Exp, scale=-1.0).then_inc(w_exp, 1)

            def packed(layer, i, par):
                b = i * 2 + (layer * NB + par)
                steps = i * (2 * MOE_STEPS) + (layer * LAYER_STEPS + MIX_STEPS + par * MOE_STEPS)
                act.wait_ge(steps_done, steps + KT)
                act.activation(sig, hy[0][:, :], ACT.Sigmoid).then_inc(sig_done, 1)
                act.wait_ge(hT_full, b + 1)
                act.activation(hT[:, :, :].rearrange("p f c -> p (f c)"), turn_ps[:, :], ACT.Copy)\
                    .then_inc(hT_ready, 1)
                act.wait_ge(steps_done, steps + MOE_STEPS)
                act.activation(y_s[:, 0:HALF], hy[0][:, :], ACT.Copy).then_inc(y_act, 1)

            def experts(layer):
                norm_squares(1 + 2 * layer)
                act.wait_ge(route_arg, layer + 1)
                act.activation(rs[:, 10:20], rs[:, 0:10], ACT.Exp).then_inc(route_exp, 1)
                with act.Fori(0, NB // 2) as i:
                    for par in range(2):
                        packed(layer, i, par)

            def dense(layer):
                act.wait_ge(flag_ready, layer + 1)
                over = act.value_load(flag[0:1, layer:layer + 1], min_val=0, max_val=1)
                with act.If(over != 0):
                    with act.Fori(0, NE) as e:
                        for f in range(FT):
                            act.wait_ge(dense_gu[layer], e * FT + (f + 1))
                            act.wait_ge(dense_h[layer], e * FT + (f + 2))
                            act.activation(ovs, psum[f % 2][:, 0:S], ACT.Sigmoid).then_inc(dense_sig[layer], 1)

            experts(0)
            dense(0)

            norm_squares(2)
            act.wait_ge(lsum_ready, 1)
            act.activation(lsum, lsum, ACT.Exp).then_inc(lsum_exp, 1)
            for x, dst in (("dq", dq), ("dk", dk)):
                for i in range(4):
                    copy_fill(pair(dst, i), f"{x}{i}")
            for n in range(NH):
                for t in range(TT):
                    copy_fill(dv[:, t, n * HALF:(n + 1) * HALF], f"dv{2 * n + t}")
            def unit_exp(u):
                nk = (u % TT + 1) * P
                act.wait_ge(soft_max, u + 1)
                for c in range(2):
                    ins = act.activation(sp_[:, u % 2, c, 0:nk], sp_[:, u % 2, c, 0:nk], ACT.Exp, scale=Q_SCALE,
                                         bias=mx[:, 2 * (u % 2) + c:2 * (u % 2) + c + 1],
                                         accum_out=sums[:, 2 * (u % 2) + c:2 * (u % 2) + c + 1])
                ins.then_inc(soft_exp, 1)

            def unit_turn(u):
                nk = (u % TT + 1) * P
                name = f"dt{u}"
                wait_full(act, name)
                free(act.activation(dT[:, u % 2, 0:nk], bank_of(name)[:, 0:nk], ACT.Copy), name)

            unit_exp(0)
            for u in range(TT * DH):
                if u + 1 < TT * DH:
                    unit_exp(u + 1)
                unit_turn(u)
            act.wait_ge(pv_done, TT * DH)
            for t in range(TT):
                for n in range(NH):
                    act.activation(on[:, t, n * HALF:(n + 1) * HALF], o_ps[t * NH + n][:, :], ACT.Copy)\
                        .then_inc(o_copied, 1)
            experts(1)
            act.dma_start(fg, final_norm_g.partition_broadcast(P)).then_inc(fgain_loaded, 16)
            dense(1)
            norm_squares(4)

        @block.vector
        def _(dve):
            steps = [0]
            roots = [0]

            def link(ins):
                steps[0] += 1
                ins.then_inc(dve_step, 1)
                dve.wait_ge(dve_step, steps[0])

            def log1p(y, z, q):
                link(dve.tensor_scalar(z, y, 2.0, None, ALU.add))
                link(dve.reciprocal(z, z))
                link(dve.tensor_tensor(z, z, y, ALU.mult))
                link(dve.tensor_tensor(y, z, z, ALU.mult))
                link(dve.tensor_scalar(q, y, 1.0 / 15, None, ALU.mult))
                for odd in (13, 11, 9, 7, 5, 3):
                    link(dve.scalar_tensor_tensor(out=q, in0=q, scalar=1.0 / odd, in1=y, op0=ALU.add, op1=ALU.mult))
                link(dve.scalar_tensor_tensor(out=q, in0=q, scalar=1.0, in1=z, op0=ALU.add, op1=ALU.mult))
                link(dve.tensor_scalar(y, q, 2.0, None, ALU.mult))

            def inverse_root(dst, src, n):
                dve.tensor_scalar(dst, src, 1.0 / n, EPS, ALU.mult, ALU.add).then_inc(mean_ready, 1)
                roots[0] += 1
                dve.wait_ge(root_ready, roots[0])

            def norm_rows(n, gain=None):
                dve.wait_ge(squares, TT * (n + 1))
                inverse_root(rstd, ss, D)
                for t in range(TT):
                    ins = dve.tensor_scalar(xs[:, t, :], h[:, t, :], rstd[:, t:t + 1], None, ALU.mult)
                ins.then_inc(xs_ready, 1)

            def norm_turned(n, at):
                for i in range(4):
                    name = f"norm{n}.{i}"
                    wait_full(dve, name)
                    g = cols[:, at + 2 * i:at + 2 * i + 2].unsqueeze(2).broadcast_to([P, 2, S])
                    free(dve.tensor_tensor(xT[:, 2 * i:2 * i + 2, :],
                                           bank_of(name)[:, :].rearrange("p (a s) -> p a s", a=2), g, ALU.mult), name)

            dve.memset(xpad[:, :, 0:TAPS - 1], 0.0)
            wait_full(dve, "columns")
            free(dve.tensor_copy(cols[:, :], bank_of("columns")[:, 0:NR]), "columns")
            dve.wait_ge(fill_free[TURN["columns"] % FILL_BANKS], 1)
            norm_rows(0)
            lam_c = cols[:, R_LAM:R_LAM + WT]
            dve.scalar_tensor_tensor(out=l1a, in0=lam_c, scalar=-1.0, in1=lam_c, op0=ALU.mult, op1=ALU.max)\
                .then_inc(lam_abs, 1)
            norm_turned(0, R_MIX)
            dve.wait_ge(lam_exp, 1)
            log1p(l1b, l1a, l1c)
            link(dve.tensor_scalar(l1a, lam_c, -1.0, 0.0, ALU.mult, ALU.max))
            link(dve.tensor_tensor(l1a, l1a, l1b, ALU.add))
            link(dve.tensor_scalar(c4, l1a, LRU_C / 2, None, ALU.mult))
            ig, fgr, tabs, mmax, a_row, nm_row = gr
            name = "gates"
            wait_full(dve, name)
            dve.wait_ge(params_loaded, 16 * N_PARAMS)
            dve.tensor_scalar(ig[:, :], bank_of(name)[0:MH, 0:S], b_if[:, 0:1], None, ALU.add)
            free(dve.tensor_scalar(fgr[:, :], bank_of(name)[0:MH, S:2 * S], b_if[:, 1:2], None, ALU.add), name)
            dve.wait_ge(fill_free[TURN[name] % FILL_BANKS], TURN[name] // FILL_BANKS + 1)
            dve.scalar_tensor_tensor(out=tabs, in0=fgr[:, :], scalar=-1.0, in1=fgr[:, :], op0=ALU.mult,
                                     op1=ALU.max).then_inc(f_abs, 1)
            dve.wait_ge(f_exp, 1)
            log1p(tabs, mmax, a_row)
            link(dve.tensor_scalar(fgr[:, :], fgr[:, :], -1.0, 0.0, ALU.mult, ALU.max))
            link(dve.tensor_tensor(fgr[:, :], fgr[:, :], tabs, ALU.add))
            link(dve.tensor_tensor_scan(tabs, fgr[:, :], fgr[:, :], 0.0, ALU.add, ALU.max))
            link(dve.tensor_tensor(a_row, ig[:, :], tabs, ALU.add))
            link(dve.tensor_tensor_scan(mmax, a_row, a_row, 0.0, ALU.max, ALU.max))
            dve.tensor_tensor(nm_row, tabs, mmax, ALU.subtract).then_inc(am_rows, 1)

            for i in range(2):
                name = f"xa{i}"
                dve.wait_ge(fill_free[TURN[name] % FILL_BANKS], TURN[name] // FILL_BANKS + 1)
            for w in range(TAPS - 1, -1, -1):
                for j in range(WT):
                    cw = cols[:, R_CW + w * WT + j:R_CW + w * WT + j + 1]
                    src = xpad[:, j, w:w + S]
                    if w == TAPS - 1:
                        ins = dve.tensor_scalar(xc[:, j, :], src, cw, cols[:, R_CB + j:R_CB + j + 1], ALU.mult, ALU.add)
                    else:
                        ins = dve.scalar_tensor_tensor(out=xc[:, j, :], in0=src, scalar=cw, in1=xc[:, j, :],
                                                       op0=ALU.mult, op1=ALU.add)
                if w:
                    link(ins)
            ins.then_inc(conv_done, 1)
            for i in range(2):
                name = f"ga{i}"
                dve.wait_ge(fill_free[TURN[name] % FILL_BANKS], TURN[name] // FILL_BANKS + 1)
            dve.wait_ge(fill_full[TURN["norm0.3"] % FILL_BANKS], TURN["norm0.3"] // FILL_BANKS + 1)
            gt = yT[:, 0:WT, :].rearrange("p a s -> p (a s)")
            link(dve.tensor_tensor(gt, ga_f, ga_f, ALU.mult))
            link(dve.tensor_scalar(gt, gt, 0.044715, 1.0, ALU.mult, ALU.add))
            dve.tensor_tensor(gt, gt, ga_f, ALU.mult).then_inc(gelu_in, 1)
            dve.wait_ge(conv_done, 1)
            dve.wait_ge(lru_tanh, 1)
            dve.tensor_scalar(root, r_f, 1e-34, None, ALU.max).then_inc(lru_floor, 1)
            link(dve.tensor_scalar(t1_f, r_f, 1.0, None, ALU.add))
            link(dve.reciprocal(t1_f, t1_f))
            link(dve.tensor_tensor(i_f, i_f, xc_f, ALU.mult))
            dve.wait_ge(lru_root, 1)
            link(dve.scalar_tensor_tensor(out=root, in0=root, scalar=2.0, in1=t1_f, op0=ALU.mult, op1=ALU.mult))
            link(dve.tensor_tensor(i_f, i_f, root, ALU.mult))
            link(dve.tensor_scalar(r_f, r_f, -1.0, 1.0, ALU.mult, ALU.add))
            link(dve.tensor_tensor(r_f, r_f, t1_f, ALU.mult))
            for j in range(WT):
                ins = dve.tensor_tensor_scan(xc[:, j, :], r_g[:, j, :], i_g[:, j, :], 0.0, ALU.mult, ALU.add)
            link(ins)
            dve.wait_ge(gelu_tanh, 1)
            link(dve.scalar_tensor_tensor(out=ga_f, in0=gt, scalar=1.0, in1=ga_f, op0=ALU.add, op1=ALU.mult))
            dve.scalar_tensor_tensor(out=gt, in0=ga_f, scalar=0.5, in1=xc_f, op0=ALU.mult, op1=ALU.mult)\
                .then_inc(ya_ready, 1)

            name = "cols_am"
            wait_full(dve, name)
            free(dve.tensor_copy(am, bank_of(name)[:, 0:16]), name)
            dve.wait_ge(fill_free[TURN[name] % FILL_BANKS], TURN[name] // FILL_BANKS + 1)

            def head_args(hd):
                name = f"mmax{hd}"
                wait_full(dve, name)
                bank = bank_of(name)
                if hd >= 2:
                    dve.wait_ge(p_ready, hd - 1)
                dve.tensor_scalar(wbuf[:, hd % 2, 0:S], bank[:, 0:S], am[:, hd:hd + 1], 0.0, ALU.subtract, ALU.max)
                free(dve.tensor_scalar(wbuf[:, hd % 2, S:S + P], bank[:, P:S], am[:, MH + hd:MH + hd + 1], 0.0,
                                       ALU.subtract, ALU.max), name)
                dve.wait_ge(fill_free[TURN[name] % FILL_BANKS], TURN[name] // FILL_BANKS + 1)
                dve.tensor_copy(lrow[:, 0:1], am[:, 0:1]).then_inc(w_arg, 1)

            def head_weights(hd):
                name = f"sc{hd}"
                dve.wait_ge(w_exp, hd + 1)
                w = wbuf[:, hd % 2, :]
                diag = w.rearrange("p (a c) -> p a c", a=3)[:, 0:3:2, :]
                link(dve.tensor_tensor(diag, diag, upto[:, :].unsqueeze(1).broadcast_to([P, 2, P]), ALU.mult))
                wait_full(dve, name)
                if hd >= 2:
                    dve.wait_ge(num_done, hd - 1)
                free(dve.scalar_tensor_tensor(out=pbuf[:, hd % 2, :], in0=bank_of(name)[:, 0:S + P], scalar=K_SCALE,
                                              in1=w, op0=ALU.mult, op1=ALU.mult), name)
                dve.wait_ge(fill_free[TURN[name] % FILL_BANKS], TURN[name] // FILL_BANKS + 1)
                dve.tensor_copy(lrow[:, 1:2], am[:, 0:1]).then_inc(p_ready, 1)

            dve.tensor_copy(lrow[:, 2:3], am[:, 0:1]).then_inc(am_cols, 1)
            dve.wait_ge(consts_ready, 1)
            head_args(0)
            for hd in range(MH):
                if hd + 1 < MH:
                    head_args(hd + 1)
                head_weights(hd)
            dve.wait_ge(num_done, MH)
            link(dve.tensor_copy(den, den_ps[:, 0:8]))
            link(dve.scalar_tensor_tensor(out=den2, in0=den, scalar=-1.0, in1=den, op0=ALU.mult, op1=ALU.max))
            dve.wait_ge(enm_ready, 1)
            link(dve.tensor_tensor(den2, den2, enm, ALU.max))
            link(dve.reciprocal(den, den2))
            for t in range(TT):
                ins = dve.tensor_tensor(yb[:, t, :, :], num_ps[t][:, :].rearrange("p (h e) -> p h e", h=MH),
                                        den[:, t * MH:(t + 1) * MH].unsqueeze(2).broadcast_to([P, MH, P]), ALU.mult)
            link(ins)
            yb_v = yb.rearrange("p t h e -> p (t h) e")
            sq_v = sq.rearrange("p t h e -> p (t h) e")
            link(dve.tensor_tensor(sq_v, yb_v, yb_v, ALU.mult))
            link(dve.tensor_reduce(hss, sq_v, AX.X, ALU.add))
            inverse_root(hss, hss, P)
            dve.tensor_tensor(yb_v, yb_v, hss.unsqueeze(2).broadcast_to([P, 8, P]), ALU.mult).then_inc(yb_ready, 1)
            for i in range(2):
                name = f"yb{i}"
                wait_full(dve, name)
                for c in range(2):
                    hd = 2 * i + c
                    dve.wait_ge(fill_free[TURN[f"o{i}"] % FILL_BANKS], TURN[f"o{i}"] // FILL_BANKS + 1)
                    ins = dve.scalar_tensor_tensor(out=yT[:, WT + hd, :], in0=bank_of(name)[:, c * S:(c + 1) * S],
                                                   scalar=cols[:, R_MNG + hd:R_MNG + hd + 1], in1=so[:, hd, :],
                                                   op0=ALU.mult, op1=ALU.mult)
                free(ins, name)
            dve.wait_ge(fill_free[TURN["yb1"] % FILL_BANKS], TURN["yb1"] // FILL_BANKS + 1)
            dve.tensor_copy(lrow[:, 3:4], am[:, 0:1]).then_inc(yT_ready, 1)

            def residual(layer):
                for n in range(NH):
                    for t in range(TT):
                        name = f"mix{layer}.{2 * n + t}"
                        wait_full(dve, name)
                        hh = h[:, t, n * HALF:(n + 1) * HALF]
                        free(dve.tensor_tensor(hh, bank_of(name)[:, :], hh, ALU.add), name)
                dve.wait_ge(fill_free[TURN[name] % FILL_BANKS], TURN[name] // FILL_BANKS + 1)
                dve.tensor_copy(small[:, 135:136], h[:, 0, 0:1]).then_inc(h_ready, 1)

            residual(0)

            def bc(v, n):
                return v.broadcast_to([P, TT, n])

            def first_max(mask, values, best, n):
                link(dve.tensor_tensor(mask, values, bc(best, n), ALU.is_equal))
                link(dve.tensor_tensor(mask, mask, prio[:, 0:n].unsqueeze(1).broadcast_to([P, TT, n]), ALU.mult))
                link(dve.tensor_reduce(rs2[:, :, 2], mask, AX.X, ALU.max))
                link(dve.tensor_tensor(mask, mask, bc(rs2[:, :, 2:3], n), ALU.is_equal))

            def route(layer):
                name = f"router{layer}"
                wait_full(dve, name)
                ex = rs[:, 0:10].rearrange("p (t n) -> p t n", t=TT)
                eo = rs[:, 10:20].rearrange("p (t n) -> p t n", t=TT)
                best, best2 = rs2[:, :, 0:1], rs2[:, :, 1:2]
                free(dve.tensor_tensor(lg, bank_of(name)[:, 0:TT * (NG + NE)].rearrange("p (t n) -> p t n", t=TT),
                                       b_route[:, layer, :].unsqueeze(1).broadcast_to([P, TT, NG + NE]), ALU.add),
                     name)
                dve.wait_ge(fill_free[TURN[name] % FILL_BANKS], TURN[name] // FILL_BANKS + 1)
                gl = lg[:, :, 0:NG]
                link(dve.tensor_reduce(rs2[:, :, 0], gl, AX.X, ALU.max))
                link(dve.tensor_tensor(ex[:, :, 0:NG], gl, bc(best, NG), ALU.subtract))
                first_max(mg, gl, best, NG)
                mg_e = mg.unsqueeze(3).broadcast_to([P, TT, NG, EPG])
                el4 = el.rearrange("p t (g e) -> p t g e", g=NG)
                tmp4 = tmp.rearrange("p t (g e) -> p t g e", g=NG)
                link(dve.tensor_tensor(el4, lg[:, :, NG:].rearrange("p t (g e) -> p t g e", g=NG), mg_e, ALU.mult))
                link(dve.tensor_scalar(tmp4, mg_e, 1.0, 1e30, ALU.subtract, ALU.mult))
                link(dve.tensor_tensor(el, el, tmp, ALU.add))
                link(dve.tensor_reduce(rs2[:, :, 0], el, AX.X, ALU.max))
                first_max(m1, el, best, NE)
                link(dve.scalar_tensor_tensor(out=el, in0=m1, scalar=-3e30, in1=el, op0=ALU.mult, op1=ALU.add))
                link(dve.tensor_reduce(rs2[:, :, 1], el, AX.X, ALU.max))
                dve.tensor_tensor(ex[:, :, NG], rs2[:, :, 1], rs2[:, :, 0], ALU.subtract).then_inc(route_arg, 1)
                first_max(m2, el, best2, NE)
                dve.tensor_tensor(both, m1, m2, ALU.add).then_inc(picked, 1)
                dve.wait_ge(route_exp, layer + 1)
                link(dve.tensor_reduce(rs2[:, :, 0], eo[:, :, 0:NG], AX.X, ALU.add))
                link(dve.tensor_scalar(rs2[:, :, 1], eo[:, :, NG], 1.0, None, ALU.add))
                link(dve.tensor_tensor(rs2[:, :, 0], rs2[:, :, 0], rs2[:, :, 1], ALU.mult))
                link(dve.reciprocal(rs2[:, :, 0], rs2[:, :, 0]))
                link(dve.tensor_tensor(rs2[:, :, 1], rs2[:, :, 0], eo[:, :, NG], ALU.mult))
                link(dve.tensor_tensor(m1, m1, bc(best, NE), ALU.mult))
                link(dve.tensor_tensor(m2, m2, bc(best2, NE), ALU.mult))
                link(dve.memset(gates[:, :, NE:], 0.0))
                link(dve.memset(rankm[:, :, NE:], -1.0))
                link(dve.tensor_tensor(gates[:, :, 0:NE], m1, m2, ALU.add))
                name = f"rank{layer}"
                wait_full(dve, name)
                rank = bank_of(name)[:, 0:TT * NE].rearrange("p (t n) -> p t n", t=TT)
                link(dve.tensor_scalar(el, rank, 1.0, None, ALU.add))
                link(dve.tensor_tensor(el, el, both, ALU.mult))
                link(dve.tensor_scalar(rankm[:, :, 0:NE], el, 1.0, None, ALU.subtract))
                link(dve.tensor_scalar(el, el, CAP + 0.5, None, ALU.is_gt))
                link(dve.tensor_tensor(extra, el, gates[:, :, 0:NE], ALU.mult))
                link(dve.tensor_reduce(small[0:1, 134:135], bank_of(name)[0:1, 2 * NE:3 * NE], AX.X, ALU.max))
                free(dve.tensor_copy(small[0:1, 133:134], bank_of(name)[0:1, 0:1]), name)
                dve.tensor_scalar(flag[0:1, layer:layer + 1], small[0:1, 134:135], CAP + 0.5, None, ALU.is_gt)\
                    .then_inc(flag_ready, 1)

            def places(e0, g):
                dve.tensor_tensor(sel, slot_no[:, :].unsqueeze(1).unsqueeze(1).broadcast_to([P, TT, EB, CAP]),
                                  rankm[:, :, bass.ds(e0, EB)].unsqueeze(3).broadcast_to([P, TT, EB, CAP]),
                                  ALU.is_equal).then_inc(sel_step, 1)
                dve.wait_ge(sel_step, g + 1)
                dve.tensor_tensor(selg, sel, gates[:, :, bass.ds(e0, EB)].unsqueeze(3)
                                  .broadcast_to([P, TT, EB, CAP]), ALU.mult).then_inc(sel_ready, 1)

            def take_gathered(layer, g, buf, part):
                at = R_FFN + layer * KT + part * GH
                dve.wait_ge(gather_full, g * 3 + (part + 1))
                dve.tensor_tensor(xg[:, buf, part * GH:(part + 1) * GH, :],
                                  gather_ps[:, :].rearrange("p (k c) -> p k c", k=GH),
                                  cols[:, at:at + GH].unsqueeze(2).broadcast_to([P, GH, P]), ALU.mult)\
                    .then_inc(gather_free, 1)

            def take_gates(g, buf):
                dve.wait_ge(gather_full, g * 3 + 3)
                dve.tensor_copy(sgt[:, buf, :, :].rearrange("p t c -> p (t c)"), gather_ps[:, 0:TT * P])\
                    .then_inc(gather_free, 1)

            def packed(layer, i, par):
                b = i * 2 + (layer * NB + par)
                g = i * 2 + (layer * (NB + 1) + par + 1)
                done = i * (2 * MOE_STEPS) + (layer * LAYER_STEPS + MIX_STEPS + par * MOE_STEPS)
                places(i * (2 * EB) + (par + 1) * EB, g)
                take_gathered(layer, g, 1 - par, 0)
                take_gathered(layer, g, 1 - par, 1)
                dve.wait_ge(steps_done, done + KT)
                dve.wait_ge(sig_done, b + 1)
                dve.tensor_tensor(sig, sig, hy[0][:, :], ALU.mult).then_inc(hid_step, 1)
                dve.wait_ge(hid_step, b + 1)
                dve.tensor_tensor(hid, sig, hy[1][:, :], ALU.mult).then_inc(hid_done, 1)
                take_gates(g, 1 - par)
                dve.wait_ge(steps_done, done + MOE_STEPS)
                dve.tensor_copy(y_s[:, HALF:D], hy[1][:, :]).then_inc(y_dve, 1)

            def dense(layer):
                dve.wait_ge(flag_ready, layer + 1)
                over = dve.value_load(flag[0:1, layer:layer + 1], min_val=0, max_val=1)
                with dve.If(over != 0):
                    dve.memset(ovs, 0.0).then_inc(dense_h[layer], 2)
                    dve.memset(small[:, 132:133], 0.0).then_inc(dense_add[layer], 2)
                    with dve.Fori(0, NE) as e:
                        for f in range(FT):
                            dve.wait_ge(dense_sig[layer], e * FT + (f + 1))
                            dve.tensor_tensor(ovs, ovs, psum[f % 2][:, 0:S], ALU.mult).then_inc(dense_mul[layer], 1)
                            dve.wait_ge(dense_mul[layer], e * FT + (f + 1))
                            dve.tensor_tensor(ovh[:, f, :], ovs, psum[f % 2][:, S:2 * S], ALU.mult)\
                                .then_inc(dense_h[layer], 1)
                        for n in range(TT * NH):
                            t, half = n // NH, n % NH
                            dve.wait_ge(dense_y[layer], e * 4 + (n + 1))
                            hh = h[:, t, half * HALF:(half + 1) * HALF]
                            dve.scalar_tensor_tensor(out=hh, in0=psum[2 + n % 2][:, :],
                                                     scalar=extra[:, t, bass.ds(e, 1)], in1=hh, op0=ALU.mult,
                                                     op1=ALU.add).then_inc(dense_add[layer], 1)
                    dve.wait_ge(dense_add[layer], 4 * NE + 2)

            def experts(layer):
                norm_rows(1 + 2 * layer)
                norm_turned(1 + 2 * layer, R_FFN + layer * KT)
                route(layer)
                if layer == 0:
                    dve.memset(small[:, 131:132], 0.0).then_inc(gather_free, 1)
                g = layer * (NB + 1)
                places(0, g)
                take_gathered(layer, g, 0, 0)
                take_gathered(layer, g, 0, 1)
                take_gates(g, 0)
                with dve.Fori(0, NB // 2) as i:
                    for par in range(2):
                        packed(layer, i, par)
                dense(layer)
                dve.wait_ge(scattered, NB * (layer + 1))
                for t in range(TT):
                    for half in range(NH):
                        hh = h[:, t, half * HALF:(half + 1) * HALF]
                        ins = dve.tensor_tensor(hh, acc[t * NH + half][:, :], hh, ALU.add)
                ins.then_inc(h_ready, 1)

            experts(0)

            norm_rows(2)
            norm_turned(2, R_MIX + KT)
            for c in range(2):
                ins = dve.tensor_tensor_reduce(out=lam_rows[:, 2 * c, :], in0=lam_rows[:, 2 * c, :],
                                               in1=lam_rows[:, 2 * c + 1, :], scale=1.0, scalar=0.0, op0=ALU.mult,
                                               op1=ALU.add, accum_out=lsum[:, c:c + 1])
            ins.then_inc(lsum_ready, 1)
            dve.wait_ge(lsum_exp, 1)
            link(dve.tensor_tensor(nlam, lsum[:, 1:2], lsum[:, 0:1], ALU.subtract))
            link(dve.tensor_scalar(nlam, nlam, LAMBDA_INIT, None, ALU.subtract))
            link(dve.tensor_scalar(dng2, cols[:, R_DNG:R_DNG + DH], 1.0 - LAMBDA_INIT, None, ALU.mult))
            dve.wait_ge(dist_ready, 1)

            def unit_max(u):
                hd, t = u // TT, u % TT
                nk = (t + 1) * P
                slope = 2.0 ** (-8.0 * (hd + 1) / DH) / Q_SCALE
                for c in range(2):
                    name = f"ds{u}.{c}"
                    wait_full(dve, name)
                    ins = dve.scalar_tensor_tensor(out=sp_[:, u % 2, c, 0:nk], in0=dist[:, t, 0:nk], scalar=slope,
                                                   in1=bank_of(name)[:, 0:nk], op0=ALU.mult, op1=ALU.add)
                    free(ins, name)
                for c in range(2):
                    name = f"ds{u}.{c}"
                    dve.wait_ge(fill_free[TURN[name] % FILL_BANKS], TURN[name] // FILL_BANKS + 1)
                m = mx[:, 2 * (u % 2):2 * (u % 2) + 2]
                link(dve.tensor_reduce(m, sp_[:, u % 2, :, 0:nk], AX.X, ALU.max))
                dve.tensor_scalar(m, m, -Q_SCALE, None, ALU.mult).then_inc(soft_max, 1)

            def unit_diff(u):
                nk = (u % TT + 1) * P
                b = u % 2
                dve.wait_ge(soft_exp, u + 1)
                r = rsum[:, 2 * b:2 * b + 2]
                link(dve.reciprocal(r, sums[:, 2 * b:2 * b + 2]))
                link(dve.tensor_tensor(r[:, 1:2], r[:, 1:2], nlam, ALU.mult))
                if u >= 2:
                    dve.wait_ge(fill_full[TURN[f"dt{u - 2}"] % FILL_BANKS], TURN[f"dt{u - 2}"] // FILL_BANKS + 1)
                link(dve.tensor_scalar(dif[:, b, 0:nk], sp_[:, b, 0, 0:nk], r[:, 0:1], None, ALU.mult))
                dve.scalar_tensor_tensor(out=dif[:, b, 0:nk], in0=sp_[:, b, 1, 0:nk], scalar=r[:, 1:2],
                                         in1=dif[:, b, 0:nk], op0=ALU.mult, op1=ALU.add).then_inc(diff_ready, 1)

            unit_max(0)
            for u in range(TT * DH):
                if u + 1 < TT * DH:
                    unit_max(u + 1)
                unit_diff(u)
            dve.wait_ge(o_copied, TT * NH)
            on_v = on.rearrange("p t (h e) -> p (t h) e", e=P)
            sq2 = view(0, TT * DH, P)
            link(dve.tensor_tensor(sq2, on_v, on_v, ALU.mult))
            link(dve.tensor_reduce(oss, sq2, AX.X, ALU.add))
            inverse_root(oss, oss, P)
            dve.tensor_tensor(on_v, on_v, oss.unsqueeze(2).broadcast_to([P, TT * DH, P]), ALU.mult)\
                .then_inc(on_ready, 1)
            for i in range(4):
                name = f"dy{i}"
                wait_full(dve, name)
                free(dve.tensor_tensor(yT[:, 2 * i:2 * i + 2, :],
                                       bank_of(name)[:, :].rearrange("p (a s) -> p a s", a=2),
                                       dng2[:, 2 * i:2 * i + 2].unsqueeze(2).broadcast_to([P, 2, S]), ALU.mult), name)
            residual(1)
            experts(1)

            dve.wait_ge(squares, TT * 5)
            inverse_root(rstd, ss, D)
            dve.wait_ge(fgain_loaded, 16)
            for t in range(TT):
                dve.scalar_tensor_tensor(out=xs[:, t, :], in0=h[:, t, :], scalar=rstd[:, t:t + 1], in1=fg,
                                         op0=ALU.mult, op1=ALU.mult).then_inc(fin_ready, 1)


INPUTS = ["x", "norm_mix_g", "norm_ffn_g", "ab_w_in", "ab_w_out", "lru_conv_w", "lru_conv_b", "lru_w_r", "lru_b_r",
          "lru_w_i", "lru_b_i", "lru_lambda", "mlstm_b_i", "mlstm_b_f", "mlstm_norm_g", "diff_w_qkv", "diff_w_o",
          "diff_lambda_q1", "diff_lambda_k1", "diff_lambda_q2", "diff_lambda_k2", "diff_norm_g", "moe_w_group",
          "moe_b_group", "moe_w_expert", "moe_b_expert", "moe_w_up", "moe_w_down", "final_norm_g"]


def kernel(**inputs):
    import numpy as np
    import concourse.bacc as bacc
    from concourse.bass_utils import run_bass_kernel_spmd

    nc = bacc.Bacc("TRN2", target_bir_lowering=False, num_devices=1)
    arrays, args = {}, []
    for name in INPUTS:
        a = np.ascontiguousarray(inputs[name])
        arrays[f"in_{name}"] = a
        args.append(nc.dram_tensor(f"in_{name}", a.shape, mybir.dt.from_np(a.dtype), kind="ExternalInput").ap())
    out = nc.dram_tensor("out_0", (1, S, D), F32, kind="ExternalOutput").ap()
    build(nc, *args, out)
    r = run_bass_kernel_spmd(nc, [arrays], core_ids=[0])
    return r.results[0]["out_0"]
```

```python
import math
from contextlib import ExitStack

import concourse.bass as bass
from concourse import mybir

F32 = mybir.dt.float32
I32 = mybir.dt.int32
ALU = mybir.AluOpType
ACT = mybir.ActivationFunctionType
AX = mybir.AxisListType

P = 128
D = 1024
KT = D // P
S = 256
TT = S // P
EPS = 1e-6
HALF = 512
NH = D // HALF

W = 512
WT = W // P
TAPS = 4
LRU_C = 8.0
MH = 4
K_SCALE = float(P) ** -0.5
CHUNK = 64

DH = 8
DQK = 64
Q_SCALE = float(DQK) ** -0.5
LAMBDA_INIT = 0.8 - 0.6 * math.exp(-0.3 * 1)

LAYERS = 2
NG = 4
EPG = 8
NE = NG * EPG
FF = 512
FT = FF // P
CAP = 32
EB = P // CAP
NB = NE // EB
GH = KT // 2

SLOTS = 8
SLOT = 4096
MIX_STEPS = 8
MOE_STEPS = KT + FT
LAYER_STEPS = MIX_STEPS + NB * MOE_STEPS
FILL_BANKS = 4

R_MIX, R_FFN, R_CW, R_CB, R_BR, R_BI, R_LAM, R_MNG, R_DNG = 0, 16, 32, 48, 52, 56, 60, 64, 68
NR = 76

UNITS = TT * DH
ATTEND = ("S0 S1 P0 S2 V0 P1 S3 V1 P2 S4 V2 S5 V3 P3 S6 V4 P4 S7 V5 P5 S8 V6 S9 V7 S10 V8 S11 V9 TA S12 V10 OA "
          "S13 V11 S14 V12 S15 V13 V14 V15").split()
PIECES = ["dq2", "dq3", "dk2", "dk3", "dv2", "dv3"]


def attend_fills():
    for x in ATTEND:
        if x == "TA":
            yield from ("dy0", "dy1")
        elif x[0] == "S":
            yield from (f"ds{x[1:]}.0", f"ds{x[1:]}.1")
        elif x[0] == "V":
            yield f"dt{x[1:]}"
        elif x[0] == "P":
            yield PIECES[int(x[1:])]


FILLS = (
    ["columns"] + [f"norm0.{i}" for i in range(4)] + ["gates", "xa0", "xa1", "q0", "q1"]
    + [f"lru{j}" for j in range(WT)] + ["k0", "k1", "v0", "v1", "cols_am", "mmax0", "sc0", "ga0", "mmax1", "sc1", "ga1",
                                        "mmax2", "sc2", "o0", "mmax3", "sc3", "o1"]
    + [f"mix0.{i}" for i in range(4)] + ["norm1.0", "norm1.1", "router0", "norm1.2", "norm1.3", "rank0"]
    + [f"norm2.{i}" for i in range(4)] + [f"{x}{i}" for x in ("dq", "dk", "dv") for i in range(2)]
    + list(attend_fills()) + ["dy2", "dy3", "mix1.2", "mix1.3"]
    + ["norm3.0", "norm3.1", "router1", "norm3.2", "norm3.3", "rank1"]
)
TURN = {name: n for n, name in enumerate(FILLS)}


def build(nc, x, param_rows, gate_bias, block_weights, route_weights, route_bias, lambda_vectors, ab_w_in, ab_w_out,
          diff_w_qkv, diff_w_o, moe_w_up, moe_w_down, final_norm_g, out):
    with ExitStack() as ctx:
        def sb(name, shape, dt=F32):
            return ctx.enter_context(nc.sbuf_tensor(name, shape, dt))

        def sem(name):
            return ctx.enter_context(nc.semaphore(name))

        ring = sb("ring", [P, SLOTS, SLOT])
        h = sb("h", [P, TT, D])
        xs = sb("xs", [P, TT, D])
        xT = sb("xT", [P, KT, S])
        rows = sb("rows", [NR, P])
        cols = sb("cols", [P, NR])
        ident = sb("ident", [P, P])
        before = sb("before", [P, P])
        upto = sb("upto", [P, P])
        ones = sb("ones", [P, P])
        slot_no = sb("slot_no", [P, CAP])
        prio = sb("prio", [P, NE])
        zrow = sb("zrow", [1, P])
        w_gate = sb("w_gate", [P, KT, 2 * MH])
        w_route = sb("w_route", [P, LAYERS, KT, NG + NE])
        b_route = sb("b_route", [P, LAYERS, NG + NE])
        w_block = sb("w_block", [P, 2, WT, P])
        b_if = sb("b_if", [32 + MH, 1])
        lam_rows = sb("lam_rows", [P, 4, DQK])
        small = sb("small", [P, 136])
        flag = sb("flag", [1, LAYERS], I32)
        arena = sb("arena", [P, 10560])

        def view(at, *dims):
            n = 1
            for d in dims:
                n *= d
            v = arena[:, at:at + n]
            if len(dims) == 1:
                return v
            names = "abcd"[:len(dims)]
            return v.rearrange(f"p ({' '.join(names)}) -> p {' '.join(names)}",
                               **{c: d for c, d in zip(names, dims)})

        xpad = view(0, WT, S + TAPS - 1)
        root = view(0, WT * S)
        xc, r_g, i_g, t1, ga = (view(1040 + 1024 * n, WT, S) for n in range(5))
        flat = [view(1040 + 1024 * n, WT * S) for n in range(5)]
        xc_f, r_f, i_f, t1_f, ga_f = flat
        qT, kT, v_t, so = (view(6160 + 1024 * n, WT, S) for n in range(4))
        v_n = view(6160 + 2048, TT, W)
        yb = view(6160, TT, MH, P)
        sq = view(7184, TT, MH, P)
        lrow = view(10256, 256)
        wbuf = r_f[:, 0:2 * (S + P)].rearrange("p (b w) -> p b w", b=2)
        pbuf = i_f[:, 0:2 * (S + P)].rearrange("p (b w) -> p b w", b=2)
        yT = xs[:, :, :].rearrange("p a (b s) -> p (a b) s", s=S)
        gr = [sb(f"gr{n}", [MH, S]) for n in range(2)] + [yT[0:MH, WT + n, :] for n in range(4)]
        dq = view(0, DH, S)
        dk = view(2048, DH, S)
        dv = view(4096, TT, D)
        sp_ = view(6144, 2, 2, S)
        dif = view(7168, 2, S)
        dT = view(7680, 2, S)
        dist = view(8192, TT, S)
        on = view(8704, TT, HALF)
        xg = view(0, 2, KT, P)
        sel = view(2048, TT, EB, CAP)
        selg = view(2304, TT, EB, CAP)
        sgt = view(2560, TT, P)
        sig = view(3072, FF)
        hid = view(3584, FF)
        hT = view(4096, FT, P)
        y_s = view(4608, D)
        lg = view(5632, TT, NG + NE)
        mg = view(5704, TT, NG)
        el = view(5712, TT, NE)
        m1 = view(5776, TT, NE)
        m2 = view(5840, TT, NE)
        tmp = view(5904, TT, NE)
        both = view(5968, TT, NE)
        rankm = view(6032, TT, NE + EB)
        gates = view(6104, TT, NE + EB)
        extra = view(6176, TT, NE)
        rs = view(6240, 64)
        rs2 = view(6304, TT, NG)
        ovh = view(6400, FT, S)
        ovs = view(7424, S)
        fg = view(8192, D)

        rstd = small[:, 2:4]
        ss = sb("ss", [P, TT, NH])
        c4 = small[:, 4:8]
        l1a, l1b, l1c = small[:, 8:12], small[:, 12:16], small[:, 16:20]
        am = small[:, 20:36]
        enm = small[:, 36:44]
        den = small[:, 44:52]
        den2 = small[:, 52:60]
        hss = small[:, 60:68]
        lsum = small[:, 68:70]
        nlam = small[:, 70:71]
        mx = small[:, 72:76]
        sums = small[:, 76:80]
        rsum = small[:, 80:84]
        oss = small[:, 84:100]
        dng2 = small[:, 100:108]
        minus_half = small[:, 108:124]

        psum = [ctx.enter_context(nc.psum_tensor(f"bank{n}", [P, HALF], F32)) for n in range(8)]
        den_ps = psum[5]
        num_ps = psum[6:8]
        o_ps = psum[4:8]
        hy = psum[0:2]
        gather_ps, turn_ps = psum[2:4], psum[3]
        yb_ps = psum[4:6]
        acc = psum[4:8]

        x_loaded = [sem(f"x_loaded{t}") for t in range(TT)]
        rows_loaded = sem("rows_loaded")
        blocks_zeroed = sem("blocks_zeroed")
        params_loaded = sem("params_loaded")
        gates_loaded = sem("gates_loaded")
        blocks_loaded = sem("blocks_loaded")
        fgain_loaded = sem("fgain_loaded")
        slot_loaded = [sem(f"slot_loaded{n}") for n in range(SLOTS)]
        steps_done = sem("steps_done")
        ident_ready = sem("ident_ready")
        consts_ready = sem("consts_ready")
        pool_step = sem("pool_step")
        dist_ready = sem("dist_ready")
        qk_free = sem("qk_free")
        fill_full = [sem(f"fill_full{n}") for n in range(FILL_BANKS)]
        fill_free = [sem(f"fill_free{n}") for n in range(FILL_BANKS)]
        dve_step = sem("dve_step")
        act_step = sem("act_step")
        cols_ready = sem("cols_ready")
        squares = sem("squares")
        mean_ready = sem("mean_ready")
        root_ready = sem("root_ready")
        xs_ready = sem("xs_ready")
        h_ready = sem("h_ready")
        lam_abs = sem("lam_abs")
        lam_exp = sem("lam_exp")
        lsum_ready = sem("lsum_ready")
        lsum_exp = sem("lsum_exp")
        f_abs = sem("f_abs")
        f_exp = sem("f_exp")
        am_rows = sem("am_rows")
        am_cols = sem("am_cols")
        enm_ready = sem("enm_ready")
        conv_done = sem("conv_done")
        lru_sig = sem("lru_sig")
        lru_tanh = sem("lru_tanh")
        lru_floor = sem("lru_floor")
        lru_root = sem("lru_root")
        gelu_in = sem("gelu_in")
        gelu_tanh = sem("gelu_tanh")
        ya_ready = sem("ya_ready")
        w_arg = sem("w_arg")
        w_exp = sem("w_exp")
        p_ready = sem("p_ready")
        num_done = sem("num_done")
        yb_ready = sem("yb_ready")
        yT_ready = sem("yT_ready")
        soft_max = sem("soft_max")
        soft_exp = sem("soft_exp")
        diff_ready = sem("diff_ready")
        pv_done = sem("pv_done")
        on_squares = sem("on_squares")
        early_out = sem("early_out")
        on_ready = sem("on_ready")
        yb_full = sem("yb_full")
        route_arg = sem("route_arg")
        route_exp = sem("route_exp")
        picked = sem("picked")
        flag_ready = sem("flag_ready")
        sel_ready = sem("sel_ready")
        gather_full = sem("gather_full")
        gather_free = sem("gather_free")
        selg_ready = sem("selg_ready")
        sgt_full = sem("sgt_full")
        sgt_ready = sem("sgt_ready")
        sig_done = sem("sig_done")
        hid_step = sem("hid_step")
        hid_done = sem("hid_done")
        hT_full = sem("hT_full")
        hT_ready = sem("hT_ready")
        y_act = sem("y_act")
        y_dve = sem("y_dve")
        scattered = sem("scattered")
        dense_load = [sem(f"dense_load{l}") for l in range(LAYERS)]
        dense_turned = [sem(f"dense_turned{l}") for l in range(LAYERS)]
        dense_x = [sem(f"dense_x{l}") for l in range(LAYERS)]
        dense_gu = [sem(f"dense_gu{l}") for l in range(LAYERS)]
        dense_sig = [sem(f"dense_sig{l}") for l in range(LAYERS)]
        dense_mul = [sem(f"dense_mul{l}") for l in range(LAYERS)]
        dense_h = [sem(f"dense_h{l}") for l in range(LAYERS)]
        dense_y = [sem(f"dense_y{l}") for l in range(LAYERS)]
        dense_add = [sem(f"dense_add{l}") for l in range(LAYERS)]
        fin_ready = sem("fin_ready")
        out_stored = sem("out_stored")

        N_PARAMS = 3
        GATE_LOADS = 3
        BLOCKS = 4

        def bank_of(name):
            return psum[TURN[name] % FILL_BANKS]

        def wait_full(eng, name):
            eng.wait_ge(fill_full[TURN[name] % FILL_BANKS], TURN[name] // FILL_BANKS + 1)

        def wait_free(eng, name):
            if TURN[name] >= FILL_BANKS:
                eng.wait_ge(fill_free[TURN[name] % FILL_BANKS], TURN[name] // FILL_BANKS)

        def full(ins, name):
            ins.then_inc(fill_full[TURN[name] % FILL_BANKS], 1)

        def free(ins, name):
            ins.then_inc(fill_free[TURN[name] % FILL_BANKS], 1)

        def slot(step):
            return ring[:, step % SLOTS, :]

        def slot_k(step):
            return slot(step).rearrange("p (k n) -> p k n", k=KT)

        def slot_e(step):
            return slot(step).rearrange("p (e n) -> p e n", e=EB)

        def wait_slot(eng, step):
            eng.wait_ge(slot_loaded[step % SLOTS], 16 * (step // SLOTS + 1))

        block = ctx.enter_context(nc.Block())

        @block.sync
        def _(sp):
            for t in range(TT):
                sp.dma_start(h[:, t, :], x[0, t * P:(t + 1) * P, :]).then_inc(x_loaded[t], 16)
                if t == 0:
                    sp.dma_start(rows[:, :], param_rows).then_inc(rows_loaded, 16)

            def mixer(layer, w_in, w_out, order):
                base = layer * LAYER_STEPS
                chunks = [w_in[:, HALF * n:HALF * (n + 1)] for n in order]
                chunks += [w_out[:, HALF * n:HALF * (n + 1)] for n in range(NH)]
                for n, src in enumerate(chunks):
                    step = base + n
                    if step >= SLOTS:
                        sp.wait_ge(steps_done, step - SLOTS + 1)
                    sp.dma_start(slot_k(step), src.rearrange("(k p) n -> p k n", p=P))\
                        .then_inc(slot_loaded[step % SLOTS], 16)

            def experts(layer):
                base = layer * LAYER_STEPS + MIX_STEPS
                with sp.Fori(0, NB // 2) as i:
                    for par in range(2):
                        e0 = i * (2 * EB) + par * EB
                        for n in range(MOE_STEPS):
                            j = par * MOE_STEPS + n
                            w = moe_w_up if n < KT else moe_w_down
                            k = n if n < KT else n - KT
                            sp.wait_ge(steps_done, i * (2 * MOE_STEPS) + (base + j - SLOTS + 1))
                            sp.dma_start(slot_e(j), w[layer, bass.ds(e0, EB), k * P:(k + 1) * P, :]
                                         .rearrange("e p n -> p e n")).then_inc(slot_loaded[j % SLOTS], 16)

            def dense_expert(layer, e):
                sp.dma_start(ring[:, 0:2, :].rearrange("p a (k n) -> p (a k) n", k=KT // 2),
                             moe_w_up[layer, e].rearrange("(k p) n -> p k n", p=P)).then_inc(dense_load[layer], 16)
                sp.dma_start(ring[:, 2, :].rearrange("p (k n) -> p k n", k=FT),
                             moe_w_down[layer, e].rearrange("(k p) n -> p k n", p=P)).then_inc(dense_load[layer], 16)

            def dense(layer):
                sp.wait_ge(flag_ready, layer + 1)
                over = sp.value_load(flag[0:1, layer:layer + 1], min_val=0, max_val=1)
                with sp.If(over != 0):
                    sp.wait_ge(steps_done, (layer + 1) * LAYER_STEPS)
                    dense_expert(layer, 0)
                    with sp.Fori(0, NE - 1) as e:
                        sp.wait_ge(dense_y[layer], e * 4 + 4)
                        dense_expert(layer, e + 1)
                    sp.wait_ge(dense_y[layer], 4 * NE)

            mixer(0, ab_w_in[0], ab_w_out[0], (0, 2, 3, 4, 1, 5))
            experts(0)
            dense(0)
            mixer(1, diff_w_qkv[0], diff_w_o[0], (0, 2, 4, 1, 3, 5))
            experts(1)
            dense(1)
            for t in range(TT):
                sp.wait_ge(fin_ready, t + 1)
                sp.dma_start(out[0, t * P:(t + 1) * P, :], xs[:, t, :]).then_inc(out_stored, 16)
            sp.wait_ge(out_stored, 16 * TT)

        @block.gpsimd
        def _(pool):
            steps = [0]

            def link(ins):
                steps[0] += 1
                ins.then_inc(pool_step, 1)
                pool.wait_ge(pool_step, steps[0])

            link(pool.memset(minus_half, -0.5))
            pool.memset(w_block[:, :, :, :], 0.0).then_inc(blocks_zeroed, 1)
            link(pool.memset(ident[:, :], 0.0))
            pool.affine_select(out=ident[:, :], in_=ident[:, :], compare_op=ALU.not_equal, fill=1.0, base=0,
                               pattern=[[-1, P]], channel_multiplier=1).then_inc(ident_ready, 1)
            link(pool.memset(ones[:, :], 1.0))
            pool.affine_select(out=before[:, :], in_=ones[:, :], compare_op=ALU.is_gt, fill=0.0, base=0,
                               pattern=[[1, P]], channel_multiplier=-1)
            pool.affine_select(out=upto[:, :], in_=ones[:, :], compare_op=ALU.is_ge, fill=0.0, base=0,
                               pattern=[[1, P]], channel_multiplier=-1)
            pool.iota(slot_no[:, :], pattern=[[1, CAP]], base=0, channel_multiplier=0,
                      allow_small_or_imprecise_dtypes=True)
            pool.iota(prio[:, :], pattern=[[-1, NE]], base=NE, channel_multiplier=0,
                      allow_small_or_imprecise_dtypes=True)
            pool.memset(zrow[:, :], 0.0).then_inc(consts_ready, 1)
            n_roots = [0]

            def inverse_root(v):
                n_roots[0] += 1
                pool.wait_ge(mean_ready, n_roots[0])
                pool.tensor_tensor(v, v, minus_half[:, 0:v.shape[1]], ALU.pow).then_inc(root_ready, 1)

            inverse_root(rstd)
            inverse_root(hss)
            inverse_root(rstd)
            inverse_root(rstd)
            pool.wait_ge(h_ready, 8)
            for t in range(TT):
                for n, sign in enumerate((1, -1)):
                    part = sp_[:, n, t, :]
                    link(pool.iota(part, pattern=[[sign, S]], base=-sign * t * P, channel_multiplier=-sign,
                                   allow_small_or_imprecise_dtypes=True))
                    link(pool.affine_select(out=part, in_=part, compare_op=ALU.is_gt, fill=0.0, base=sign * t * P,
                                            pattern=[[-sign, S]], channel_multiplier=sign))
                link(pool.tensor_tensor(dist[:, t, :], sp_[:, 0, t, :], sp_[:, 1, t, :], ALU.add))
            for t in range(TT):
                for c in range(P // CHUNK):
                    seen = t * P + (c + 1) * CHUNK
                    if seen < S:
                        ins = pool.memset(dist[c * CHUNK:(c + 1) * CHUNK, t, seen:S], -1e30)
            ins.then_inc(dist_ready, 1)
            for half in range(2):
                inverse_root(oss[:, 8 * half:8 * half + 8])
            inverse_root(rstd)
            inverse_root(rstd)

        @block.tensor
        def _(pe):
            def turn_tiles(bank, rows_of, i):
                for c in range(2):
                    for t in range(TT):
                        k = 2 * i + c
                        ins = pe.transpose(bank[:, c * S + t * P:c * S + (t + 1) * P],
                                           rows_of[:, t, k * P:(k + 1) * P], ident[:, :])
                return ins

            def feature_major(n):
                pe.wait_ge(xs_ready, TT * (n + 1))
                for i in range(4):
                    wait_free(pe, f"norm{n}.{i}")
                    full(turn_tiles(bank_of(f"norm{n}.{i}"), xs, i), f"norm{n}.{i}")

            def stream_turned(layer, fills):
                for i in fills:
                    name = f"norm{1 + 2 * layer}.{i}"
                    pe.wait_ge(h_ready, 8 * layer + (2 if i < 2 else 4))
                    wait_free(pe, name)
                    full(turn_tiles(bank_of(name), h, i), name)

            def router(layer, fills):
                name = f"router{layer}"
                for i in fills:
                    turn = TURN[f"norm{1 + 2 * layer}.{i}"]
                    pe.wait_ge(fill_free[turn % FILL_BANKS], turn // FILL_BANKS + 1)
                    for k in (2 * i, 2 * i + 1):
                        for t in range(TT):
                            at = t * (NG + NE)
                            ins = pe.matmul(bank_of(name)[:, at:at + NG + NE], xT[:, k, t * P:(t + 1) * P],
                                            w_route[:, layer, k, :], start=(k == 0 and t == 0), stop=(k == KT - 1),
                                            skip_group_check=True)
                return ins

            def mix_end(layer, finish):
                finish(2)
                stream_turned(layer, (0, 1))
                finish(3)
                wait_free(pe, f"router{layer}")
                if layer == 0:
                    pe.wait_ge(params_loaded, 16 * N_PARAMS)
                router(layer, (0, 1))
                stream_turned(layer, (2, 3))
                full(router(layer, (2, 3)), f"router{layer}")

            def xT_complete(n):
                for i in range(4):
                    pe.wait_ge(fill_free[TURN[f"norm{n}.{i}"] % FILL_BANKS], TURN[f"norm{n}.{i}"] // FILL_BANKS + 1)

            def project_T(step, names, first=0):
                wait_slot(pe, step)
                w = slot_k(step)
                for i, name in enumerate(names, first):
                    wait_free(pe, name)
                    for c in range(2):
                        for k in range(KT):
                            n = (2 * i + c) * P
                            ins = pe.matmul(bank_of(name)[:, c * S:(c + 1) * S], w[:, k, n:n + P], xT[:, k, :],
                                            start=(k == 0), stop=(k == KT - 1))
                    full(ins, name)

            def project_N(step, names, lhs=xT, first=0):
                wait_slot(pe, step)
                w = slot_k(step)
                for t, name in enumerate(names, first):
                    wait_free(pe, name)
                    for k in range(KT):
                        ins = pe.matmul(bank_of(name)[:, :], lhs[:, k, t * P:(t + 1) * P], w[:, k, :],
                                        start=(k == 0), stop=(k == KT - 1))
                    full(ins, name)

            pe.wait_ge(ident_ready, 1)
            pe.wait_ge(rows_loaded, 16)
            full(pe.transpose(bank_of("columns")[:, 0:NR], rows[:, :], ident[0:NR, 0:NR]), "columns")
            feature_major(0)
            xT_complete(0)
            pe.wait_ge(gates_loaded, 16 * GATE_LOADS)
            wait_free(pe, "gates")
            for k in range(KT):
                for g in range(2):
                    ins = pe.matmul(bank_of("gates")[32 * g:32 * g + MH, 0:S], w_gate[:, k, g * MH:(g + 1) * MH],
                                    xT[:, k, :], start=(k == 0), stop=(k == KT - 1), skip_group_check=True)
            full(ins, "gates")
            project_T(0, ["xa0", "xa1"])
            project_T(1, ["q0", "q1"])
            pe.wait_ge(conv_done, 1)
            pe.wait_ge(blocks_loaded, 16 * BLOCKS)
            for j in range(WT):
                name = f"lru{j}"
                wait_free(pe, name)
                for g in range(2):
                    ins = pe.matmul(bank_of(name)[:, g * S:(g + 1) * S], w_block[:, g, j, :], xc[:, j, :],
                                    start=True, stop=True)
                full(ins, name)
            project_T(2, ["k0", "k1"])
            project_N(3, ["v0", "v1"])
            pe.wait_ge(am_rows, 1)
            wait_free(pe, "cols_am")
            for g, src in enumerate((gr[4], gr[5])):
                for t in range(TT):
                    at = (g * TT + t) * MH
                    ins = pe.transpose(bank_of("cols_am")[:, at:at + MH], src[:, t * P:(t + 1) * P],
                                       ident[0:MH, 0:MH])
            full(ins, "cols_am")

            def head_scores(hd):
                name = f"mmax{hd}"
                wait_free(pe, name)
                full(pe.matmul(bank_of(name)[:, 0:S], ident[0:MH, hd:hd + 1].broadcast_to([MH, P]), gr[3],
                               start=True, stop=True), name)
                name = f"sc{hd}"
                wait_free(pe, name)
                pe.matmul(bank_of(name)[:, 0:S], kT[:, hd, 0:P], qT[:, hd, :], start=True, stop=True)
                full(pe.matmul(bank_of(name)[:, S:S + P], kT[:, hd, P:S], qT[:, hd, P:S], start=True, stop=True),
                     name)

            def head_values(hd):
                pe.wait_ge(p_ready, hd + 1)
                pb = pbuf[:, hd % 2, :]
                vh = slice(hd * P, (hd + 1) * P)
                pe.matmul(num_ps[0][:, vh], pb[:, 0:P], v_n[:, 0, vh], start=True, stop=True)
                pe.matmul(num_ps[1][:, vh], pb[:, P:2 * P], v_n[:, 0, vh], start=True, stop=False)
                pe.matmul(num_ps[1][:, vh], pb[:, 2 * P:3 * P], v_n[:, 1, vh], start=False, stop=True)
                pe.matmul(den_ps[:, hd:hd + 1], pb[:, 0:P], ones[:, 0:1], start=True, stop=True)
                pe.matmul(den_ps[:, MH + hd:MH + hd + 1], pb[:, P:2 * P], ones[:, 0:1], start=True, stop=False)
                pe.matmul(den_ps[:, MH + hd:MH + hd + 1], pb[:, 2 * P:3 * P], ones[:, 0:1], start=False,
                          stop=True).then_inc(num_done, 1)

            for name in ("q0", "q1", "k0", "k1", "v0", "v1"):
                pe.wait_ge(fill_free[TURN[name] % FILL_BANKS], TURN[name] // FILL_BANKS + 1)
            pe.wait_ge(consts_ready, 1)
            head_scores(0)
            project_T(4, ["ga0"])
            head_scores(1)
            head_values(0)
            project_T(4, ["ga1"], 1)
            head_scores(2)
            head_values(1)
            project_T(5, ["o0"])
            head_scores(3)
            head_values(2)
            project_T(5, ["o1"], 1)
            head_values(3)

            def mix(layer, turn, ks):
                n, t = turn // TT, turn % TT
                for k in ks:
                    ins = pe.matmul(bank_of(f"mix{layer}.{turn}")[:, :], yT[:, k, t * P:(t + 1) * P],
                                    slot_k(layer * LAYER_STEPS + 6 + n)[:, k, :], start=(k == 0), stop=(k == KT - 1))
                return ins

            pe.wait_ge(ya_ready, 1)
            for turn in range(4):
                wait_slot(pe, 6 + turn // TT)
                wait_free(pe, f"mix0.{turn}")
                mix(0, turn, range(WT))
            pe.wait_ge(yb_ready, 1)
            for i in range(2):
                for c in range(2):
                    for t in range(TT):
                        ins = pe.transpose(yb_ps[i][:, c * S + t * P:c * S + (t + 1) * P],
                                           yb[:, t, 2 * i + c, :], ident[:, :])
                ins.then_inc(yb_full, 1)
            pe.wait_ge(yT_ready, 1)

            def finish(turn):
                full(mix(0, turn, range(WT, KT)), f"mix0.{turn}")

            finish(0)
            finish(1)
            mix_end(0, finish)

            def gather(g, buf, part):
                for k in range(GH):
                    kt = part * GH + k
                    for t in range(TT):
                        ins = pe.matmul(gather_ps[part][:, k * P:(k + 1) * P], xs[:, t, kt * P:(kt + 1) * P],
                                        sel[:, t, :, :].rearrange("p e c -> p (e c)"), start=(t == 0),
                                        stop=(t == TT - 1))
                ins.then_inc(gather_full, 1)

            def packed(layer, i, par):
                base = layer * LAYER_STEPS + MIX_STEPS
                b = i * 2 + (layer * NB + par)
                g = i * 2 + (layer * (NB + 1) + par)
                buf = par
                for n in range(KT):
                    j = par * MOE_STEPS + n
                    if n % GH == 0:
                        pe.wait_ge(gather_free, g * 2 + (n // GH + 1))
                    pe.wait_ge(slot_loaded[j % SLOTS], i * (16 * 3) + 16 * ((base + j) // SLOTS + 1))
                    for half in range(NH):
                        for e in range(EB):
                            ins = pe.matmul(hy[half][e * CAP:(e + 1) * CAP, :], xg[:, buf, n, e * CAP:(e + 1) * CAP],
                                            slot_e(j)[:, e, half * HALF:(half + 1) * HALF],
                                            start=(n == 0), stop=(n == KT - 1), skip_group_check=True)
                    ins.then_inc(steps_done, 1)
                    if n == 1:
                        pe.wait_ge(selg_ready, b + 1)
                        for t in range(TT):
                            ins = pe.transpose(gather_ps[0][:, t * P:(t + 1) * P],
                                               selg[:, t, :, :].rearrange("p e c -> p (e c)"), ident[:, :])
                        ins.then_inc(sgt_full, 1)
                    if n == GH - 1:
                        pe.wait_ge(sel_ready, g + 2)
                        pe.wait_ge(sgt_ready, b + 1)
                        gather(g + 1, 1 - buf, 0)
                gather(g + 1, 1 - buf, 1)
                pe.wait_ge(hid_done, b + 1)
                pe.wait_ge(gather_free, g * 2 + 4)
                for f in range(FT):
                    ins = pe.transpose(turn_ps[:, f * P:(f + 1) * P], hid[:, f * P:(f + 1) * P], ident[:, :])
                ins.then_inc(hT_full, 1)
                pe.wait_ge(hT_ready, b + 1)
                for n in range(FT):
                    j = par * MOE_STEPS + KT + n
                    pe.wait_ge(slot_loaded[j % SLOTS], i * (16 * 3) + 16 * ((base + j) // SLOTS + 1))
                    for half in range(NH):
                        for e in range(EB):
                            ins = pe.matmul(hy[half][e * CAP:(e + 1) * CAP, :], hT[:, n, e * CAP:(e + 1) * CAP],
                                            slot_e(j)[:, e, half * HALF:(half + 1) * HALF],
                                            start=(n == 0), stop=(n == FT - 1), skip_group_check=True)
                    ins.then_inc(steps_done, 1)
                pe.wait_ge(y_act, b + 1)
                pe.wait_ge(y_dve, b + 1)
                for t in range(TT):
                    for half in range(NH):
                        ins = pe.matmul(acc[t * NH + half][:, :], sgt[:, t, :], y_s[:, half * HALF:(half + 1) * HALF],
                                        start=False, stop=False, skip_group_check=True)
                ins.then_inc(scattered, 1)

            def experts(layer):
                pe.wait_ge(squares, 4 * (2 * layer + 2))
                for a in acc:
                    pe.matmul(a[:, :], zrow[:, :], h[0:1, 0, 0:HALF], start=True, stop=False, skip_group_check=True)
                name = f"rank{layer}"
                wait_free(pe, name)
                pe.wait_ge(picked, layer + 1)
                bank = bank_of(name)
                pe.matmul(bank[:, 0:NE], before[:, :], both[:, 0, :], start=True, stop=True)
                pe.matmul(bank[:, NE:2 * NE], ones[:, :], both[:, 0, :], start=True, stop=False)
                pe.matmul(bank[:, NE:2 * NE], before[:, :], both[:, 1, :], start=False, stop=True)
                pe.matmul(bank[:, 2 * NE:3 * NE], ones[:, :], both[:, 0, :], start=True, stop=False)
                full(pe.matmul(bank[:, 2 * NE:3 * NE], ones[:, :], both[:, 1, :], start=False, stop=True), name)
                for b in range(FILL_BANKS):
                    last = max(t for t in range(TURN[name] + 1) if t % FILL_BANKS == b)
                    pe.wait_ge(fill_free[b], last // FILL_BANKS + 1)
                g = layer * (NB + 1)
                pe.wait_ge(xs_ready, TT * (2 * layer + 2))
                pe.wait_ge(sel_ready, g + 1)
                for part in range(2):
                    gather(g, 0, part)
                with pe.Fori(0, NB // 2) as i:
                    for par in range(2):
                        packed(layer, i, par)

            def dense(layer):
                pe.wait_ge(flag_ready, layer + 1)
                over = pe.value_load(flag[0:1, layer:layer + 1], min_val=0, max_val=1)
                with pe.If(over != 0):
                    pe.wait_ge(dense_h[layer], 2)
                    for i in range(4):
                        turn_tiles(psum[i], xs, i).then_inc(dense_turned[layer], 1)
                    pe.wait_ge(dense_x[layer], 4)
                    up = ring[:, 0:2, :].rearrange("p a (k n) -> p (a k) n", k=KT // 2)
                    down = ring[:, 2, :].rearrange("p (k n) -> p k n", k=FT)
                    with pe.Fori(0, NE) as e:
                        pe.wait_ge(dense_load[layer], e * 32 + 32)
                        for f in range(FT):
                            pe.wait_ge(dense_h[layer], e * FT + (f + 1))
                            for g in range(2):
                                for k in range(KT):
                                    ins = pe.matmul(psum[f % 2][:, g * S:(g + 1) * S],
                                                    up[:, k, g * FF + f * P:g * FF + (f + 1) * P], xT[:, k, :],
                                                    start=(k == 0), stop=(k == KT - 1))
                            ins.then_inc(dense_gu[layer], 1)
                        pe.wait_ge(dense_h[layer], e * FT + (FT + 2))
                        for n in range(TT * NH):
                            pe.wait_ge(dense_add[layer], e * 4 + (n + 1))
                            for f in range(FT):
                                ins = pe.matmul(psum[2 + n % 2][:, :], ovh[:, f, (n // NH) * P:(n // NH + 1) * P],
                                                down[:, f, (n % NH) * HALF:(n % NH + 1) * HALF],
                                                start=(f == 0), stop=(f == FT - 1))
                            ins.then_inc(dense_y[layer], 1)

            experts(0)
            dense(0)

            feature_major(2)
            xT_complete(2)
            s1 = LAYER_STEPS
            project_T(s1, ["dq0", "dq1"])
            project_T(s1 + 1, ["dk0", "dk1"])
            project_N(s1 + 2, ["dv0", "dv1"])

            def piece(i):
                project = (project_T, project_T, project_N)[i // 2]
                project(s1 + 3 + i // 2, [PIECES[i]], first=i % 2)

            def unit_scores(u):
                hd, t = u // TT, u % TT
                nk = (t + 1) * P
                for c in range(2):
                    name = f"ds{u}.{c}"
                    wait_free(pe, name)
                    full(pe.matmul(bank_of(name)[:, 0:nk], dq[c * DQK:(c + 1) * DQK, hd, t * P:(t + 1) * P],
                                   dk[c * DQK:(c + 1) * DQK, hd, 0:nk], start=True, stop=True), name)

            def unit_values(u):
                hd, t = u // TT, u % TT
                name = f"dt{u}"
                wait_free(pe, name)
                pe.wait_ge(diff_ready, u + 1)
                for kt in range(t + 1):
                    ins = pe.transpose(bank_of(name)[:, kt * P:(kt + 1) * P], dif[:, u % 2, kt * P:(kt + 1) * P],
                                       ident[:, :])
                full(ins, name)
                pe.wait_ge(fill_free[TURN[name] % FILL_BANKS], TURN[name] // FILL_BANKS + 1)
                at = (hd % 4) * P
                for kt in range(t + 1):
                    ins = pe.matmul(o_ps[(hd // 4) * TT + t][:, at:at + P], dT[:, u % 2, kt * P:(kt + 1) * P],
                                    dv[:, kt, hd * P:(hd + 1) * P], start=(kt == 0), stop=(kt == t))
                ins.then_inc(pv_done, 1)

            def copied(names):
                for name in names:
                    pe.wait_ge(fill_free[TURN[name] % FILL_BANKS], TURN[name] // FILL_BANKS + 1)

            def turn_heads(half):
                pe.wait_ge(on_ready, half + 1)
                for i in range(2):
                    name = f"dy{2 * half + i}"
                    wait_free(pe, name)
                    for c in range(2):
                        for t in range(TT):
                            k = 2 * i + c
                            ins = pe.transpose(bank_of(name)[:, c * S + t * P:c * S + (t + 1) * P],
                                               on[:, t, k * P:(k + 1) * P], ident[:, :])
                    full(ins, name)

            def open_out(ks):
                for t in range(TT):
                    for k in ks:
                        ins = pe.matmul(o_ps[t][:, :], yT[:, k, t * P:(t + 1) * P], slot_k(s1 + 6)[:, k, :],
                                        start=(k == 0), stop=(k == KT - 1))
                return ins

            copied(["dq0", "dq1", "dk0", "dk1", "dv0", "dv1"])
            for x in ATTEND:
                if x == "TA":
                    turn_heads(0)
                elif x == "OA":
                    copied(["dy0", "dy1"])
                    wait_slot(pe, s1 + 6)
                    open_out(range(KT // 2))
                elif x[0] == "P":
                    piece(int(x[1:]))
                elif x[0] == "S":
                    if x == "S8":
                        copied(["dq2", "dq3", "dk2", "dk3"])
                    unit_scores(int(x[1:]))
                else:
                    if x == "V8":
                        copied(["dv2", "dv3"])
                    unit_values(int(x[1:]))
            turn_heads(1)
            copied(["dy2", "dy3"])
            open_out(range(KT // 2, KT)).then_inc(early_out, 1)
            wait_slot(pe, s1 + 7)

            def whole(turn):
                wait_free(pe, f"mix1.{turn}")
                full(mix(1, turn, range(KT)), f"mix1.{turn}")

            mix_end(1, whole)
            experts(1)
            dense(1)

        @block.scalar
        def _(act):
            n_params = [0]

            def load(dst, src):
                act.dma_start(dst, src).then_inc(params_loaded, 16)
                n_params[0] += 1

            act.dma_start(w_gate[:, :, :], ab_w_in[0][:, 6 * HALF:6 * HALF + 2 * MH].rearrange("(k p) n -> p k n", p=P))\
                .then_inc(gates_loaded, 16)
            for g in range(2):
                act.dma_start(b_if[32 * g:32 * g + MH, :], gate_bias[g]).then_inc(gates_loaded, 16)
            act.wait_ge(blocks_zeroed, 1)
            for half in range(2):
                lo = half * 64
                for g in range(2):
                    act.dma_start(w_block[lo:lo + 64, g, :, lo:lo + 64], block_weights[g, half])\
                        .then_inc(blocks_loaded, 16)
            load(w_route[:, :, :, :], route_weights)
            load(b_route[:, :, :], route_bias.partition_broadcast(P))
            load(lam_rows[:, :, :], lambda_vectors.partition_broadcast(P))
            assert n_params[0] == N_PARAMS

            def norm_squares(n, pieces=range(TT * NH)):
                for piece in pieces:
                    t, half = (piece % TT, piece // TT) if n in (1, 3) else (piece // NH, piece % NH)
                    if n == 0:
                        act.wait_ge(x_loaded[t], 16)
                    else:
                        act.wait_ge(h_ready, 4 * (n - 1) + piece + 1)
                    if n in (0, 1, 3) and piece >= 2:
                        act.wait_ge(squares, 4 * n + piece - 1)
                    bank = psum[6 + piece % 2] if n in (0, 1, 3) else acc[piece]
                    act.activation(bank[:, :], h[:, t, half * HALF:(half + 1) * HALF], ACT.Square,
                                   accum_out=ss[:, t, half:half + 1]).then_inc(squares, 1)
                    if n in (1, 3) and t == TT - 1:
                        act.sem_inc(steps_done, 1)

            def second_rows(root):
                act.wait_ge(root_ready, root)
                act.activation(xs[:, 1, :], h[:, 1, :], ACT.Copy, scale=rstd[:, 1:2]).then_inc(xs_ready, 1)

            def turned(n, i, at):
                name = f"norm{n}.{i}"
                wait_full(act, name)
                for c in range(2):
                    k = 2 * i + c
                    ins = act.activation(xT[:, k, :], bank_of(name)[:, c * S:(c + 1) * S], ACT.Copy,
                                         scale=cols[:, at + k:at + k + 1])
                free(ins, name)

            def copy_fill(dst, name):
                wait_full(act, name)
                free(act.activation(dst, bank_of(name)[:, :], ACT.Copy), name)

            def step_done():
                act.sem_inc(steps_done, 1)

            def pair(t, i):
                return t[:, 2 * i:2 * i + 2, :].rearrange("p a s -> p (a s)")

            norm_squares(0)
            act.wait_ge(cols_ready, 1)
            second_rows(1)
            turned(0, 1, R_MIX)
            turned(0, 3, R_MIX)
            act.wait_ge(lam_abs, 1)
            act.activation(l1b, l1a, ACT.Exp, scale=-1.0).then_inc(lam_exp, 1)
            act.wait_ge(f_abs, 1)
            act.activation(gr[2], gr[2], ACT.Exp, scale=-1.0).then_inc(f_exp, 1)
            for i in range(2):
                name = f"xa{i}"
                wait_full(act, name)
                free(act.activation(xpad[:, 2 * i:2 * i + 2, TAPS - 1:],
                                    bank_of(name)[:, :].rearrange("p (a s) -> p a s", a=2), ACT.Copy), name)
            step_done()
            for i in range(2):
                copy_fill(pair(qT, i), f"q{i}")
            step_done()
            for j in range(WT):
                name = f"lru{j}"
                wait_full(act, name)
                act.activation(r_g[:, j, :], bank_of(name)[:, 0:S], ACT.Sigmoid, bias=cols[:, R_BR + j:R_BR + j + 1])
                free(act.activation(i_g[:, j, :], bank_of(name)[:, S:2 * S], ACT.Sigmoid,
                                    bias=cols[:, R_BI + j:R_BI + j + 1]), name)
            for j in range(WT):
                name = f"lru{j}"
                act.wait_ge(fill_free[TURN[name] % FILL_BANKS], TURN[name] // FILL_BANKS + 1)
            for j in range(WT):
                ins = act.activation(r_g[:, j, :], r_g[:, j, :], ACT.Tanh, scale=c4[:, j:j + 1])
            ins.then_inc(lru_tanh, 1)
            act.wait_ge(lru_floor, 1)
            act.activation(root, root, ACT.Sqrt).then_inc(lru_root, 1)
            for i in range(2):
                copy_fill(pair(kT, i), f"k{i}")
            step_done()
            for t in range(TT):
                copy_fill(v_n[:, t, :], f"v{t}")
            step_done()
            act.wait_ge(am_cols, 1)
            act.activation(enm, am[:, 8:16], ACT.Exp).then_inc(enm_ready, 1)

            def head_exp(hd):
                act.wait_ge(w_arg, hd + 1)
                act.activation(wbuf[:, hd % 2, :], wbuf[:, hd % 2, :], ACT.Exp, scale=-1.0).then_inc(w_exp, 1)

            def gate_sigmoid(i):
                name = f"o{i}"
                wait_full(act, name)
                free(act.activation(pair(so, i), bank_of(name)[:, :], ACT.Sigmoid), name)

            head_exp(0)
            copy_fill(pair(ga, 0), "ga0")
            head_exp(1)
            copy_fill(pair(ga, 1), "ga1")
            step_done()
            head_exp(2)
            act.wait_ge(gelu_in, 1)
            gt = yT[:, 0:WT, :].rearrange("p a s -> p (a s)")
            act.activation(gt, gt, ACT.Tanh, scale=math.sqrt(2.0 / math.pi)).then_inc(gelu_tanh, 1)
            gate_sigmoid(0)
            head_exp(3)
            gate_sigmoid(1)
            step_done()

            def packed(layer, i, par):
                b = i * 2 + (layer * NB + par)
                steps = i * (2 * MOE_STEPS) + (layer * LAYER_STEPS + MIX_STEPS + par * MOE_STEPS)
                act.wait_ge(steps_done, steps + KT)
                act.activation(sig, hy[0][:, :], ACT.Sigmoid).then_inc(sig_done, 1)
                act.wait_ge(hT_full, b + 1)
                act.activation(hT[:, :, :].rearrange("p f c -> p (f c)"), turn_ps[:, :], ACT.Copy)\
                    .then_inc(hT_ready, 1)
                act.wait_ge(steps_done, steps + MOE_STEPS)
                act.activation(y_s[:, 0:HALF], hy[0][:, :], ACT.Copy).then_inc(y_act, 1)

            def experts(layer):
                n, at = 1 + 2 * layer, R_FFN + layer * KT
                norm_squares(n, range(3))
                turned(n, 1, at)
                norm_squares(n, range(3, 4))
                turned(n, 3, at)
                second_rows((3, 7)[layer])
                act.wait_ge(route_arg, layer + 1)
                act.activation(rs[:, 10:20], rs[:, 0:10], ACT.Exp).then_inc(route_exp, 1)
                with act.Fori(0, NB // 2) as i:
                    for par in range(2):
                        packed(layer, i, par)

            def dense(layer):
                act.wait_ge(flag_ready, layer + 1)
                over = act.value_load(flag[0:1, layer:layer + 1], min_val=0, max_val=1)
                with act.If(over != 0):
                    with act.Fori(0, NE) as e:
                        for f in range(FT):
                            act.wait_ge(dense_gu[layer], e * FT + (f + 1))
                            act.wait_ge(dense_h[layer], e * FT + (f + 2))
                            act.activation(ovs, psum[f % 2][:, 0:S], ACT.Sigmoid).then_inc(dense_sig[layer], 1)

            experts(0)
            dense(0)

            norm_squares(2)
            second_rows(4)
            turned(2, 1, R_MIX + KT)
            turned(2, 3, R_MIX + KT)
            act.wait_ge(lsum_ready, 1)
            act.activation(lsum, lsum, ACT.Exp).then_inc(lsum_exp, 1)

            def attend_copy(name):
                kind, i = name[:2], int(name[2:])
                if kind == "dv":
                    copy_fill(dv[:, i % TT, (i // TT) * HALF:(i // TT + 1) * HALF], name)
                else:
                    copy_fill(pair(dq if kind == "dq" else dk, i), name)
                if i % 2:
                    step_done()

            for name in ("dq0", "dq1", "dk0", "dk1", "dv0", "dv1"):
                attend_copy(name)

            def unit_exp(u):
                nk = (u % TT + 1) * P
                act.wait_ge(soft_max, u + 1)
                for c in range(2):
                    ins = act.activation(sp_[:, u % 2, c, 0:nk], sp_[:, u % 2, c, 0:nk], ACT.Exp, scale=Q_SCALE,
                                         bias=mx[:, 2 * (u % 2) + c:2 * (u % 2) + c + 1],
                                         accum_out=sums[:, 2 * (u % 2) + c:2 * (u % 2) + c + 1])
                ins.then_inc(soft_exp, 1)

            def unit_turn(u):
                nk = (u % TT + 1) * P
                name = f"dt{u}"
                wait_full(act, name)
                free(act.activation(dT[:, u % 2, 0:nk], bank_of(name)[:, 0:nk], ACT.Copy), name)

            def head_squares(half):
                act.wait_ge(pv_done, UNITS // 2 * (half + 1))
                for t in range(TT):
                    for hd in range(4):
                        c = 8 * half + 4 * t + hd
                        ins = act.activation(on[:, t, hd * P:(hd + 1) * P], o_ps[half * TT + t][:, hd * P:(hd + 1) * P], ACT.Square,
                                             accum_out=oss[:, c:c + 1])
                ins.then_inc(on_squares, 1)

            unit_exp(0)
            unit_exp(1)
            for x in ATTEND:
                if x[0] == "P":
                    attend_copy(PIECES[int(x[1:])])
                elif x[0] == "V":
                    u = int(x[1:])
                    unit_turn(u)
                    if u + 2 < UNITS:
                        unit_exp(u + 2)
                    if u == UNITS // 2 - 1:
                        head_squares(0)
            head_squares(1)
            experts(1)
            act.dma_start(fg, final_norm_g.partition_broadcast(P)).then_inc(fgain_loaded, 16)
            dense(1)
            norm_squares(4)

        @block.vector
        def _(dve):
            steps = [0]
            roots = [0]

            def link(ins):
                steps[0] += 1
                ins.then_inc(dve_step, 1)
                dve.wait_ge(dve_step, steps[0])

            def log1p(y, z, q):
                link(dve.tensor_scalar(z, y, 2.0, None, ALU.add))
                link(dve.reciprocal(z, z))
                link(dve.tensor_tensor(z, z, y, ALU.mult))
                link(dve.tensor_tensor(y, z, z, ALU.mult))
                link(dve.tensor_scalar(q, y, 1.0 / 15, None, ALU.mult))
                for odd in (13, 11, 9, 7, 5, 3):
                    link(dve.scalar_tensor_tensor(out=q, in0=q, scalar=1.0 / odd, in1=y, op0=ALU.add, op1=ALU.mult))
                link(dve.scalar_tensor_tensor(out=q, in0=q, scalar=1.0, in1=z, op0=ALU.add, op1=ALU.mult))
                link(dve.tensor_scalar(y, q, 2.0, None, ALU.mult))

            def mean(dst, src, n):
                dve.tensor_scalar(dst, src, 1.0 / n, EPS, ALU.mult, ALU.add).then_inc(mean_ready, 1)

            def wait_root():
                roots[0] += 1
                dve.wait_ge(root_ready, roots[0])

            def norm_mean(n):
                dve.wait_ge(squares, TT * NH * (n + 1))
                link(dve.tensor_reduce(rstd, ss[:, :, :], AX.X, ALU.add))
                mean(rstd, rstd, D)

            def first_rows():
                wait_root()
                dve.tensor_scalar(xs[:, 0, :], h[:, 0, :], rstd[:, 0:1], None, ALU.mult).then_inc(xs_ready, 1)

            def gained(bank, i, at):
                g = cols[:, at + 2 * i:at + 2 * i + 2].unsqueeze(2).broadcast_to([P, 2, S])
                return dve.tensor_tensor(xT[:, 2 * i:2 * i + 2, :], bank[:, :].rearrange("p (a s) -> p a s", a=2), g,
                                         ALU.mult)

            def turned(n, i, at):
                name = f"norm{n}.{i}"
                wait_full(dve, name)
                free(gained(bank_of(name), i, at), name)

            dve.memset(xpad[:, :, 0:TAPS - 1], 0.0)
            wait_full(dve, "columns")
            free(dve.tensor_copy(cols[:, :], bank_of("columns")[:, 0:NR]), "columns")
            dve.wait_ge(fill_free[TURN["columns"] % FILL_BANKS], 1)
            dve.sem_inc(cols_ready, 1)
            norm_mean(0)
            first_rows()
            lam_c = cols[:, R_LAM:R_LAM + WT]
            dve.scalar_tensor_tensor(out=l1a, in0=lam_c, scalar=-1.0, in1=lam_c, op0=ALU.mult, op1=ALU.max)\
                .then_inc(lam_abs, 1)
            turned(0, 0, R_MIX)
            turned(0, 2, R_MIX)
            ig, fgr, tabs, mmax, a_row, nm_row = gr
            name = "gates"
            wait_full(dve, name)
            dve.wait_ge(gates_loaded, 16 * GATE_LOADS)
            dve.tensor_scalar(ig[:, :], bank_of(name)[0:MH, 0:S], b_if[0:MH, :], None, ALU.add)
            free(dve.tensor_scalar(fgr[:, :], bank_of(name)[32:32 + MH, 0:S], b_if[32:32 + MH, :], None, ALU.add),
                 name)
            dve.wait_ge(fill_free[TURN[name] % FILL_BANKS], TURN[name] // FILL_BANKS + 1)
            dve.scalar_tensor_tensor(out=tabs, in0=fgr[:, :], scalar=-1.0, in1=fgr[:, :], op0=ALU.mult,
                                     op1=ALU.max).then_inc(f_abs, 1)
            dve.wait_ge(f_exp, 1)
            log1p(tabs, mmax, a_row)
            link(dve.tensor_scalar(fgr[:, :], fgr[:, :], -1.0, 0.0, ALU.mult, ALU.max))
            link(dve.tensor_tensor(fgr[:, :], fgr[:, :], tabs, ALU.add))
            link(dve.tensor_tensor_scan(tabs, fgr[:, :], fgr[:, :], 0.0, ALU.add, ALU.max))
            link(dve.tensor_tensor(a_row, ig[:, :], tabs, ALU.add))
            link(dve.tensor_tensor_scan(mmax, a_row, a_row, 0.0, ALU.max, ALU.max))
            dve.tensor_tensor(nm_row, tabs, mmax, ALU.subtract).then_inc(am_rows, 1)

            dve.wait_ge(lam_exp, 1)
            log1p(l1b, l1a, l1c)
            link(dve.tensor_scalar(l1a, lam_c, -1.0, 0.0, ALU.mult, ALU.max))
            link(dve.tensor_tensor(l1a, l1a, l1b, ALU.add))
            link(dve.tensor_scalar(c4, l1a, LRU_C / 2, None, ALU.mult))
            for i in range(2):
                name = f"xa{i}"
                dve.wait_ge(fill_free[TURN[name] % FILL_BANKS], TURN[name] // FILL_BANKS + 1)
            for w in range(TAPS - 1, -1, -1):
                for j in range(WT):
                    cw = cols[:, R_CW + w * WT + j:R_CW + w * WT + j + 1]
                    src = xpad[:, j, w:w + S]
                    if w == TAPS - 1:
                        ins = dve.tensor_scalar(xc[:, j, :], src, cw, cols[:, R_CB + j:R_CB + j + 1], ALU.mult, ALU.add)
                    else:
                        ins = dve.scalar_tensor_tensor(out=xc[:, j, :], in0=src, scalar=cw, in1=xc[:, j, :],
                                                       op0=ALU.mult, op1=ALU.add)
                if w:
                    link(ins)
            ins.then_inc(conv_done, 1)
            dve.wait_ge(conv_done, 1)
            dve.wait_ge(lru_tanh, 1)
            dve.tensor_scalar(root, r_f, 1e-34, None, ALU.max).then_inc(lru_floor, 1)
            link(dve.tensor_scalar(t1_f, r_f, 1.0, None, ALU.add))
            link(dve.reciprocal(t1_f, t1_f))
            link(dve.tensor_tensor(i_f, i_f, xc_f, ALU.mult))
            dve.wait_ge(lru_root, 1)
            link(dve.scalar_tensor_tensor(out=root, in0=root, scalar=2.0, in1=t1_f, op0=ALU.mult, op1=ALU.mult))
            link(dve.tensor_tensor(i_f, i_f, root, ALU.mult))
            link(dve.tensor_scalar(r_f, r_f, -1.0, 1.0, ALU.mult, ALU.add))
            link(dve.tensor_tensor(r_f, r_f, t1_f, ALU.mult))
            for j in range(WT):
                ins = dve.tensor_tensor_scan(xc[:, j, :], r_g[:, j, :], i_g[:, j, :], 0.0, ALU.mult, ALU.add)
            link(ins)

            gt = yT[:, 0:WT, :].rearrange("p a s -> p (a s)")

            def gelu_argument():
                for i in range(2):
                    name = f"ga{i}"
                    dve.wait_ge(fill_free[TURN[name] % FILL_BANKS], TURN[name] // FILL_BANKS + 1)
                link(dve.tensor_tensor(gt, ga_f, ga_f, ALU.mult))
                link(dve.tensor_scalar(gt, gt, 0.044715, 1.0, ALU.mult, ALU.add))
                dve.tensor_tensor(gt, gt, ga_f, ALU.mult).then_inc(gelu_in, 1)

            def gelu_product():
                dve.wait_ge(gelu_tanh, 1)
                link(dve.scalar_tensor_tensor(out=ga_f, in0=gt, scalar=1.0, in1=ga_f, op0=ALU.add, op1=ALU.mult))
                dve.scalar_tensor_tensor(out=gt, in0=ga_f, scalar=0.5, in1=xc_f, op0=ALU.mult, op1=ALU.mult)\
                    .then_inc(ya_ready, 1)

            name = "cols_am"
            wait_full(dve, name)
            free(dve.tensor_copy(am, bank_of(name)[:, 0:16]), name)
            dve.wait_ge(fill_free[TURN[name] % FILL_BANKS], TURN[name] // FILL_BANKS + 1)

            def head_args(hd):
                name = f"mmax{hd}"
                wait_full(dve, name)
                bank = bank_of(name)
                if hd >= 2:
                    dve.wait_ge(p_ready, hd - 1)
                dve.tensor_scalar(wbuf[:, hd % 2, 0:S], bank[:, 0:S], am[:, hd:hd + 1], 0.0, ALU.subtract, ALU.max)
                free(dve.tensor_scalar(wbuf[:, hd % 2, S:S + P], bank[:, P:S], am[:, MH + hd:MH + hd + 1], 0.0,
                                       ALU.subtract, ALU.max), name)
                dve.wait_ge(fill_free[TURN[name] % FILL_BANKS], TURN[name] // FILL_BANKS + 1)
                dve.tensor_copy(lrow[:, 0:1], am[:, 0:1]).then_inc(w_arg, 1)

            def head_weights(hd):
                name = f"sc{hd}"
                dve.wait_ge(w_exp, hd + 1)
                w = wbuf[:, hd % 2, :]
                diag = w.rearrange("p (a c) -> p a c", a=3)[:, 0:3:2, :]
                link(dve.tensor_tensor(diag, diag, upto[:, :].unsqueeze(1).broadcast_to([P, 2, P]), ALU.mult))
                wait_full(dve, name)
                if hd >= 2:
                    dve.wait_ge(num_done, hd - 1)
                free(dve.scalar_tensor_tensor(out=pbuf[:, hd % 2, :], in0=bank_of(name)[:, 0:S + P], scalar=K_SCALE,
                                              in1=w, op0=ALU.mult, op1=ALU.mult), name)
                dve.wait_ge(fill_free[TURN[name] % FILL_BANKS], TURN[name] // FILL_BANKS + 1)
                dve.tensor_copy(lrow[:, 1:2], am[:, 0:1]).then_inc(p_ready, 1)

            dve.tensor_copy(lrow[:, 2:3], am[:, 0:1]).then_inc(am_cols, 1)
            dve.wait_ge(consts_ready, 1)
            head_args(0)
            head_weights(0)
            head_args(1)
            head_weights(1)
            head_args(2)
            gelu_argument()
            head_weights(2)
            head_args(3)
            gelu_product()
            head_weights(3)
            dve.wait_ge(num_done, MH)
            link(dve.tensor_copy(den, den_ps[:, 0:8]))
            link(dve.scalar_tensor_tensor(out=den2, in0=den, scalar=-1.0, in1=den, op0=ALU.mult, op1=ALU.max))
            dve.wait_ge(enm_ready, 1)
            link(dve.tensor_tensor(den2, den2, enm, ALU.max))
            link(dve.reciprocal(den, den2))
            for t in range(TT):
                ins = dve.tensor_tensor(yb[:, t, :, :], num_ps[t][:, :].rearrange("p (h e) -> p h e", h=MH),
                                        den[:, t * MH:(t + 1) * MH].unsqueeze(2).broadcast_to([P, MH, P]), ALU.mult)
            link(ins)
            yb_v = yb.rearrange("p t h e -> p (t h) e")
            sq_v = sq.rearrange("p t h e -> p (t h) e")
            link(dve.tensor_tensor(sq_v, yb_v, yb_v, ALU.mult))
            link(dve.tensor_reduce(hss, sq_v, AX.X, ALU.add))
            mean(hss, hss, P)
            wait_root()
            dve.tensor_tensor(yb_v, yb_v, hss.unsqueeze(2).broadcast_to([P, 8, P]), ALU.mult).then_inc(yb_ready, 1)
            for i in range(2):
                dve.wait_ge(yb_full, i + 1)
                for c in range(2):
                    hd = 2 * i + c
                    dve.wait_ge(fill_free[TURN[f"o{i}"] % FILL_BANKS], TURN[f"o{i}"] // FILL_BANKS + 1)
                    ins = dve.scalar_tensor_tensor(out=yT[:, WT + hd, :], in0=yb_ps[i][:, c * S:(c + 1) * S],
                                                   scalar=cols[:, R_MNG + hd:R_MNG + hd + 1], in1=so[:, hd, :],
                                                   op0=ALU.mult, op1=ALU.mult)
            ins.then_inc(yT_ready, 1)

            def residual(layer):
                for n in range(NH):
                    for t in range(TT):
                        early = layer == 1 and n == 0
                        name = f"mix{layer}.{2 * n + t}"
                        if early:
                            dve.wait_ge(early_out, 1)
                        else:
                            wait_full(dve, name)
                        bank = o_ps[t] if early else bank_of(name)
                        hh = h[:, t, n * HALF:(n + 1) * HALF]
                        dve.tensor_tensor(hh, bank[:, :], hh, ALU.add).then_inc(h_ready, 1)
                        if not early:
                            dve.wait_ge(h_ready, 8 * layer + 2 * n + t + 1)
                            dve.sem_inc(fill_free[TURN[name] % FILL_BANKS], 1)
                        if n == 1 and t == 0:
                            turned(1 + 2 * layer, 0, R_FFN + layer * KT)
                norm_mean(1 + 2 * layer)
                turned(1 + 2 * layer, 2, R_FFN + layer * KT)
                first_rows()

            residual(0)

            def bc(v, n):
                return v.broadcast_to([P, TT, n])

            def first_max(mask, values, best, n):
                link(dve.tensor_tensor(mask, values, bc(best, n), ALU.is_equal))
                link(dve.tensor_tensor(mask, mask, prio[:, 0:n].unsqueeze(1).broadcast_to([P, TT, n]), ALU.mult))
                link(dve.tensor_reduce(rs2[:, :, 2], mask, AX.X, ALU.max))
                link(dve.tensor_tensor(mask, mask, bc(rs2[:, :, 2:3], n), ALU.is_equal))

            def route(layer):
                name = f"router{layer}"
                wait_full(dve, name)
                if layer == 0:
                    dve.wait_ge(params_loaded, 16 * N_PARAMS)
                ex = rs[:, 0:10].rearrange("p (t n) -> p t n", t=TT)
                eo = rs[:, 10:20].rearrange("p (t n) -> p t n", t=TT)
                best, best2 = rs2[:, :, 0:1], rs2[:, :, 1:2]
                for t in range(TT):
                    at = t * (NG + NE)
                    ins = dve.scalar_tensor_tensor(out=lg[:, t, :], in0=bank_of(name)[:, at:at + NG + NE],
                                                   scalar=rstd[:, t:t + 1], in1=b_route[:, layer, :],
                                                   op0=ALU.mult, op1=ALU.add)
                free(ins, name)
                dve.wait_ge(fill_free[TURN[name] % FILL_BANKS], TURN[name] // FILL_BANKS + 1)
                gl = lg[:, :, 0:NG]
                link(dve.tensor_reduce(rs2[:, :, 0], gl, AX.X, ALU.max))
                link(dve.tensor_tensor(ex[:, :, 0:NG], gl, bc(best, NG), ALU.subtract))
                first_max(mg, gl, best, NG)
                mg_e = mg.unsqueeze(3).broadcast_to([P, TT, NG, EPG])
                el4 = el.rearrange("p t (g e) -> p t g e", g=NG)
                tmp4 = tmp.rearrange("p t (g e) -> p t g e", g=NG)
                link(dve.tensor_tensor(el4, lg[:, :, NG:].rearrange("p t (g e) -> p t g e", g=NG), mg_e, ALU.mult))
                link(dve.tensor_scalar(tmp4, mg_e, 1.0, 1e30, ALU.subtract, ALU.mult))
                link(dve.tensor_tensor(el, el, tmp, ALU.add))
                link(dve.tensor_reduce(rs2[:, :, 0], el, AX.X, ALU.max))
                first_max(m1, el, best, NE)
                link(dve.scalar_tensor_tensor(out=el, in0=m1, scalar=-3e30, in1=el, op0=ALU.mult, op1=ALU.add))
                link(dve.tensor_reduce(rs2[:, :, 1], el, AX.X, ALU.max))
                dve.tensor_tensor(ex[:, :, NG], rs2[:, :, 1], rs2[:, :, 0], ALU.subtract).then_inc(route_arg, 1)
                first_max(m2, el, best2, NE)
                dve.tensor_tensor(both, m1, m2, ALU.add).then_inc(picked, 1)
                link(dve.memset(rankm[:, :, NE:], -1.0))
                name = f"rank{layer}"
                wait_full(dve, name)
                rank = bank_of(name)[:, 0:TT * NE].rearrange("p (t n) -> p t n", t=TT)
                link(dve.scalar_tensor_tensor(out=el, in0=rank, scalar=1.0, in1=both, op0=ALU.add, op1=ALU.mult))
                link(dve.tensor_scalar(rankm[:, :, 0:NE], el, 1.0, None, ALU.subtract))
                places(0, layer * (NB + 1))
                link(dve.tensor_reduce(small[0:1, 134:135], bank_of(name)[0:1, 2 * NE:3 * NE], AX.X, ALU.max))
                free(dve.tensor_copy(small[0:1, 133:134], bank_of(name)[0:1, 0:1]), name)
                dve.wait_ge(route_exp, layer + 1)
                link(dve.tensor_reduce(rs2[:, :, 0], eo[:, :, 0:NG], AX.X, ALU.add))
                link(dve.tensor_scalar(rs2[:, :, 1], eo[:, :, NG], 1.0, None, ALU.add))
                link(dve.tensor_tensor(rs2[:, :, 0], rs2[:, :, 0], rs2[:, :, 1], ALU.mult))
                link(dve.reciprocal(rs2[:, :, 0], rs2[:, :, 0]))
                link(dve.tensor_tensor(rs2[:, :, 1], rs2[:, :, 0], eo[:, :, NG], ALU.mult))
                link(dve.tensor_tensor(m1, m1, bc(best, NE), ALU.mult))
                link(dve.tensor_tensor(m2, m2, bc(best2, NE), ALU.mult))
                link(dve.tensor_tensor(gates[:, :, 0:NE], m1, m2, ALU.add))
                link(dve.tensor_scalar(el, el, CAP + 0.5, None, ALU.is_gt))
                link(dve.tensor_tensor(extra, el, gates[:, :, 0:NE], ALU.mult))
                dve.tensor_scalar(flag[0:1, layer:layer + 1], small[0:1, 134:135], CAP + 0.5, None, ALU.is_gt)\
                    .then_inc(flag_ready, 1)

            def places(e0, g):
                dve.tensor_tensor(sel, slot_no[:, :].unsqueeze(1).unsqueeze(1).broadcast_to([P, TT, EB, CAP]),
                                  rankm[:, :, bass.ds(e0, EB)].unsqueeze(3).broadcast_to([P, TT, EB, CAP]),
                                  ALU.is_equal).then_inc(sel_ready, 1)

            def weigh(e0, g, b):
                dve.wait_ge(sel_ready, g + 1)
                dve.tensor_tensor(selg, sel, gates[:, :, bass.ds(e0, EB)].unsqueeze(3)
                                  .broadcast_to([P, TT, EB, CAP]), ALU.mult).then_inc(selg_ready, 1)
                dve.wait_ge(selg_ready, b + 1)

            def take_gathered(layer, g, buf, part):
                at = R_FFN + layer * KT + part * GH
                dve.wait_ge(gather_full, g * 2 + (part + 1))
                dve.tensor_tensor(xg[:, buf, part * GH:(part + 1) * GH, :],
                                  gather_ps[part][:, :].rearrange("p (k c) -> p k c", k=GH),
                                  cols[:, at:at + GH].unsqueeze(2).broadcast_to([P, GH, P]), ALU.mult)\
                    .then_inc(gather_free, 1)

            def packed(layer, i, par):
                b = i * 2 + (layer * NB + par)
                g = i * 2 + (layer * (NB + 1) + par)
                done = i * (2 * MOE_STEPS) + (layer * LAYER_STEPS + MIX_STEPS + par * MOE_STEPS)
                e0 = i * (2 * EB) + par * EB
                weigh(e0, g, b)
                places(e0 + EB, g + 1)
                dve.wait_ge(sgt_full, b + 1)
                dve.tensor_copy(sgt[:, :, :].rearrange("p t c -> p (t c)"), gather_ps[0][:, 0:TT * P])\
                    .then_inc(sgt_ready, 1)
                take_gathered(layer, g + 1, 1 - par, 0)
                take_gathered(layer, g + 1, 1 - par, 1)
                dve.wait_ge(steps_done, done + KT)
                dve.wait_ge(sig_done, b + 1)
                dve.tensor_tensor(sig, sig, hy[0][:, :], ALU.mult).then_inc(hid_step, 1)
                dve.wait_ge(hid_step, b + 1)
                dve.tensor_tensor(hid, sig, hy[1][:, :], ALU.mult).then_inc(hid_done, 1)
                dve.wait_ge(steps_done, done + MOE_STEPS)
                dve.tensor_copy(y_s[:, HALF:D], hy[1][:, :]).then_inc(y_dve, 1)

            def dense(layer):
                dve.wait_ge(flag_ready, layer + 1)
                over = dve.value_load(flag[0:1, layer:layer + 1], min_val=0, max_val=1)
                with dve.If(over != 0):
                    dve.memset(ovs, 0.0).then_inc(dense_h[layer], 2)
                    dve.memset(small[:, 132:133], 0.0).then_inc(dense_add[layer], 2)
                    for i in range(4):
                        dve.wait_ge(dense_turned[layer], i + 1)
                        gained(psum[i], i, R_FFN + layer * KT).then_inc(dense_x[layer], 1)
                    with dve.Fori(0, NE) as e:
                        for f in range(FT):
                            dve.wait_ge(dense_sig[layer], e * FT + (f + 1))
                            dve.tensor_tensor(ovs, ovs, psum[f % 2][:, 0:S], ALU.mult).then_inc(dense_mul[layer], 1)
                            dve.wait_ge(dense_mul[layer], e * FT + (f + 1))
                            dve.tensor_tensor(ovh[:, f, :], ovs, psum[f % 2][:, S:2 * S], ALU.mult)\
                                .then_inc(dense_h[layer], 1)
                        for n in range(TT * NH):
                            t, half = n // NH, n % NH
                            dve.wait_ge(dense_y[layer], e * 4 + (n + 1))
                            hh = h[:, t, half * HALF:(half + 1) * HALF]
                            dve.scalar_tensor_tensor(out=hh, in0=psum[2 + n % 2][:, :],
                                                     scalar=extra[:, t, bass.ds(e, 1)], in1=hh, op0=ALU.mult,
                                                     op1=ALU.add).then_inc(dense_add[layer], 1)
                    dve.wait_ge(dense_add[layer], 4 * NE + 2)

            def experts(layer):
                route(layer)
                g = layer * (NB + 1)
                take_gathered(layer, g, 0, 0)
                take_gathered(layer, g, 0, 1)
                with dve.Fori(0, NB // 2) as i:
                    for par in range(2):
                        packed(layer, i, par)
                dense(layer)
                dve.wait_ge(scattered, NB * (layer + 1))
                for t in range(TT):
                    for half in range(NH):
                        hh = h[:, t, half * HALF:(half + 1) * HALF]
                        dve.tensor_tensor(hh, acc[t * NH + half][:, :], hh, ALU.add).then_inc(h_ready, 1)

            experts(0)

            norm_mean(2)
            first_rows()
            turned(2, 0, R_MIX + KT)
            turned(2, 2, R_MIX + KT)
            for c in range(2):
                ins = dve.tensor_tensor_reduce(out=lam_rows[:, 2 * c, :], in0=lam_rows[:, 2 * c, :],
                                               in1=lam_rows[:, 2 * c + 1, :], scale=1.0, scalar=0.0, op0=ALU.mult,
                                               op1=ALU.add, accum_out=lsum[:, c:c + 1])
            ins.then_inc(lsum_ready, 1)
            dve.wait_ge(lsum_exp, 1)
            link(dve.tensor_tensor(nlam, lsum[:, 1:2], lsum[:, 0:1], ALU.subtract))
            link(dve.tensor_scalar(nlam, nlam, LAMBDA_INIT, None, ALU.subtract))
            link(dve.tensor_scalar(dng2, cols[:, R_DNG:R_DNG + DH], 1.0 - LAMBDA_INIT, None, ALU.mult))
            dve.wait_ge(dist_ready, 1)

            def unit_max(u):
                hd, t = u // TT, u % TT
                nk = (t + 1) * P
                slope = 2.0 ** (-8.0 * (hd + 1) / DH) / Q_SCALE
                if u >= 2:
                    dve.wait_ge(diff_ready, u - 1)
                for c in range(2):
                    name = f"ds{u}.{c}"
                    wait_full(dve, name)
                    ins = dve.scalar_tensor_tensor(out=sp_[:, u % 2, c, 0:nk], in0=dist[:, t, 0:nk], scalar=slope,
                                                   in1=bank_of(name)[:, 0:nk], op0=ALU.mult, op1=ALU.add)
                    free(ins, name)
                for c in range(2):
                    name = f"ds{u}.{c}"
                    dve.wait_ge(fill_free[TURN[name] % FILL_BANKS], TURN[name] // FILL_BANKS + 1)
                m = mx[:, 2 * (u % 2):2 * (u % 2) + 2]
                link(dve.tensor_reduce(m, sp_[:, u % 2, :, 0:nk], AX.X, ALU.max))
                dve.tensor_scalar(m, m, -Q_SCALE, None, ALU.mult).then_inc(soft_max, 1)

            def unit_diff(u):
                nk = (u % TT + 1) * P
                b = u % 2
                dve.wait_ge(soft_exp, u + 1)
                r = rsum[:, 2 * b:2 * b + 2]
                link(dve.reciprocal(r, sums[:, 2 * b:2 * b + 2]))
                link(dve.tensor_tensor(r[:, 1:2], r[:, 1:2], nlam, ALU.mult))
                if u >= 2:
                    dve.wait_ge(fill_full[TURN[f"dt{u - 2}"] % FILL_BANKS], TURN[f"dt{u - 2}"] // FILL_BANKS + 1)
                link(dve.tensor_scalar(dif[:, b, 0:nk], sp_[:, b, 0, 0:nk], r[:, 0:1], None, ALU.mult))
                dve.scalar_tensor_tensor(out=dif[:, b, 0:nk], in0=sp_[:, b, 1, 0:nk], scalar=r[:, 1:2],
                                         in1=dif[:, b, 0:nk], op0=ALU.mult, op1=ALU.add).then_inc(diff_ready, 1)

            def head_scale(half):
                wait_root()
                if half == 1:
                    for name in ("dy0", "dy1"):
                        wait_full(dve, name)
                for t in range(TT):
                    r = oss[:, 8 * half + 4 * t:8 * half + 4 * t + 4].unsqueeze(2).broadcast_to([P, 4, P])
                    ins = dve.tensor_tensor(on[:, t, :].rearrange("p (h e) -> p h e", h=4),
                                            o_ps[half * TT + t][:, :].rearrange("p (h e) -> p h e", h=4), r, ALU.mult)
                ins.then_inc(on_ready, 1)

            def head_turned(half):
                for i in range(2):
                    k = 4 * half + 2 * i
                    name = f"dy{2 * half + i}"
                    wait_full(dve, name)
                    free(dve.tensor_tensor(yT[:, k:k + 2, :], bank_of(name)[:, :].rearrange("p (a s) -> p a s", a=2),
                                           dng2[:, k:k + 2].unsqueeze(2).broadcast_to([P, 2, S]), ALU.mult), name)

            unit_max(0)
            unit_max(1)
            for u in range(UNITS):
                unit_diff(u)
                if u == UNITS // 2 + 2:
                    head_turned(0)
                if u + 2 < UNITS:
                    unit_max(u + 2)
                if u == UNITS // 2:
                    dve.wait_ge(on_squares, 1)
                    mean(oss[:, 0:8], oss[:, 0:8], P)
                if u == UNITS // 2 + 1:
                    head_scale(0)
            dve.wait_ge(on_squares, 2)
            mean(oss[:, 8:16], oss[:, 8:16], P)
            head_scale(1)
            head_turned(1)
            residual(1)
            experts(1)

            norm_mean(4)
            wait_root()
            dve.wait_ge(fgain_loaded, 16)
            for t in range(TT):
                dve.scalar_tensor_tensor(out=xs[:, t, :], in0=h[:, t, :], scalar=rstd[:, t:t + 1], in1=fg,
                                         op0=ALU.mult, op1=ALU.mult).then_inc(fin_ready, 1)


def laid_out(v):
    import numpy as np

    a = {name: np.ascontiguousarray(x) for name, x in v.items()}
    rows = ("norm_mix_g", "norm_ffn_g", "lru_conv_w", "lru_conv_b", "lru_b_r", "lru_b_i", "lru_lambda",
            "mlstm_norm_g", "diff_norm_g")
    blocks = [a[n][0].reshape(WT, 2, 64, 64).transpose(1, 2, 0, 3) for n in ("lru_w_r", "lru_w_i")]
    route = np.concatenate([a["moe_w_group"], a["moe_w_expert"]], axis=2)
    return {
        "x": a["x"],
        "param_rows": np.concatenate([a[n].reshape(-1, P) for n in rows]),
        "gate_bias": np.stack([a["mlstm_b_i"][0], a["mlstm_b_f"][0]])[:, :, None],
        "block_weights": np.stack(blocks),
        "route_weights": route.reshape(LAYERS, KT, P, NG + NE).transpose(2, 0, 1, 3),
        "route_bias": np.concatenate([a["moe_b_group"], a["moe_b_expert"]], axis=1),
        "lambda_vectors": np.concatenate([a[f"diff_lambda_{n}"] for n in ("q1", "k1", "q2", "k2")]),
        **{n: a[n] for n in ("ab_w_in", "ab_w_out", "diff_w_qkv", "diff_w_o", "moe_w_up", "moe_w_down",
                             "final_norm_g")},
    }


def kernel(**inputs):
    import numpy as np
    import concourse.bacc as bacc
    from concourse.bass_utils import run_bass_kernel_spmd

    nc = bacc.Bacc("TRN2", target_bir_lowering=False, num_devices=1)
    arrays, args = {}, []
    for name, a in laid_out(inputs).items():
        a = np.ascontiguousarray(a)
        arrays[f"in_{name}"] = a
        args.append(nc.dram_tensor(f"in_{name}", a.shape, mybir.dt.from_np(a.dtype), kind="ExternalInput").ap())
    out = nc.dram_tensor("out_0", (1, S, D), F32, kind="ExternalOutput").ap()
    build(nc, *args, out)
    r = run_bass_kernel_spmd(nc, [arrays], core_ids=[0])
    return r.results[0]["out_0"]
```

```python
import math
from contextlib import ExitStack

import concourse.bass as bass
from concourse import mybir

F32 = mybir.dt.float32
I32 = mybir.dt.int32
ALU = mybir.AluOpType
ACT = mybir.ActivationFunctionType
AX = mybir.AxisListType

P = 128
D = 1024
KT = D // P
S = 256
TT = S // P
EPS = 1e-6
HALF = 512
NH = D // HALF

W = 512
WT = W // P
TAPS = 4
LRU_C = 8.0
MH = 4
K_SCALE = float(P) ** -0.5
CHUNK = 64

DH = 8
DQK = 64
Q_SCALE = float(DQK) ** -0.5
LAMBDA_INIT = 0.8 - 0.6 * math.exp(-0.3 * 1)

LAYERS = 2
NG = 4
EPG = 8
NE = NG * EPG
FF = 512
FT = FF // P
CAP = 32
EB = P // CAP
NB = NE // EB
GH = KT // 2

SLOTS = 8
SLOT = 4096
MIX_STEPS = 8
MOE_STEPS = KT + FT
LAYER_STEPS = MIX_STEPS + NB * MOE_STEPS
EXTRA = MIX_STEPS + 6
PAIR = 2 * MOE_STEPS


def ring_turn(step):
    layer, n = divmod(step, LAYER_STEPS)
    assert n != EXTRA
    return layer * (LAYER_STEPS - 1) + n - (n > EXTRA)


def slot_user(step):
    return max(n for n in range(step) if n % LAYER_STEPS != EXTRA and ring_turn(n) == ring_turn(step) - SLOTS)


FILL_BANKS = 4

R_MIX, R_FFN, R_CW, R_CB, R_BR, R_BI, R_LAM, R_MNG, R_DNG = 0, 16, 32, 48, 52, 56, 60, 64, 68
NR = 76

ATTEND = ("S0 S1 P0 T0 S2 V0 P1 T1 S3 V1 P2 T2 P3 V2 T3 P4 V3 QA S4 S5 P5 MA T4 S6 V4 TA T5 DA S7 V5 O0 T6 O1 V6 "
          "T7 O2 V7 O3").split()
PIECES = ["dq2", "dq3", "dk2", "dk3", "dv2", "dv3"]


def attend_fills():
    for x in ATTEND:
        if x == "TA":
            yield from ("dy0", "dy1")
        elif x in ("O2", "O3"):
            yield f"mix1.{x[1]}"
        elif x[0] == "S":
            yield from (f"ds{x[1]}.0", f"ds{x[1]}.1")
        elif x[0] == "T":
            yield f"dt{x[1]}"
        elif x[0] == "P":
            yield PIECES[int(x[1])]


FILLS = (
    ["columns"] + [f"norm0.{i}" for i in range(4)] + ["gates", "xa0", "xa1", "q0", "q1"]
    + [f"lru{j}" for j in range(WT)] + ["k0", "k1", "v0", "v1", "cols_am", "mmax0", "sc0", "ga0", "mmax1", "sc1", "ga1",
                                        "mmax2", "sc2", "o0", "mmax3", "sc3", "o1"]
    + [f"mix0.{i}" for i in range(4)] + ["norm1.0", "norm1.1", "router0", "norm1.2", "norm1.3", "rank0", "total0"]
    + [f"norm2.{i}" for i in range(4)] + [f"{x}{i}" for x in ("dq", "dk", "dv") for i in range(2)]
    + list(attend_fills()) + ["dy2", "dy3", "end mix1.2", "norm3.0", "norm3.1", "end mix1.3", "router1", "norm3.2",
                              "norm3.3", "rank1", "total1"]
)
HELD = ("mix1.2", "mix1.3")


def assign():
    rested, count, bank, nth = list(range(FILL_BANKS)), [0] * FILL_BANKS, {}, {}
    for name in FILLS:
        if name.startswith("end "):
            rested.append(bank[name[4:]])
            continue
        b = bank[name] = rested.pop(0)
        nth[name] = count[b]
        count[b] += 1
        if name not in HELD:
            rested.append(b)
    return bank, nth


BANK, NTH = assign()


def build(nc, x, param_rows, gate_bias, block_weights, route_weights, route_bias, lambda_vectors, ab_w_in, ab_w_out,
          diff_w_qkv, diff_w_o, moe_w_up, moe_w_down, final_norm_g, out):
    with ExitStack() as ctx:
        def sb(name, shape, dt=F32):
            return ctx.enter_context(nc.sbuf_tensor(name, shape, dt))

        def sem(name):
            return ctx.enter_context(nc.semaphore(name))

        ring = sb("ring", [P, SLOTS, SLOT])
        h = sb("h", [P, TT, D])
        xs = sb("xs", [P, TT, D])
        xT = sb("xT", [P, KT, S])
        rows = sb("rows", [NR, P])
        cols = sb("cols", [P, NR])
        ident = sb("ident", [P, P])
        before = sb("before", [P, P])
        upto = sb("upto", [P, P])
        ones = sb("ones", [P, P])
        slot_no = sb("slot_no", [P, CAP])
        prio = sb("prio", [P, NE])
        zrow = sb("zrow", [1, P])
        w_gate = sb("w_gate", [P, KT, 2 * MH])
        w_route = sb("w_route", [P, LAYERS, KT, NG + NE])
        b_route = sb("b_route", [P, LAYERS, NG + NE])
        w_block = sb("w_block", [P, 2, WT, P])
        b_if = sb("b_if", [32 + MH, 1])
        lam_rows = sb("lam_rows", [P, 4, DQK])
        small = sb("small", [P, 136])
        flag = sb("flag", [1, LAYERS], I32)
        arena = sb("arena", [P, 10624])

        def view(at, *dims):
            n = 1
            for d in dims:
                n *= d
            v = arena[:, at:at + n]
            if len(dims) == 1:
                return v
            names = "abcd"[:len(dims)]
            return v.rearrange(f"p ({' '.join(names)}) -> p {' '.join(names)}",
                               **{c: d for c, d in zip(names, dims)})

        xpad = view(0, WT, S + TAPS - 1)
        root = view(0, WT * S)
        xc, r_g, i_g, _, ga = (view(1040 + 1024 * n, WT, S) for n in range(5))
        xc_f, r_f, i_f, t1_f, ga_f = (view(1040 + 1024 * n, WT * S) for n in range(5))
        qT, kT, so = (view(6160 + 1024 * n, WT, S) for n in (0, 1, 3))
        v_n = view(6160 + 2048, TT, W)
        yb = view(6160, TT, MH, P)
        sq = view(7184, TT, MH, P)
        wbuf = r_f[:, 0:2 * (S + P)].rearrange("p (b w) -> p b w", b=2)
        pbuf = i_f[:, 0:2 * (S + P)].rearrange("p (b w) -> p b w", b=2)
        yT = xs[:, :, :].rearrange("p a (b s) -> p (a b) s", s=S)
        gr = [sb(f"gr{n}", [MH, S]) for n in range(2)] + [yT[0:MH, WT + n, :] for n in range(4)]
        dq = view(0, DH, S)
        dk = view(2048, DH, S)
        dv = view(4096, TT, D)
        KEYS = [slice(t * P, t * P + (t + 1) * P) for t in range(TT)]
        SEEN = sum(t + 1 for t in range(TT))
        sp_ = view(6144, 2, 2, SEEN * P)
        dif = view(7680, 2, SEEN * P)
        dT = view(8448, 2, SEEN * P)
        dist = view(9216, SEEN * P)
        on = view(9600, TT, HALF)
        diag = view(7680, TT, P)
        spread_roots = view(8448, S)
        xg = view(0, 2, KT, P)
        sel = view(2048, TT, EB, CAP)
        selg = view(2304, TT, EB, CAP)
        sgt = view(2560, TT, P)
        sig = view(3072, FF)
        hid = view(3584, FF)
        hT = view(4096, FT, P)
        y_s = view(4608, D)
        lg = view(5632, TT, NG + NE)
        mg = view(5704, TT, NG)
        el = view(5712, TT, NE)
        m1 = view(5776, TT, NE)
        m2 = view(5840, TT, NE)
        tmp = view(5904, TT, NE)
        both = view(5968, TT, NE)
        rankm = view(6032, TT, NE + EB)
        gates = view(6104, TT, NE + EB)
        extra = view(6176, TT, NE)
        rs = view(6240, 64)
        rs2 = view(6304, TT, NG)
        ovh = view(6400, FT, S)
        ovs = view(7424, S)
        fg = view(8192, D)
        extra_slot = view(6400, SLOT)

        rstd = small[:, 2:4]
        ss = sb("ss", [P, TT, NH])
        c4 = small[:, 4:8]
        l1a, l1b, l1c = small[:, 8:12], small[:, 12:16], small[:, 16:20]
        am = small[:, 20:36]
        enm = small[:, 36:44]
        den = small[:, 44:52]
        den2 = small[:, 52:60]
        hss = small[:, 60:68]
        lsum = small[:, 68:70]
        nlam = small[:, 70:71]
        mx, sums, rsum = small[:, 20:28], small[:, 28:36], small[:, 36:44]
        oss = small[:, 84:100]
        dng2 = small[:, 100:108]
        minus_half = small[:, 108:124]

        psum = [ctx.enter_context(nc.psum_tensor(f"bank{n}", [P, HALF], F32)) for n in range(8)]
        root_ps = psum[4]
        den_ps = psum[5]
        num_ps = psum[6:8]
        o_ps = psum[4:8]
        hy = psum[0:2]
        gather_ps, turn_ps = psum[2:4], psum[3]
        yb_ps = psum[4:6]
        acc = psum[4:8]

        x_loaded = [sem(f"x_loaded{t}") for t in range(TT)]
        rows_loaded = sem("rows_loaded")
        blocks_zeroed = sem("blocks_zeroed")
        params_loaded = sem("params_loaded")
        gates_loaded = sem("gates_loaded")
        blocks_loaded = sem("blocks_loaded")
        fgain_loaded = sem("fgain_loaded")
        slot_loaded = [sem(f"slot_loaded{n}") for n in range(SLOTS)]
        extra_loaded = sem("extra_loaded")
        steps_done = sem("steps_done")
        ident_ready = sem("ident_ready")
        consts_ready = sem("consts_ready")
        pool_step = sem("pool_step")
        dist_ready = sem("dist_ready")
        fill_full = [sem(f"fill_full{n}") for n in range(FILL_BANKS)]
        fill_free = [sem(f"fill_free{n}") for n in range(FILL_BANKS)]
        dve_step = sem("dve_step")
        cols_ready = sem("cols_ready")
        squares = sem("squares")
        mean_ready = sem("mean_ready")
        root_ready = sem("root_ready")
        diag_ready = sem("diag_ready")
        root_spread = sem("root_spread")
        xs_ready = sem("xs_ready")
        h_ready = sem("h_ready")
        lam_abs = sem("lam_abs")
        lam_exp = sem("lam_exp")
        lsum_ready = sem("lsum_ready")
        lsum_exp = sem("lsum_exp")
        f_abs = sem("f_abs")
        f_exp = sem("f_exp")
        am_rows = sem("am_rows")
        am_cols = sem("am_cols")
        enm_ready = sem("enm_ready")
        conv_done = sem("conv_done")
        lru_tanh = sem("lru_tanh")
        lru_floor = sem("lru_floor")
        lru_root = sem("lru_root")
        gelu_in = sem("gelu_in")
        gelu_tanh = sem("gelu_tanh")
        ya_ready = sem("ya_ready")
        w_arg = sem("w_arg")
        w_exp = sem("w_exp")
        p_ready = sem("p_ready")
        num_done = sem("num_done")
        yb_ready = sem("yb_ready")
        yT_ready = sem("yT_ready")
        soft_max = sem("soft_max")
        soft_exp = sem("soft_exp")
        diff_ready = sem("diff_ready")
        pv_done = sem("pv_done")
        on_squares = sem("on_squares")
        early_out = sem("early_out")
        on_ready = sem("on_ready")
        yb_full = sem("yb_full")
        route_arg = sem("route_arg")
        route_exp = sem("route_exp")
        picked = sem("picked")
        flag_ready = sem("flag_ready")
        sel_ready = sem("sel_ready")
        gather_full = sem("gather_full")
        gather_free = sem("gather_free")
        selg_ready = sem("selg_ready")
        sgt_full = sem("sgt_full")
        sgt_ready = sem("sgt_ready")
        sig_done = sem("sig_done")
        hid_step = sem("hid_step")
        hid_done = sem("hid_done")
        hT_full = sem("hT_full")
        hT_ready = sem("hT_ready")
        y_half = sem("y_half")
        y_act = sem("y_act")
        y_dve = sem("y_dve")
        scattered = sem("scattered")
        dense_load = [sem(f"dense_load{l}") for l in range(LAYERS)]
        dense_turned = [sem(f"dense_turned{l}") for l in range(LAYERS)]
        dense_x = [sem(f"dense_x{l}") for l in range(LAYERS)]
        dense_gu = [sem(f"dense_gu{l}") for l in range(LAYERS)]
        dense_sig = [sem(f"dense_sig{l}") for l in range(LAYERS)]
        dense_mul = [sem(f"dense_mul{l}") for l in range(LAYERS)]
        dense_h = [sem(f"dense_h{l}") for l in range(LAYERS)]
        dense_y = [sem(f"dense_y{l}") for l in range(LAYERS)]
        dense_add = [sem(f"dense_add{l}") for l in range(LAYERS)]
        fin_ready = sem("fin_ready")
        out_stored = sem("out_stored")

        N_PARAMS = 3
        GATE_LOADS = 3
        BLOCKS = 4

        def bank_of(name):
            return psum[BANK[name]]

        def wait_full(eng, name):
            eng.wait_ge(fill_full[BANK[name]], NTH[name] + 1)

        def wait_free(eng, name):
            if NTH[name] > 0:
                eng.wait_ge(fill_free[BANK[name]], NTH[name])

        def wait_read(eng, name):
            eng.wait_ge(fill_free[BANK[name]], NTH[name] + 1)

        def full(ins, name):
            ins.then_inc(fill_full[BANK[name]], 1)

        def free(ins, name):
            ins.then_inc(fill_free[BANK[name]], 1)

        def slot(step):
            if step % LAYER_STEPS == EXTRA:
                return extra_slot
            return ring[:, ring_turn(step) % SLOTS, :]

        def slot_k(step):
            return slot(step).rearrange("p (k n) -> p k n", k=KT)

        def slot_e(step):
            return slot(step).rearrange("p (e n) -> p e n", e=EB)

        def loaded(step):
            if step % LAYER_STEPS == EXTRA:
                return extra_loaded
            return slot_loaded[ring_turn(step) % SLOTS]

        def wait_slot(eng, step, i=0):
            if step % LAYER_STEPS == EXTRA:
                eng.wait_ge(extra_loaded, 16 * (step // LAYER_STEPS + 1))
            else:
                eng.wait_ge(slot_loaded[ring_turn(step) % SLOTS],
                            i * (16 * PAIR // SLOTS) + 16 * (ring_turn(step) // SLOTS + 1))

        block = ctx.enter_context(nc.Block())

        @block.sync
        def _(sp):
            for t in range(TT):
                sp.dma_start(h[:, t, :], x[0, t * P:(t + 1) * P, :]).then_inc(x_loaded[t], 16)
                if t == 0:
                    sp.dma_start(rows[:, :], param_rows).then_inc(rows_loaded, 16)

            def small_parameters():
                sp.wait_ge(blocks_zeroed, 1)
                for half in range(2):
                    lo = half * 64
                    for g in range(2):
                        sp.dma_start(w_block[lo:lo + 64, g, :, lo:lo + 64], block_weights[g, half])\
                            .then_inc(blocks_loaded, 16)
                sp.dma_start(w_route[:, :, :, :], route_weights).then_inc(params_loaded, 16)
                sp.dma_start(b_route[:, :, :], route_bias.partition_broadcast(P)).then_inc(params_loaded, 16)
                sp.dma_start(lam_rows[:, :, :], lambda_vectors.partition_broadcast(P)).then_inc(params_loaded, 16)

            def mixer(layer, w_in, w_out, order):
                base = layer * LAYER_STEPS
                chunks = [w_in[:, HALF * n:HALF * (n + 1)] for n in order]
                chunks += [w_out[:, HALF * n:HALF * (n + 1)] for n in range(NH)]
                for n, src in enumerate(chunks):
                    step = base + n
                    if step >= SLOTS:
                        sp.wait_ge(steps_done, slot_user(step) + 1)
                    sp.dma_start(slot_k(step), src.rearrange("(k p) n -> p k n", p=P))\
                        .then_inc(loaded(step), 16)
                    if step == 1:
                        small_parameters()

            def packed(layer, i, par):
                base = layer * LAYER_STEPS + MIX_STEPS + par * MOE_STEPS
                e0 = i * (2 * EB) + par * EB
                for n in range(MOE_STEPS):
                    w, k = (moe_w_up, n) if n < KT else (moe_w_down, n - KT)
                    if base + n == layer * LAYER_STEPS + EXTRA:
                        if layer == 0:
                            sp.wait_ge(yT_ready, 1)
                        else:
                            wait_full(sp, "dy3")
                    else:
                        sp.wait_ge(steps_done, i * PAIR + (slot_user(base + n) + 1))
                    sp.dma_start(slot_e(base + n), w[layer, bass.ds(e0, EB), k * P:(k + 1) * P, :]
                                 .rearrange("e p n -> p e n")).then_inc(loaded(base + n), 16)

            def experts(layer):
                packed(layer, 0, 0)
                packed(layer, 0, 1)
                with sp.Fori(0, NB // 2 - 1) as i:
                    packed(layer, i, 2)
                    packed(layer, i, 3)

            def dense_expert(layer, e):
                sp.dma_start(ring[:, 0:2, :].rearrange("p a (k n) -> p (a k) n", k=KT // 2),
                             moe_w_up[layer, e].rearrange("(k p) n -> p k n", p=P)).then_inc(dense_load[layer], 16)
                sp.dma_start(ring[:, 2, :].rearrange("p (k n) -> p k n", k=FT),
                             moe_w_down[layer, e].rearrange("(k p) n -> p k n", p=P)).then_inc(dense_load[layer], 16)

            def dense(layer):
                sp.wait_ge(flag_ready, layer + 1)
                over = sp.value_load(flag[0:1, layer:layer + 1], min_val=0, max_val=1)
                with sp.If(over != 0):
                    sp.wait_ge(steps_done, (layer + 1) * LAYER_STEPS)
                    dense_expert(layer, 0)
                    with sp.Fori(0, NE - 1) as e:
                        sp.wait_ge(dense_y[layer], e * 4 + 4)
                        dense_expert(layer, e + 1)
                    sp.wait_ge(dense_y[layer], 4 * NE)

            mixer(0, ab_w_in[0], ab_w_out[0], (0, 2, 3, 4, 1, 5))
            experts(0)
            dense(0)
            mixer(1, diff_w_qkv[0], diff_w_o[0], (0, 2, 4, 1, 3, 5))
            experts(1)
            dense(1)
            for t in range(TT):
                sp.wait_ge(fin_ready, t + 1)
                sp.dma_start(out[0, t * P:(t + 1) * P, :], xs[:, t, :]).then_inc(out_stored, 16)
            sp.wait_ge(out_stored, 16 * TT)

        @block.gpsimd
        def _(pool):
            steps = [0]

            def link(ins):
                steps[0] += 1
                ins.then_inc(pool_step, 1)
                pool.wait_ge(pool_step, steps[0])

            link(pool.memset(minus_half, -0.5))
            pool.memset(w_block[:, :, :, :], 0.0).then_inc(blocks_zeroed, 1)
            link(pool.memset(ident[:, :], 0.0))
            pool.affine_select(out=ident[:, :], in_=ident[:, :], compare_op=ALU.not_equal, fill=1.0, base=0,
                               pattern=[[-1, P]], channel_multiplier=1).then_inc(ident_ready, 1)
            link(pool.memset(ones[:, :], 1.0))
            pool.affine_select(out=before[:, :], in_=ones[:, :], compare_op=ALU.is_gt, fill=0.0, base=0,
                               pattern=[[1, P]], channel_multiplier=-1)
            pool.affine_select(out=upto[:, :], in_=ones[:, :], compare_op=ALU.is_ge, fill=0.0, base=0,
                               pattern=[[1, P]], channel_multiplier=-1)
            pool.iota(slot_no[:, :], pattern=[[1, CAP]], base=0, channel_multiplier=0,
                      allow_small_or_imprecise_dtypes=True)
            pool.iota(prio[:, :], pattern=[[-1, NE]], base=NE, channel_multiplier=0,
                      allow_small_or_imprecise_dtypes=True)
            pool.memset(zrow[:, :], 0.0).then_inc(consts_ready, 1)
            n_roots = [0]

            def inverse_root(v):
                n_roots[0] += 1
                pool.wait_ge(mean_ready, n_roots[0])
                pool.tensor_tensor(v, v, minus_half[:, 0:v.shape[1]], ALU.pow).then_inc(root_ready, 1)

            inverse_root(rstd)
            inverse_root(hss)
            inverse_root(rstd)
            inverse_root(rstd)
            pool.wait_ge(h_ready, 8)
            for t in range(TT):
                nk = (t + 1) * P
                for n, sign in enumerate((1, -1)):
                    part = sp_[:, n, t, 0:nk]
                    link(pool.iota(part, pattern=[[sign, nk]], base=-sign * t * P, channel_multiplier=-sign,
                                   allow_small_or_imprecise_dtypes=True))
                    link(pool.affine_select(out=part, in_=part, compare_op=ALU.is_gt, fill=0.0, base=sign * t * P,
                                            pattern=[[-sign, nk]], channel_multiplier=sign))
                link(pool.tensor_tensor(dist[:, KEYS[t]], sp_[:, 0, t, 0:nk], sp_[:, 1, t, 0:nk], ALU.add))
            for t in range(TT):
                for c in range(P // CHUNK):
                    seen = (c + 1) * CHUNK
                    if seen < P:
                        ins = pool.memset(dist[c * CHUNK:(c + 1) * CHUNK, KEYS[t].stop - P + seen:KEYS[t].stop],
                                          -1e30)
            ins.then_inc(dist_ready, 1)
            for half in range(2):
                inverse_root(oss[:, 8 * half:8 * half + 8])
            inverse_root(rstd)
            for t in range(TT):
                inverse_root(rstd[:, t:t + 1])

        @block.tensor
        def _(pe):
            def turn_tiles(bank, rows_of, i):
                for c in range(2):
                    for t in range(TT):
                        k = 2 * i + c
                        ins = pe.transpose(bank[:, c * S + t * P:c * S + (t + 1) * P],
                                           rows_of[:, t, k * P:(k + 1) * P], ident[:, :])
                return ins

            def feature_major(n):
                for t in range(TT):
                    if n == 0:
                        pe.wait_ge(x_loaded[t], 16)
                    else:
                        pe.wait_ge(h_ready, 4 + NH * (t + 1))
                    for i in range(4):
                        if t == 0:
                            wait_free(pe, f"norm{n}.{i}")
                        for c in range(2):
                            k = 2 * i + c
                            ins = pe.transpose(bank_of(f"norm{n}.{i}")[:, c * S + t * P:c * S + (t + 1) * P],
                                               h[:, t, k * P:(k + 1) * P], ident[:, :])
                        if t == TT - 1:
                            full(ins, f"norm{n}.{i}")
                if n == 0:
                    pe.wait_ge(consts_ready, 1)
                pe.wait_ge(diag_ready, n // 2 + 1)
                for t in range(TT):
                    ins = pe.matmul(root_ps[:, t * P:(t + 1) * P], ones[:, :], diag[:, t, :], start=True, stop=True)
                ins.then_inc(root_spread, 1)

            def stream_turned(layer, fills):
                for i in fills:
                    name = f"norm{1 + 2 * layer}.{i}"
                    pe.wait_ge(h_ready, 8 * layer + (2 if i < 2 else 4))
                    wait_free(pe, name)
                    full(turn_tiles(bank_of(name), h, i), name)

            def router(layer, fills):
                name = f"router{layer}"
                for i in fills:
                    wait_read(pe, f"norm{1 + 2 * layer}.{i}")
                    for k in (2 * i, 2 * i + 1):
                        for t in range(TT):
                            at = t * (NG + NE)
                            ins = pe.matmul(bank_of(name)[:, at:at + NG + NE], xT[:, k, t * P:(t + 1) * P],
                                            w_route[:, layer, k, :], start=(k == 0 and t == 0), stop=(k == KT - 1),
                                            skip_group_check=True)
                return ins

            def mix_end(layer, finish):
                finish(2)
                stream_turned(layer, (0, 1))
                finish(3)
                wait_free(pe, f"router{layer}")
                if layer == 0:
                    pe.wait_ge(params_loaded, 16 * N_PARAMS)
                router(layer, (0, 1))
                stream_turned(layer, (2, 3))
                full(router(layer, (2, 3)), f"router{layer}")

            def wait_xT(n, k):
                if k % 2 == 0:
                    wait_read(pe, f"norm{n}.{k // 2}")

            def project_T(step, names, first=0, norm=None):
                wait_slot(pe, step)
                w = slot_k(step)
                for i, name in enumerate(names, first):
                    wait_free(pe, name)
                    for c in range(2):
                        for k in range(KT):
                            n = (2 * i + c) * P
                            if norm is not None and (i, c) == (0, 0):
                                wait_xT(norm, k)
                            ins = pe.matmul(bank_of(name)[:, c * S:(c + 1) * S], w[:, k, n:n + P], xT[:, k, :],
                                            start=(k == 0), stop=(k == KT - 1))
                    full(ins, name)

            def project_N(step, names, lhs=xT, first=0):
                wait_slot(pe, step)
                w = slot_k(step)
                for t, name in enumerate(names, first):
                    wait_free(pe, name)
                    for k in range(KT):
                        ins = pe.matmul(bank_of(name)[:, :], lhs[:, k, t * P:(t + 1) * P], w[:, k, :],
                                        start=(k == 0), stop=(k == KT - 1))
                    full(ins, name)

            pe.wait_ge(ident_ready, 1)
            pe.wait_ge(rows_loaded, 16)
            full(pe.transpose(bank_of("columns")[:, 0:NR], rows[:, :], ident[0:NR, 0:NR]), "columns")
            feature_major(0)
            pe.wait_ge(gates_loaded, 16 * GATE_LOADS)
            wait_free(pe, "gates")
            for k in range(KT):
                wait_xT(0, k)
                for g in range(2):
                    ins = pe.matmul(bank_of("gates")[32 * g:32 * g + MH, 0:S], w_gate[:, k, g * MH:(g + 1) * MH],
                                    xT[:, k, :], start=(k == 0), stop=(k == KT - 1), skip_group_check=True)
            full(ins, "gates")
            project_T(0, ["xa0", "xa1"])
            project_T(1, ["q0", "q1"])
            pe.wait_ge(conv_done, 1)
            pe.wait_ge(blocks_loaded, 16 * BLOCKS)
            for j in range(WT):
                name = f"lru{j}"
                wait_free(pe, name)
                for g in range(2):
                    ins = pe.matmul(bank_of(name)[:, g * S:(g + 1) * S], w_block[:, g, j, :], xc[:, j, :],
                                    start=True, stop=True)
                full(ins, name)
            project_T(2, ["k0", "k1"])
            project_N(3, ["v0", "v1"])
            pe.wait_ge(am_rows, 1)
            wait_free(pe, "cols_am")
            for g, src in enumerate((gr[4], gr[5])):
                for t in range(TT):
                    at = (g * TT + t) * MH
                    ins = pe.transpose(bank_of("cols_am")[:, at:at + MH], src[:, t * P:(t + 1) * P],
                                       ident[0:MH, 0:MH])
            full(ins, "cols_am")

            def head_scores(hd):
                name = f"mmax{hd}"
                wait_free(pe, name)
                full(pe.matmul(bank_of(name)[:, 0:S], ident[0:MH, hd:hd + 1].broadcast_to([MH, P]), gr[3],
                               start=True, stop=True), name)
                name = f"sc{hd}"
                wait_free(pe, name)
                pe.matmul(bank_of(name)[:, 0:S], kT[:, hd, 0:P], qT[:, hd, :], start=True, stop=True)
                full(pe.matmul(bank_of(name)[:, S:S + P], kT[:, hd, P:S], qT[:, hd, P:S], start=True, stop=True),
                     name)

            def head_values(hd):
                pe.wait_ge(p_ready, hd + 1)
                pb = pbuf[:, hd % 2, :]
                vh = slice(hd * P, (hd + 1) * P)
                pe.matmul(num_ps[0][:, vh], pb[:, 0:P], v_n[:, 0, vh], start=True, stop=True)
                pe.matmul(num_ps[1][:, vh], pb[:, P:2 * P], v_n[:, 0, vh], start=True, stop=False)
                pe.matmul(num_ps[1][:, vh], pb[:, 2 * P:3 * P], v_n[:, 1, vh], start=False, stop=True)
                pe.matmul(den_ps[:, hd:hd + 1], pb[:, 0:P], ones[:, 0:1], start=True, stop=True)
                pe.matmul(den_ps[:, MH + hd:MH + hd + 1], pb[:, P:2 * P], ones[:, 0:1], start=True, stop=False)
                pe.matmul(den_ps[:, MH + hd:MH + hd + 1], pb[:, 2 * P:3 * P], ones[:, 0:1], start=False,
                          stop=True).then_inc(num_done, 1)

            for name in ("q0", "q1", "k0", "k1", "v0", "v1"):
                wait_read(pe, name)
            pe.wait_ge(consts_ready, 1)
            head_scores(0)
            project_T(4, ["ga0"])
            head_scores(1)
            head_values(0)
            project_T(4, ["ga1"], 1)
            head_scores(2)
            head_values(1)
            project_T(5, ["o0"])
            head_scores(3)
            head_values(2)
            project_T(5, ["o1"], 1)
            head_values(3)

            def mix(layer, turn, ks):
                n, t = turn // TT, turn % TT
                for k in ks:
                    ins = pe.matmul(bank_of(f"mix{layer}.{turn}")[:, :], yT[:, k, t * P:(t + 1) * P],
                                    slot_k(layer * LAYER_STEPS + 6 + n)[:, k, :], start=(k == 0), stop=(k == KT - 1))
                return ins

            pe.wait_ge(ya_ready, 1)
            for turn in range(4):
                wait_slot(pe, 6 + turn // TT)
                wait_free(pe, f"mix0.{turn}")
                mix(0, turn, range(WT))
            pe.wait_ge(yb_ready, 1)
            for i in range(2):
                for c in range(2):
                    for t in range(TT):
                        ins = pe.transpose(yb_ps[i][:, c * S + t * P:c * S + (t + 1) * P],
                                           yb[:, t, 2 * i + c, :], ident[:, :])
                ins.then_inc(yb_full, 1)
            pe.wait_ge(yT_ready, 1)

            def finish(turn):
                full(mix(0, turn, range(WT, KT)), f"mix0.{turn}")

            finish(0)
            finish(1)
            mix_end(0, finish)

            def gather(g, buf, part):
                for k in range(GH):
                    kt = part * GH + k
                    for t in range(TT):
                        ins = pe.matmul(gather_ps[part][:, k * P:(k + 1) * P], xs[:, t, kt * P:(kt + 1) * P],
                                        sel[:, t, :, :].rearrange("p e c -> p (e c)"), start=(t == 0),
                                        stop=(t == TT - 1))
                ins.then_inc(gather_full, 1)

            def packed(layer, i, par):
                base = layer * LAYER_STEPS + MIX_STEPS
                b = i * 2 + (layer * NB + par)
                g = i * 2 + (layer * (NB + 1) + par)
                buf = par % 2
                for n in range(KT):
                    j = par * MOE_STEPS + n
                    if n % GH == 0:
                        pe.wait_ge(gather_free, g * 2 + (n // GH + 1))
                    wait_slot(pe, base + j, i)
                    for half in range(NH):
                        for e in range(EB):
                            ins = pe.matmul(hy[half][e * CAP:(e + 1) * CAP, :], xg[:, buf, n, e * CAP:(e + 1) * CAP],
                                            slot_e(base + j)[:, e, half * HALF:(half + 1) * HALF],
                                            start=(n == 0), stop=(n == KT - 1), skip_group_check=True)
                    ins.then_inc(steps_done, 1)
                    if n == 1:
                        pe.wait_ge(selg_ready, b + 1)
                        for t in range(TT):
                            ins = pe.transpose(gather_ps[0][:, t * P:(t + 1) * P],
                                               selg[:, t, :, :].rearrange("p e c -> p (e c)"), ident[:, :])
                        ins.then_inc(sgt_full, 1)
                    if n == GH - 1:
                        pe.wait_ge(sel_ready, g + 2)
                        pe.wait_ge(sgt_ready, b + 1)
                        gather(g + 1, 1 - buf, 0)
                gather(g + 1, 1 - buf, 1)
                pe.wait_ge(hid_done, b + 1)
                pe.wait_ge(gather_free, g * 2 + 4)
                for f in range(FT):
                    ins = pe.transpose(turn_ps[:, f * P:(f + 1) * P], hid[:, f * P:(f + 1) * P], ident[:, :])
                ins.then_inc(hT_full, 1)
                pe.wait_ge(hT_ready, b + 1)
                for n in range(FT):
                    j = par * MOE_STEPS + KT + n
                    wait_slot(pe, base + j, i)
                    for half in range(NH):
                        for e in range(EB):
                            ins = pe.matmul(hy[half][e * CAP:(e + 1) * CAP, :], hT[:, n, e * CAP:(e + 1) * CAP],
                                            slot_e(base + j)[:, e, half * HALF:(half + 1) * HALF],
                                            start=(n == 0), stop=(n == FT - 1), skip_group_check=True)
                        if n == FT - 1 and half == 0:
                            ins.then_inc(y_half, 1)
                    ins.then_inc(steps_done, 1)
                pe.wait_ge(y_act, b + 1)
                for t in range(TT):
                    for half in range(NH):
                        if t == 0 and half == 1:
                            pe.wait_ge(y_dve, b + 1)
                        pe.matmul(acc[t * NH + half][:, :], sgt[:, t, :], y_s[:, half * HALF:(half + 1) * HALF],
                                  start=False, stop=False, skip_group_check=True).then_inc(scattered, 1)

            def experts(layer):
                pe.wait_ge(squares, 4 * (2 * layer + 2))
                for a in acc:
                    pe.matmul(a[:, :], zrow[:, :], h[0:1, 0, 0:HALF], start=True, stop=False, skip_group_check=True)
                name = f"rank{layer}"
                wait_free(pe, name)
                pe.wait_ge(picked, layer + 1)
                bank = bank_of(name)
                pe.matmul(bank[:, 0:TT * NE], before[:, :], both.rearrange("p t n -> p (t n)"), start=True,
                          stop=False, skip_group_check=True)
                full(pe.matmul(bank[:, NE:2 * NE], ones[:, :], both[:, 0, :], start=False, stop=True,
                               skip_group_check=True), name)
                name = f"total{layer}"
                wait_free(pe, name)
                for t in range(TT):
                    ins = pe.matmul(bank_of(name)[:, 0:NE], ones[:, :], both[:, t, :], start=(t == 0),
                                    stop=(t == TT - 1))
                full(ins, name)
                fills = [n for n in FILLS[:FILLS.index(name) + 1] if n in BANK]
                for b in range(FILL_BANKS):
                    wait_read(pe, [n for n in fills if BANK[n] == b][-1])
                g = layer * (NB + 1)
                pe.wait_ge(xs_ready, TT * (layer + 1))
                pe.wait_ge(sel_ready, g + 1)
                for part in range(2):
                    gather(g, 0, part)
                packed(layer, 0, 0)
                packed(layer, 0, 1)
                with pe.Fori(0, NB // 2 - 1) as i:
                    packed(layer, i, 2)
                    packed(layer, i, 3)

            def dense(layer):
                pe.wait_ge(flag_ready, layer + 1)
                over = pe.value_load(flag[0:1, layer:layer + 1], min_val=0, max_val=1)
                with pe.If(over != 0):
                    pe.wait_ge(dense_h[layer], 2)
                    for i in range(4):
                        turn_tiles(psum[i], xs, i).then_inc(dense_turned[layer], 1)
                    pe.wait_ge(dense_x[layer], 4)
                    up = ring[:, 0:2, :].rearrange("p a (k n) -> p (a k) n", k=KT // 2)
                    down = ring[:, 2, :].rearrange("p (k n) -> p k n", k=FT)
                    with pe.Fori(0, NE) as e:
                        pe.wait_ge(dense_load[layer], e * 32 + 32)
                        for f in range(FT):
                            pe.wait_ge(dense_h[layer], e * FT + (f + 1))
                            for g in range(2):
                                for k in range(KT):
                                    ins = pe.matmul(psum[f % 2][:, g * S:(g + 1) * S],
                                                    up[:, k, g * FF + f * P:g * FF + (f + 1) * P], xT[:, k, :],
                                                    start=(k == 0), stop=(k == KT - 1))
                            ins.then_inc(dense_gu[layer], 1)
                        pe.wait_ge(dense_h[layer], e * FT + (FT + 2))
                        for n in range(TT * NH):
                            pe.wait_ge(dense_add[layer], e * 4 + (n + 1))
                            for f in range(FT):
                                ins = pe.matmul(psum[2 + n % 2][:, :], ovh[:, f, (n // NH) * P:(n // NH + 1) * P],
                                                down[:, f, (n % NH) * HALF:(n % NH + 1) * HALF],
                                                start=(f == 0), stop=(f == FT - 1))
                            ins.then_inc(dense_y[layer], 1)

            experts(0)
            dense(0)

            feature_major(2)
            s1 = LAYER_STEPS
            project_T(s1, ["dq0", "dq1"], norm=2)
            project_T(s1 + 1, ["dk0", "dk1"])
            project_N(s1 + 2, ["dv0", "dv1"])

            def piece(i):
                project = (project_T, project_T, project_N)[i // 2]
                project(s1 + 3 + i // 2, [PIECES[i]], first=i % 2)

            def unit_scores(hd):
                for c in range(2):
                    name = f"ds{hd}.{c}"
                    wait_free(pe, name)
                    for t in range(TT):
                        ins = pe.matmul(bank_of(name)[:, KEYS[t]], dq[c * DQK:(c + 1) * DQK, hd, t * P:(t + 1) * P],
                                        dk[c * DQK:(c + 1) * DQK, hd, 0:(t + 1) * P], start=True, stop=True)
                    full(ins, name)

            def unit_turned(hd):
                name = f"dt{hd}"
                wait_free(pe, name)
                pe.wait_ge(diff_ready, hd + 1)
                for kt in range(SEEN):
                    ins = pe.transpose(bank_of(name)[:, kt * P:(kt + 1) * P], dif[:, hd % 2, kt * P:(kt + 1) * P],
                                       ident[:, :])
                full(ins, name)

            def unit_values(hd):
                wait_read(pe, f"dt{hd}")
                at = (hd % 4) * P
                for t in range(TT):
                    for kt in range(t + 1):
                        ins = pe.matmul(o_ps[(hd // 4) * TT + t][:, at:at + P],
                                        dT[:, hd % 2, (t + kt) * P:(t + kt + 1) * P],
                                        dv[:, kt, hd * P:(hd + 1) * P], start=(kt == 0), stop=(kt == t))
                ins.then_inc(pv_done, 1)

            def copied(names):
                for name in names:
                    wait_read(pe, name)

            def turn_heads(half):
                pe.wait_ge(on_ready, half + 1)
                for i in range(2):
                    name = f"dy{2 * half + i}"
                    wait_free(pe, name)
                    for c in range(2):
                        for t in range(TT):
                            k = 2 * i + c
                            ins = pe.transpose(bank_of(name)[:, c * S + t * P:c * S + (t + 1) * P],
                                               on[:, t, k * P:(k + 1) * P], ident[:, :])
                    full(ins, name)

            def early(t, ks):
                for k in ks:
                    ins = pe.matmul(o_ps[t][:, :], yT[:, k, t * P:(t + 1) * P], slot_k(s1 + 6)[:, k, :],
                                    start=(k == 0), stop=(k == KT - 1))
                return ins

            copied(["dq0", "dq1", "dk0", "dk1", "dv0", "dv1"])
            for x in ATTEND:
                i = int(x[1]) if x[1].isdigit() else None
                if x == "TA":
                    turn_heads(0)
                elif x[0] == "P":
                    piece(i)
                elif x[0] == "S":
                    if i == DH // 2:
                        copied(["dq2", "dq3", "dk2", "dk3"])
                    unit_scores(i)
                elif x[0] == "T":
                    unit_turned(i)
                elif x[0] == "V":
                    if i == DH // 2:
                        copied(["dv2", "dv3"])
                    unit_values(i)
                elif x in ("O0", "O1"):
                    copied(["dy0", "dy1"])
                    wait_slot(pe, s1 + 6)
                    early(i, range(KT // 2))
                elif x in ("O2", "O3"):
                    wait_slot(pe, s1 + 7)
                    wait_free(pe, f"mix1.{i}")
                    mix(1, i, range(KT // 2))
            turn_heads(1)
            copied(["dy2", "dy3"])
            early(0, range(KT // 2, KT)).then_inc(early_out, 1)
            early(1, range(KT // 2, KT)).then_inc(early_out, 1)

            def rest(turn):
                full(mix(1, turn, range(KT // 2, KT)), f"mix1.{turn}")

            mix_end(1, rest)
            experts(1)
            dense(1)

        @block.scalar
        def _(act):
            gate_columns = ab_w_in[0][:, 6 * HALF:6 * HALF + 2 * MH]
            act.dma_start(w_gate[:, :, :], gate_columns.rearrange("(k p) n -> p k n", p=P)).then_inc(gates_loaded, 16)
            for g in range(2):
                act.dma_start(b_if[32 * g:32 * g + MH, :], gate_bias[g]).then_inc(gates_loaded, 16)

            def norm_squares(n, pieces=range(TT * NH)):
                for piece in pieces:
                    t, half = (piece % TT, piece // TT) if n in (1, 3) else (piece // NH, piece % NH)
                    if n == 0:
                        act.wait_ge(x_loaded[t], 16)
                    else:
                        act.wait_ge(h_ready, 4 * (n - 1) + piece + 1)
                    if n in (0, 1, 3) and piece >= 2:
                        act.wait_ge(squares, 4 * n + piece - 1)
                    bank = psum[6 + piece % 2] if n in (0, 1, 3) else acc[piece]
                    act.activation(bank[:, :], h[:, t, half * HALF:(half + 1) * HALF], ACT.Square,
                                   accum_out=ss[:, t, half:half + 1]).then_inc(squares, 1)
                    if n in (1, 3) and t == TT - 1:
                        act.sem_inc(steps_done, 1)

            def second_rows(root):
                act.wait_ge(root_ready, root)
                act.activation(xs[:, 1, :], h[:, 1, :], ACT.Copy, scale=rstd[:, 1:2]).then_inc(xs_ready, 1)

            def turned(n, i, at):
                name = f"norm{n}.{i}"
                wait_full(act, name)
                for c in range(2):
                    k = 2 * i + c
                    ins = act.activation(xT[:, k, :], bank_of(name)[:, c * S:(c + 1) * S], ACT.Copy,
                                         scale=cols[:, at + k:at + k + 1])
                free(ins, name)

            def copy_fill(dst, name):
                wait_full(act, name)
                free(act.activation(dst, bank_of(name)[:, :], ACT.Copy), name)

            def step_done():
                act.sem_inc(steps_done, 1)

            def pair(t, i):
                return t[:, 2 * i:2 * i + 2, :].rearrange("p a s -> p (a s)")

            norm_squares(0)
            act.wait_ge(cols_ready, 1)
            act.wait_ge(lam_abs, 1)
            act.activation(l1b, l1a, ACT.Exp, scale=-1.0).then_inc(lam_exp, 1)
            act.wait_ge(f_abs, 1)
            act.activation(gr[2], gr[2], ACT.Exp, scale=-1.0).then_inc(f_exp, 1)
            for i in range(2):
                name = f"xa{i}"
                wait_full(act, name)
                free(act.activation(xpad[:, 2 * i:2 * i + 2, TAPS - 1:],
                                    bank_of(name)[:, :].rearrange("p (a s) -> p a s", a=2), ACT.Copy), name)
            step_done()
            for i in range(2):
                copy_fill(pair(qT, i), f"q{i}")
            step_done()
            for j in range(WT):
                name = f"lru{j}"
                wait_full(act, name)
                act.activation(r_g[:, j, :], bank_of(name)[:, 0:S], ACT.Sigmoid, bias=cols[:, R_BR + j:R_BR + j + 1])
                free(act.activation(i_g[:, j, :], bank_of(name)[:, S:2 * S], ACT.Sigmoid,
                                    bias=cols[:, R_BI + j:R_BI + j + 1]), name)
            for j in range(WT):
                name = f"lru{j}"
                wait_read(act, name)
            for j in range(WT):
                ins = act.activation(r_g[:, j, :], r_g[:, j, :], ACT.Tanh, scale=c4[:, j:j + 1])
            ins.then_inc(lru_tanh, 1)
            act.wait_ge(lru_floor, 1)
            act.activation(root, root, ACT.Sqrt).then_inc(lru_root, 1)
            for i in range(2):
                copy_fill(pair(kT, i), f"k{i}")
            step_done()
            for t in range(TT):
                copy_fill(v_n[:, t, :], f"v{t}")
            step_done()
            act.wait_ge(am_cols, 1)
            act.activation(enm, am[:, 8:16], ACT.Exp).then_inc(enm_ready, 1)

            def head_exp(hd):
                act.wait_ge(w_arg, hd + 1)
                act.activation(wbuf[:, hd % 2, :], wbuf[:, hd % 2, :], ACT.Exp, scale=-1.0).then_inc(w_exp, 1)

            def gate_sigmoid(i):
                name = f"o{i}"
                wait_full(act, name)
                free(act.activation(pair(so, i), bank_of(name)[:, :], ACT.Sigmoid), name)

            head_exp(0)
            copy_fill(pair(ga, 0), "ga0")
            head_exp(1)
            copy_fill(pair(ga, 1), "ga1")
            step_done()
            head_exp(2)
            act.wait_ge(gelu_in, 1)
            gt = yT[:, 0:WT, :].rearrange("p a s -> p (a s)")
            act.activation(gt, gt, ACT.Tanh, scale=math.sqrt(2.0 / math.pi)).then_inc(gelu_tanh, 1)
            gate_sigmoid(0)
            head_exp(3)
            gate_sigmoid(1)
            step_done()

            def packed(layer, i, par):
                b = i * 2 + (layer * NB + par)
                steps = i * (2 * MOE_STEPS) + (layer * LAYER_STEPS + MIX_STEPS + par * MOE_STEPS)
                act.wait_ge(steps_done, steps + KT)
                act.activation(sig, hy[0][:, :], ACT.Sigmoid).then_inc(sig_done, 1)
                act.wait_ge(hT_full, b + 1)
                act.activation(hT[:, :, :].rearrange("p f c -> p (f c)"), turn_ps[:, :], ACT.Copy)\
                    .then_inc(hT_ready, 1)
                act.wait_ge(y_half, b + 1)
                act.activation(y_s[:, 0:HALF], hy[0][:, :], ACT.Copy).then_inc(y_act, 1)

            def experts(layer):
                n, at = 1 + 2 * layer, R_FFN + layer * KT
                norm_squares(n, range(3))
                turned(n, 1, at)
                norm_squares(n, range(3, 4))
                turned(n, 3, at)
                second_rows((3, 7)[layer])
                act.wait_ge(route_arg, layer + 1)
                act.activation(rs[:, 10:20], rs[:, 0:10], ACT.Exp).then_inc(route_exp, 1)
                packed(layer, 0, 0)
                packed(layer, 0, 1)
                with act.Fori(0, NB // 2 - 1) as i:
                    packed(layer, i, 2)
                    packed(layer, i, 3)

            def dense(layer):
                act.wait_ge(flag_ready, layer + 1)
                over = act.value_load(flag[0:1, layer:layer + 1], min_val=0, max_val=1)
                with act.If(over != 0):
                    with act.Fori(0, NE) as e:
                        for f in range(FT):
                            act.wait_ge(dense_gu[layer], e * FT + (f + 1))
                            act.wait_ge(dense_h[layer], e * FT + (f + 2))
                            act.activation(ovs, psum[f % 2][:, 0:S], ACT.Sigmoid).then_inc(dense_sig[layer], 1)

            experts(0)
            dense(0)

            norm_squares(2)
            act.wait_ge(lsum_ready, 1)
            act.activation(lsum, lsum, ACT.Exp).then_inc(lsum_exp, 1)

            def attend_copy(name):
                kind, i = name[:2], int(name[2:])
                if kind == "dv":
                    copy_fill(dv[:, i % TT, (i // TT) * HALF:(i // TT + 1) * HALF], name)
                else:
                    copy_fill(pair(dq if kind == "dq" else dk, i), name)
                if i % 2:
                    step_done()

            for name in ("dq0", "dq1", "dk0", "dk1", "dv0", "dv1"):
                attend_copy(name)

            def unit_exp(hd):
                b = hd % 2
                act.wait_ge(soft_max, hd + 1)
                for t in range(TT):
                    for c in range(2):
                        n = 4 * b + 2 * t + c
                        w = sp_[:, b, c, KEYS[t]]
                        ins = act.activation(w, w, ACT.Exp, scale=Q_SCALE, bias=mx[:, n:n + 1],
                                             accum_out=sums[:, n:n + 1])
                ins.then_inc(soft_exp, 1)

            def head_squares(half):
                act.wait_ge(pv_done, DH // 2 * (half + 1))
                for t in range(TT):
                    for hd in range(4):
                        c = 8 * half + 4 * t + hd
                        ins = act.activation(on[:, t, hd * P:(hd + 1) * P], o_ps[half * TT + t][:, hd * P:(hd + 1) * P],
                                             ACT.Square, accum_out=oss[:, c:c + 1])
                ins.then_inc(on_squares, 1)

            for x in ATTEND:
                if x == "QA":
                    head_squares(0)
                elif x[0] == "P":
                    attend_copy(PIECES[int(x[1])])
                elif x[0] == "S":
                    unit_exp(int(x[1]))
                elif x[0] == "T" and x != "TA":
                    name = f"dt{x[1]}"
                    wait_full(act, name)
                    free(act.activation(dT[:, int(x[1]) % 2, :], bank_of(name)[:, 0:SEEN * P], ACT.Copy), name)
            head_squares(1)
            experts(1)
            act.dma_start(fg, final_norm_g.partition_broadcast(P)).then_inc(fgain_loaded, 16)
            dense(1)
            norm_squares(4)

        @block.vector
        def _(dve):
            steps = [0]
            roots = [0]

            def link(ins):
                steps[0] += 1
                ins.then_inc(dve_step, 1)
                dve.wait_ge(dve_step, steps[0])

            def log1p(y, z, q):
                link(dve.tensor_scalar(z, y, 2.0, None, ALU.add))
                link(dve.reciprocal(z, z))
                link(dve.tensor_tensor(z, z, y, ALU.mult))
                link(dve.tensor_tensor(y, z, z, ALU.mult))
                link(dve.tensor_scalar(q, y, 1.0 / 15, None, ALU.mult))
                for odd in (13, 11, 9, 7, 5, 3):
                    link(dve.scalar_tensor_tensor(out=q, in0=q, scalar=1.0 / odd, in1=y, op0=ALU.add, op1=ALU.mult))
                link(dve.scalar_tensor_tensor(out=q, in0=q, scalar=1.0, in1=z, op0=ALU.add, op1=ALU.mult))
                link(dve.tensor_scalar(y, q, 2.0, None, ALU.mult))

            def mean(dst, src, n):
                dve.tensor_scalar(dst, src, 1.0 / n, EPS, ALU.mult, ALU.add).then_inc(mean_ready, 1)

            def wait_root():
                roots[0] += 1
                dve.wait_ge(root_ready, roots[0])

            def norm_mean(n):
                dve.wait_ge(squares, TT * NH * (n + 1))
                link(dve.tensor_reduce(rstd, ss[:, :, :], AX.X, ALU.add))
                mean(rstd, rstd, D)

            def first_rows():
                wait_root()
                dve.tensor_scalar(xs[:, 0, :], h[:, 0, :], rstd[:, 0:1], None, ALU.mult).then_inc(xs_ready, 1)

            def gained(bank, i, at):
                g = cols[:, at + 2 * i:at + 2 * i + 2].unsqueeze(2).broadcast_to([P, 2, S])
                return dve.tensor_tensor(xT[:, 2 * i:2 * i + 2, :], bank[:, :].rearrange("p (a s) -> p a s", a=2), g,
                                         ALU.mult)

            def spread(n, at):
                wait_root()
                for t in range(TT):
                    ins = dve.tensor_scalar(diag[:, t, :], ident[:, :], rstd[:, t:t + 1], None, ALU.mult)
                ins.then_inc(diag_ready, 1)
                dve.wait_ge(root_spread, n // 2 + 1)
                link(dve.tensor_copy(spread_roots, root_ps[:, 0:S]))
                for k in range(KT):
                    name = f"norm{n}.{k // 2}"
                    wait_full(dve, name)
                    at_k, c = at + k, k % 2
                    ins = dve.scalar_tensor_tensor(out=xT[:, k, :], in0=bank_of(name)[:, c * S:(c + 1) * S],
                                                   scalar=cols[:, at_k:at_k + 1], in1=spread_roots, op0=ALU.mult,
                                                   op1=ALU.mult)
                    if c:
                        free(ins, name)

            def turned(n, i, at):
                name = f"norm{n}.{i}"
                wait_full(dve, name)
                free(gained(bank_of(name), i, at), name)

            dve.memset(xpad[:, :, 0:TAPS - 1], 0.0)
            wait_full(dve, "columns")
            free(dve.tensor_copy(cols[:, :], bank_of("columns")[:, 0:NR]), "columns")
            wait_read(dve, "columns")
            dve.sem_inc(cols_ready, 1)
            norm_mean(0)
            dve.wait_ge(ident_ready, 1)
            spread(0, R_MIX)
            lam_c = cols[:, R_LAM:R_LAM + WT]
            dve.scalar_tensor_tensor(out=l1a, in0=lam_c, scalar=-1.0, in1=lam_c, op0=ALU.mult, op1=ALU.max)\
                .then_inc(lam_abs, 1)
            ig, fgr, tabs, mmax, a_row, nm_row = gr
            name = "gates"
            wait_full(dve, name)
            dve.wait_ge(gates_loaded, 16 * GATE_LOADS)
            dve.tensor_scalar(ig[:, :], bank_of(name)[0:MH, 0:S], b_if[0:MH, :], None, ALU.add)
            free(dve.tensor_scalar(fgr[:, :], bank_of(name)[32:32 + MH, 0:S], b_if[32:32 + MH, :], None, ALU.add),
                 name)
            wait_read(dve, name)
            dve.scalar_tensor_tensor(out=tabs, in0=fgr[:, :], scalar=-1.0, in1=fgr[:, :], op0=ALU.mult,
                                     op1=ALU.max).then_inc(f_abs, 1)
            dve.wait_ge(f_exp, 1)
            log1p(tabs, mmax, a_row)
            link(dve.tensor_scalar(fgr[:, :], fgr[:, :], -1.0, 0.0, ALU.mult, ALU.max))
            link(dve.tensor_tensor(fgr[:, :], fgr[:, :], tabs, ALU.add))
            link(dve.tensor_tensor_scan(tabs, fgr[:, :], fgr[:, :], 0.0, ALU.add, ALU.max))
            link(dve.tensor_tensor(a_row, ig[:, :], tabs, ALU.add))
            link(dve.tensor_tensor_scan(mmax, a_row, a_row, 0.0, ALU.max, ALU.max))
            dve.tensor_tensor(nm_row, tabs, mmax, ALU.subtract).then_inc(am_rows, 1)

            dve.wait_ge(lam_exp, 1)
            log1p(l1b, l1a, l1c)
            link(dve.tensor_scalar(l1a, lam_c, -1.0, 0.0, ALU.mult, ALU.max))
            link(dve.tensor_tensor(l1a, l1a, l1b, ALU.add))
            link(dve.tensor_scalar(c4, l1a, LRU_C / 2, None, ALU.mult))
            for i in range(2):
                name = f"xa{i}"
                wait_read(dve, name)
            for w in range(TAPS - 1, -1, -1):
                for j in range(WT):
                    cw = cols[:, R_CW + w * WT + j:R_CW + w * WT + j + 1]
                    src = xpad[:, j, w:w + S]
                    if w == TAPS - 1:
                        ins = dve.tensor_scalar(xc[:, j, :], src, cw, cols[:, R_CB + j:R_CB + j + 1], ALU.mult, ALU.add)
                    else:
                        ins = dve.scalar_tensor_tensor(out=xc[:, j, :], in0=src, scalar=cw, in1=xc[:, j, :],
                                                       op0=ALU.mult, op1=ALU.add)
                if w:
                    link(ins)
            ins.then_inc(conv_done, 1)
            dve.wait_ge(conv_done, 1)
            dve.wait_ge(lru_tanh, 1)
            dve.tensor_scalar(root, r_f, 1e-34, None, ALU.max).then_inc(lru_floor, 1)
            link(dve.tensor_scalar(t1_f, r_f, 1.0, None, ALU.add))
            link(dve.reciprocal(t1_f, t1_f))
            link(dve.tensor_tensor(i_f, i_f, xc_f, ALU.mult))
            dve.wait_ge(lru_root, 1)
            link(dve.scalar_tensor_tensor(out=root, in0=root, scalar=2.0, in1=t1_f, op0=ALU.mult, op1=ALU.mult))
            link(dve.tensor_tensor(i_f, i_f, root, ALU.mult))
            link(dve.tensor_scalar(r_f, r_f, -1.0, 1.0, ALU.mult, ALU.add))
            link(dve.tensor_tensor(r_f, r_f, t1_f, ALU.mult))
            for j in range(WT):
                ins = dve.tensor_tensor_scan(xc[:, j, :], r_g[:, j, :], i_g[:, j, :], 0.0, ALU.mult, ALU.add)
            link(ins)

            gt = yT[:, 0:WT, :].rearrange("p a s -> p (a s)")

            def gelu_argument():
                for i in range(2):
                    name = f"ga{i}"
                    wait_read(dve, name)
                link(dve.tensor_tensor(gt, ga_f, ga_f, ALU.mult))
                link(dve.tensor_scalar(gt, gt, 0.044715, 1.0, ALU.mult, ALU.add))
                dve.tensor_tensor(gt, gt, ga_f, ALU.mult).then_inc(gelu_in, 1)

            def gelu_product():
                dve.wait_ge(gelu_tanh, 1)
                link(dve.scalar_tensor_tensor(out=ga_f, in0=gt, scalar=1.0, in1=ga_f, op0=ALU.add, op1=ALU.mult))
                dve.scalar_tensor_tensor(out=gt, in0=ga_f, scalar=0.5, in1=xc_f, op0=ALU.mult, op1=ALU.mult)\
                    .then_inc(ya_ready, 1)

            name = "cols_am"
            wait_full(dve, name)
            free(dve.tensor_copy(am, bank_of(name)[:, 0:16]), name)
            wait_read(dve, name)

            def head_args(hd):
                name = f"mmax{hd}"
                wait_full(dve, name)
                bank = bank_of(name)
                if hd >= 2:
                    dve.wait_ge(p_ready, hd - 1)
                dve.tensor_scalar(wbuf[:, hd % 2, 0:S], bank[:, 0:S], am[:, hd:hd + 1], 0.0, ALU.subtract, ALU.max)
                free(dve.tensor_scalar(wbuf[:, hd % 2, S:S + P], bank[:, P:S], am[:, MH + hd:MH + hd + 1], 0.0,
                                       ALU.subtract, ALU.max), name)
                wait_read(dve, name)
                dve.sem_inc(w_arg, 1)

            def head_weights(hd):
                name = f"sc{hd}"
                dve.wait_ge(w_exp, hd + 1)
                w = wbuf[:, hd % 2, :]
                diag = w.rearrange("p (a c) -> p a c", a=3)[:, 0:3:2, :]
                link(dve.tensor_tensor(diag, diag, upto[:, :].unsqueeze(1).broadcast_to([P, 2, P]), ALU.mult))
                wait_full(dve, name)
                if hd >= 2:
                    dve.wait_ge(num_done, hd - 1)
                free(dve.scalar_tensor_tensor(out=pbuf[:, hd % 2, :], in0=bank_of(name)[:, 0:S + P], scalar=K_SCALE,
                                              in1=w, op0=ALU.mult, op1=ALU.mult), name)
                wait_read(dve, name)
                dve.sem_inc(p_ready, 1)

            dve.sem_inc(am_cols, 1)
            dve.wait_ge(consts_ready, 1)
            head_args(0)
            head_weights(0)
            head_args(1)
            head_weights(1)
            head_args(2)
            gelu_argument()
            head_weights(2)
            head_args(3)
            gelu_product()
            head_weights(3)
            dve.wait_ge(num_done, MH)
            link(dve.tensor_copy(den, den_ps[:, 0:8]))
            link(dve.scalar_tensor_tensor(out=den2, in0=den, scalar=-1.0, in1=den, op0=ALU.mult, op1=ALU.max))
            dve.wait_ge(enm_ready, 1)
            link(dve.tensor_tensor(den2, den2, enm, ALU.max))
            link(dve.reciprocal(den, den2))
            for t in range(TT):
                ins = dve.tensor_tensor(yb[:, t, :, :], num_ps[t][:, :].rearrange("p (h e) -> p h e", h=MH),
                                        den[:, t * MH:(t + 1) * MH].unsqueeze(2).broadcast_to([P, MH, P]), ALU.mult)
            link(ins)
            yb_v = yb.rearrange("p t h e -> p (t h) e")
            sq_v = sq.rearrange("p t h e -> p (t h) e")
            link(dve.tensor_tensor(sq_v, yb_v, yb_v, ALU.mult))
            link(dve.tensor_reduce(hss, sq_v, AX.X, ALU.add))
            mean(hss, hss, P)
            wait_root()
            dve.tensor_tensor(yb_v, yb_v, hss.unsqueeze(2).broadcast_to([P, 8, P]), ALU.mult).then_inc(yb_ready, 1)
            for i in range(2):
                dve.wait_ge(yb_full, i + 1)
                for c in range(2):
                    hd = 2 * i + c
                    wait_read(dve, f"o{i}")
                    ins = dve.scalar_tensor_tensor(out=yT[:, WT + hd, :], in0=yb_ps[i][:, c * S:(c + 1) * S],
                                                   scalar=cols[:, R_MNG + hd:R_MNG + hd + 1], in1=so[:, hd, :],
                                                   op0=ALU.mult, op1=ALU.mult)
            ins.then_inc(yT_ready, 1)

            def residual(layer):
                for n in range(NH):
                    for t in range(TT):
                        early = layer == 1 and n == 0
                        name = f"mix{layer}.{2 * n + t}"
                        if early:
                            dve.wait_ge(early_out, t + 1)
                        else:
                            wait_full(dve, name)
                        bank = o_ps[t] if early else bank_of(name)
                        hh = h[:, t, n * HALF:(n + 1) * HALF]
                        dve.tensor_tensor(hh, bank[:, :], hh, ALU.add).then_inc(h_ready, 1)
                        if not early:
                            dve.wait_ge(h_ready, 8 * layer + 2 * n + t + 1)
                            dve.sem_inc(fill_free[BANK[name]], 1)
                        if n == 1 and t == 0:
                            turned(1 + 2 * layer, 0, R_FFN + layer * KT)
                norm_mean(1 + 2 * layer)
                turned(1 + 2 * layer, 2, R_FFN + layer * KT)
                first_rows()

            residual(0)

            def bc(v, n):
                return v.broadcast_to([P, TT, n])

            def first_max(mask, values, best, n):
                for t in range(TT):
                    ins = dve.scalar_tensor_tensor(out=mask[:, t, :], in0=values[:, t, :], scalar=best[:, t, :],
                                                   in1=prio[:, 0:n], op0=ALU.is_equal, op1=ALU.mult)
                link(ins)
                link(dve.tensor_reduce(rs2[:, :, 2], mask, AX.X, ALU.max))
                link(dve.tensor_tensor(mask, mask, bc(rs2[:, :, 2:3], n), ALU.is_equal))

            def route(layer):
                name = f"router{layer}"
                wait_full(dve, name)
                if layer == 0:
                    dve.wait_ge(params_loaded, 16 * N_PARAMS)
                ex = rs[:, 0:10].rearrange("p (t n) -> p t n", t=TT)
                eo = rs[:, 10:20].rearrange("p (t n) -> p t n", t=TT)
                best, best2 = rs2[:, :, 0:1], rs2[:, :, 1:2]
                for t in range(TT):
                    at = t * (NG + NE)
                    ins = dve.scalar_tensor_tensor(out=lg[:, t, :], in0=bank_of(name)[:, at:at + NG + NE],
                                                   scalar=rstd[:, t:t + 1], in1=b_route[:, layer, :],
                                                   op0=ALU.mult, op1=ALU.add)
                free(ins, name)
                wait_read(dve, name)
                gl = lg[:, :, 0:NG]
                link(dve.tensor_reduce(rs2[:, :, 0], gl, AX.X, ALU.max))
                link(dve.tensor_tensor(ex[:, :, 0:NG], gl, bc(best, NG), ALU.subtract))
                first_max(mg, gl, best, NG)
                mg_e = mg.unsqueeze(3).broadcast_to([P, TT, NG, EPG])
                el4 = el.rearrange("p t (g e) -> p t g e", g=NG)
                tmp4 = tmp.rearrange("p t (g e) -> p t g e", g=NG)
                link(dve.tensor_scalar(tmp4, mg_e, 1.0, 1e30, ALU.subtract, ALU.mult))
                link(dve.tensor_tensor(el4, lg[:, :, NG:].rearrange("p t (g e) -> p t g e", g=NG), tmp4, ALU.add))
                link(dve.tensor_reduce(rs2[:, :, 0], el, AX.X, ALU.max))
                first_max(m1, el, best, NE)
                link(dve.scalar_tensor_tensor(out=el, in0=m1, scalar=-3e30, in1=el, op0=ALU.mult, op1=ALU.add))
                link(dve.tensor_reduce(rs2[:, :, 1], el, AX.X, ALU.max))
                dve.tensor_tensor(ex[:, :, NG], rs2[:, :, 1], rs2[:, :, 0], ALU.subtract).then_inc(route_arg, 1)
                first_max(m2, el, best2, NE)
                dve.tensor_tensor(both, m1, m2, ALU.add).then_inc(picked, 1)
                link(dve.memset(rankm[:, :, NE:], -1.0))
                name = f"rank{layer}"
                wait_full(dve, name)
                rank = bank_of(name)[:, 0:TT * NE].rearrange("p (t n) -> p t n", t=TT)
                free(dve.scalar_tensor_tensor(out=el, in0=rank, scalar=1.0, in1=both, op0=ALU.add, op1=ALU.mult),
                     name)
                wait_read(dve, name)
                link(dve.tensor_scalar(rankm[:, :, 0:NE], el, 1.0, None, ALU.subtract))
                places(0)
                name = f"total{layer}"
                wait_full(dve, name)
                free(dve.tensor_reduce(small[0:1, 134:135], bank_of(name)[0:1, 0:NE], AX.X, ALU.max), name)
                dve.wait_ge(route_exp, layer + 1)
                link(dve.tensor_reduce(rs2[:, :, 0], eo[:, :, 0:NG], AX.X, ALU.add))
                link(dve.tensor_scalar(rs2[:, :, 1], eo[:, :, NG], 1.0, None, ALU.add))
                link(dve.tensor_tensor(rs2[:, :, 0], rs2[:, :, 0], rs2[:, :, 1], ALU.mult))
                link(dve.reciprocal(rs2[:, :, 0], rs2[:, :, 0]))
                link(dve.tensor_tensor(rs2[:, :, 1], rs2[:, :, 0], eo[:, :, NG], ALU.mult))
                link(dve.tensor_tensor(m1, m1, bc(best, NE), ALU.mult))
                link(dve.tensor_tensor(m2, m2, bc(best2, NE), ALU.mult))
                link(dve.tensor_tensor(gates[:, :, 0:NE], m1, m2, ALU.add))
                link(dve.tensor_scalar(el, el, CAP + 0.5, None, ALU.is_gt))
                link(dve.tensor_tensor(extra, el, gates[:, :, 0:NE], ALU.mult))
                dve.tensor_scalar(flag[0:1, layer:layer + 1], small[0:1, 134:135], CAP + 0.5, None, ALU.is_gt)\
                    .then_inc(flag_ready, 1)

            def places(e0):
                dve.tensor_tensor(sel, slot_no[:, :].unsqueeze(1).unsqueeze(1).broadcast_to([P, TT, EB, CAP]),
                                  rankm[:, :, bass.ds(e0, EB)].unsqueeze(3).broadcast_to([P, TT, EB, CAP]),
                                  ALU.is_equal).then_inc(sel_ready, 1)

            def weigh(e0, g, b):
                dve.wait_ge(sel_ready, g + 1)
                dve.tensor_tensor(selg, sel, gates[:, :, bass.ds(e0, EB)].unsqueeze(3)
                                  .broadcast_to([P, TT, EB, CAP]), ALU.mult).then_inc(selg_ready, 1)
                dve.wait_ge(selg_ready, b + 1)

            def take_gathered(layer, g, buf, part):
                at = R_FFN + layer * KT + part * GH
                dve.wait_ge(gather_full, g * 2 + (part + 1))
                dve.tensor_tensor(xg[:, buf, part * GH:(part + 1) * GH, :],
                                  gather_ps[part][:, :].rearrange("p (k c) -> p k c", k=GH),
                                  cols[:, at:at + GH].unsqueeze(2).broadcast_to([P, GH, P]), ALU.mult)\
                    .then_inc(gather_free, 1)

            def packed(layer, i, par):
                b = i * 2 + (layer * NB + par)
                g = i * 2 + (layer * (NB + 1) + par)
                done = i * (2 * MOE_STEPS) + (layer * LAYER_STEPS + MIX_STEPS + par * MOE_STEPS)
                e0 = i * (2 * EB) + par * EB
                weigh(e0, g, b)
                places(e0 + EB)
                dve.wait_ge(sgt_full, b + 1)
                dve.tensor_copy(sgt[:, :, :].rearrange("p t c -> p (t c)"), gather_ps[0][:, 0:TT * P])\
                    .then_inc(sgt_ready, 1)
                take_gathered(layer, g + 1, 1 - par % 2, 0)
                take_gathered(layer, g + 1, 1 - par % 2, 1)
                dve.wait_ge(steps_done, done + KT)
                dve.wait_ge(sig_done, b + 1)
                dve.tensor_tensor(sig, sig, hy[0][:, :], ALU.mult).then_inc(hid_step, 1)
                dve.wait_ge(hid_step, b + 1)
                dve.tensor_tensor(hid, sig, hy[1][:, :], ALU.mult).then_inc(hid_done, 1)
                dve.wait_ge(steps_done, done + MOE_STEPS)
                dve.tensor_copy(y_s[:, HALF:D], hy[1][:, :]).then_inc(y_dve, 1)

            def dense(layer):
                dve.wait_ge(flag_ready, layer + 1)
                over = dve.value_load(flag[0:1, layer:layer + 1], min_val=0, max_val=1)
                with dve.If(over != 0):
                    dve.memset(ovs, 0.0).then_inc(dense_h[layer], 2)
                    dve.memset(small[:, 132:133], 0.0).then_inc(dense_add[layer], 2)
                    for i in range(4):
                        dve.wait_ge(dense_turned[layer], i + 1)
                        gained(psum[i], i, R_FFN + layer * KT).then_inc(dense_x[layer], 1)
                    with dve.Fori(0, NE) as e:
                        for f in range(FT):
                            dve.wait_ge(dense_sig[layer], e * FT + (f + 1))
                            dve.tensor_tensor(ovs, ovs, psum[f % 2][:, 0:S], ALU.mult).then_inc(dense_mul[layer], 1)
                            dve.wait_ge(dense_mul[layer], e * FT + (f + 1))
                            dve.tensor_tensor(ovh[:, f, :], ovs, psum[f % 2][:, S:2 * S], ALU.mult)\
                                .then_inc(dense_h[layer], 1)
                        for n in range(TT * NH):
                            t, half = n // NH, n % NH
                            dve.wait_ge(dense_y[layer], e * 4 + (n + 1))
                            hh = h[:, t, half * HALF:(half + 1) * HALF]
                            dve.scalar_tensor_tensor(out=hh, in0=psum[2 + n % 2][:, :],
                                                     scalar=extra[:, t, bass.ds(e, 1)], in1=hh, op0=ALU.mult,
                                                     op1=ALU.add).then_inc(dense_add[layer], 1)
                    dve.wait_ge(dense_add[layer], 4 * NE + 2)

            def experts(layer):
                route(layer)
                g = layer * (NB + 1)
                take_gathered(layer, g, 0, 0)
                take_gathered(layer, g, 0, 1)
                packed(layer, 0, 0)
                packed(layer, 0, 1)
                with dve.Fori(0, NB // 2 - 1) as i:
                    packed(layer, i, 2)
                    packed(layer, i, 3)
                dense(layer)
                for t in range(TT):
                    for half in range(NH):
                        dve.wait_ge(scattered, 4 * (NB * (layer + 1) - 1) + t * NH + half + 1)
                        hh = h[:, t, half * HALF:(half + 1) * HALF]
                        dve.tensor_tensor(hh, acc[t * NH + half][:, :], hh, ALU.add).then_inc(h_ready, 1)

            experts(0)

            norm_mean(2)
            spread(2, R_MIX + KT)
            for c in range(2):
                ins = dve.tensor_tensor_reduce(out=lam_rows[:, 2 * c, :], in0=lam_rows[:, 2 * c, :],
                                               in1=lam_rows[:, 2 * c + 1, :], scale=1.0, scalar=0.0, op0=ALU.mult,
                                               op1=ALU.add, accum_out=lsum[:, c:c + 1])
            ins.then_inc(lsum_ready, 1)
            dve.wait_ge(lsum_exp, 1)
            link(dve.tensor_tensor(nlam, lsum[:, 1:2], lsum[:, 0:1], ALU.subtract))
            link(dve.tensor_scalar(nlam, nlam, LAMBDA_INIT, None, ALU.subtract))
            link(dve.tensor_scalar(dng2, cols[:, R_DNG:R_DNG + DH], 1.0 - LAMBDA_INIT, None, ALU.mult))
            dve.wait_ge(dist_ready, 1)

            def unit_max(hd):
                b = hd % 2
                slope = 2.0 ** (-8.0 * (hd + 1) / DH) / Q_SCALE
                if hd >= 2:
                    dve.wait_ge(diff_ready, hd - 1)
                for c in range(2):
                    name = f"ds{hd}.{c}"
                    wait_full(dve, name)
                    free(dve.scalar_tensor_tensor(out=sp_[:, b, c, :], in0=dist, scalar=slope,
                                                  in1=bank_of(name)[:, 0:SEEN * P], op0=ALU.mult, op1=ALU.add), name)
                for c in range(2):
                    wait_read(dve, f"ds{hd}.{c}")
                m = mx[:, 4 * b:4 * b + 4]
                for t in range(TT):
                    ins = dve.tensor_reduce(m[:, 2 * t:2 * t + 2], sp_[:, b, :, KEYS[t]], AX.X, ALU.max)
                link(ins)
                dve.tensor_scalar(m, m, -Q_SCALE, None, ALU.mult).then_inc(soft_max, 1)

            def unit_diff(hd):
                b = hd % 2
                dve.wait_ge(soft_exp, hd + 1)
                r = rsum[:, 4 * b:4 * b + 4]
                link(dve.reciprocal(r, sums[:, 4 * b:4 * b + 4]))
                link(dve.tensor_tensor(r[:, 1:4:2], r[:, 1:4:2], nlam.broadcast_to([P, 2]), ALU.mult))
                if hd >= 2:
                    wait_full(dve, f"dt{hd - 2}")
                for t in range(TT):
                    ins = dve.tensor_scalar(dif[:, b, KEYS[t]], sp_[:, b, 0, KEYS[t]], r[:, 2 * t:2 * t + 1], None,
                                            ALU.mult)
                link(ins)
                for t in range(TT):
                    ins = dve.scalar_tensor_tensor(out=dif[:, b, KEYS[t]], in0=sp_[:, b, 1, KEYS[t]],
                                                   scalar=r[:, 2 * t + 1:2 * t + 2], in1=dif[:, b, KEYS[t]],
                                                   op0=ALU.mult, op1=ALU.add)
                ins.then_inc(diff_ready, 1)

            def head_scale(half):
                wait_root()
                if half == 1:
                    for name in ("dy0", "dy1"):
                        wait_full(dve, name)
                for t in range(TT):
                    r = oss[:, 8 * half + 4 * t:8 * half + 4 * t + 4].unsqueeze(2).broadcast_to([P, 4, P])
                    ins = dve.tensor_tensor(on[:, t, :].rearrange("p (h e) -> p h e", h=4),
                                            o_ps[half * TT + t][:, :].rearrange("p (h e) -> p h e", h=4), r, ALU.mult)
                ins.then_inc(on_ready, 1)

            def head_turned(half):
                for i in range(2):
                    k = 4 * half + 2 * i
                    name = f"dy{2 * half + i}"
                    wait_full(dve, name)
                    free(dve.tensor_tensor(yT[:, k:k + 2, :], bank_of(name)[:, :].rearrange("p (a s) -> p a s", a=2),
                                           dng2[:, k:k + 2].unsqueeze(2).broadcast_to([P, 2, S]), ALU.mult), name)

            for x in ATTEND:
                if x == "MA":
                    dve.wait_ge(on_squares, 1)
                    mean(oss[:, 0:8], oss[:, 0:8], P)
                elif x == "TA":
                    head_scale(0)
                elif x == "DA":
                    head_turned(0)
                elif x[0] == "S":
                    unit_max(int(x[1]))
                elif x[0] == "T":
                    unit_diff(int(x[1]))
            dve.wait_ge(on_squares, 2)
            mean(oss[:, 8:16], oss[:, 8:16], P)
            head_scale(1)
            head_turned(1)
            residual(1)
            experts(1)

            dve.wait_ge(fgain_loaded, 16)
            for t in range(TT):
                dve.wait_ge(squares, TT * NH * 4 + NH * (t + 1))
                r = rstd[:, t:t + 1]
                link(dve.tensor_reduce(r, ss[:, t, :], AX.X, ALU.add))
                mean(r, r, D)
                wait_root()
                dve.scalar_tensor_tensor(out=xs[:, t, :], in0=h[:, t, :], scalar=r, in1=fg, op0=ALU.mult,
                                         op1=ALU.mult).then_inc(fin_ready, 1)


def laid_out(v):
    import numpy as np

    a = {name: np.ascontiguousarray(x) for name, x in v.items()}
    rows = ("norm_mix_g", "norm_ffn_g", "lru_conv_w", "lru_conv_b", "lru_b_r", "lru_b_i", "lru_lambda",
            "mlstm_norm_g", "diff_norm_g")
    blocks = [a[n][0].reshape(WT, 2, 64, 64).transpose(1, 2, 0, 3) for n in ("lru_w_r", "lru_w_i")]
    route = np.concatenate([a["moe_w_group"], a["moe_w_expert"]], axis=2)
    return {
        "x": a["x"],
        "param_rows": np.concatenate([a[n].reshape(-1, P) for n in rows]),
        "gate_bias": np.stack([a["mlstm_b_i"][0], a["mlstm_b_f"][0]])[:, :, None],
        "block_weights": np.stack(blocks),
        "route_weights": route.reshape(LAYERS, KT, P, NG + NE).transpose(2, 0, 1, 3),
        "route_bias": np.concatenate([a["moe_b_group"], a["moe_b_expert"]], axis=1),
        "lambda_vectors": np.concatenate([a[f"diff_lambda_{n}"] for n in ("q1", "k1", "q2", "k2")]),
        **{n: a[n] for n in ("ab_w_in", "ab_w_out", "diff_w_qkv", "diff_w_o", "moe_w_up", "moe_w_down",
                             "final_norm_g")},
    }


def kernel(**inputs):
    import numpy as np
    import concourse.bacc as bacc
    from concourse.bass_utils import run_bass_kernel_spmd

    nc = bacc.Bacc("TRN2", target_bir_lowering=False, num_devices=1)
    arrays, args = {}, []
    for name, a in laid_out(inputs).items():
        a = np.ascontiguousarray(a)
        arrays[f"in_{name}"] = a
        args.append(nc.dram_tensor(f"in_{name}", a.shape, mybir.dt.from_np(a.dtype), kind="ExternalInput").ap())
    out = nc.dram_tensor("out_0", (1, S, D), F32, kind="ExternalOutput").ap()
    build(nc, *args, out)
    r = run_bass_kernel_spmd(nc, [arrays], core_ids=[0])
    return r.results[0]["out_0"]
```
